# Optimizing a Trainium2 kernel written in Bass

```python
import jax, jax.numpy as jnp
from jax import lax
import numpy as np

D_MODEL = 1024
BATCH = 1
SEQ = 256
DEPTH = 2

HEAD_DIM = 64
N_HEADS_A = 8
N_HEADS_B = 8
WIDTH_AB = (N_HEADS_A + N_HEADS_B) * HEAD_DIM
IN_AB = 3 * WIDTH_AB + N_HEADS_B
DILATED_CONFIGS = ((128, 1), (512, 4), (2048, 16))
ROPE_THETA = 500000.0
ROPE_DIM = HEAD_DIM // 4
BLOCK = 128
HGRN_EXPAND = 128
N_HEADS_C = D_MODEL // HGRN_EXPAND
HGRN_DK = HGRN_EXPAND
HGRN_DV = D_MODEL // N_HEADS_C
HGRN_CHUNK = 64
D_FF = 2816
N_EXPERTS = 8
TOP_K = 2
D_FF_EXPERT = 3584
N_EVEN = (DEPTH + 1) // 2
N_ODD = DEPTH // 2
EPS = 1e-6

kernel_name = "hybrid_dilated_fox_hgrn2_moe"

def _rmsnorm(x, gain):
    x32 = x.astype(jnp.float32)
    y = x32 * lax.rsqrt(jnp.mean(x32 * x32, axis=-1, keepdims=True) + EPS)
    return (y * gain.astype(jnp.float32)).astype(x.dtype)

def _partial_rope(x, positions):
    half = ROPE_DIM // 2
    inv_freq = jnp.power(jnp.float32(ROPE_THETA), -jnp.arange(half, dtype=jnp.float32) / half)
    ang = positions.astype(jnp.float32)[..., None] * inv_freq
    cos = jnp.cos(ang)[:, :, None, :]
    sin = jnp.sin(ang)[:, :, None, :]
    xr = x[..., :ROPE_DIM].astype(jnp.float32)
    x1, x2 = xr[..., :half], xr[..., half:]
    rot = jnp.concatenate([x1 * cos - x2 * sin, x2 * cos + x1 * sin], axis=-1)
    return jnp.concatenate([rot.astype(x.dtype), x[..., ROPE_DIM:]], axis=-1)

def _dilated_branch(q, k, v, window, dilation):
    B_, H_, S_, Dh = q.shape
    r = dilation
    n = window // dilation
    assert n <= BLOCK
    L = S_ // r
    nb = -(-L // BLOCK)
    Lp = nb * BLOCK

    def to_sub(t):
        t = t.reshape(B_, H_, L, r, Dh).transpose(0, 1, 3, 2, 4)
        t = jnp.pad(t, ((0, 0), (0, 0), (0, 0), (0, Lp - L), (0, 0)))
        return t.reshape(B_, H_, r, nb, BLOCK, Dh)

    def band(t):
        prev = jnp.pad(t[:, :, :, :-1], ((0, 0), (0, 0), (0, 0), (1, 0), (0, 0), (0, 0)))
        return jnp.concatenate([prev, t], axis=-2)

    qs = to_sub(q)
    kb = band(to_sub(k))
    vb = band(to_sub(v))
    logits = jnp.einsum('bhrnqd,bhrnkd->bhrnqk', qs, kb).astype(jnp.float32)
    qi = jnp.arange(BLOCK)[:, None]
    kj = jnp.arange(2 * BLOCK)[None, :]
    dist = BLOCK + qi - kj
    key_pos = (jnp.arange(nb)[:, None, None] - 1) * BLOCK + kj[None]
    valid = (dist >= 0) & (dist <= n) & (key_pos >= 0)
    logits = jnp.where(valid, logits, -jnp.inf)
    m = jnp.max(logits, axis=-1, keepdims=True)
    e = jnp.exp(logits - m)
    l = jnp.sum(e, axis=-1, keepdims=True)
    o = jnp.einsum('bhrnqk,bhrnkd->bhrnqd', (e / l).astype(v.dtype), vb)
    lse = (m + jnp.log(l))[..., 0]

    def from_sub(t):
        extra = t.shape[5:]
        t = t.reshape((B_, H_, r, Lp) + extra)[:, :, :, :L]
        t = jnp.moveaxis(t, 2, 3)
        return t.reshape((B_, H_, S_) + extra)

    return from_sub(o), from_sub(lse)

def _forgetting_attention(q, k, v, logf):
    B_, H_, S_, Dh = q.shape
    nq = S_ // BLOCK
    c = jnp.cumsum(logf, axis=-1)
    qb = q.reshape(B_, H_, nq, BLOCK, Dh).transpose(2, 0, 1, 3, 4)
    cb = c.reshape(B_, H_, nq, BLOCK).transpose(2, 0, 1, 3)
    kpos = jnp.arange(S_)

    def one_block(args):
        qblk, cblk, j = args
        logits = jnp.einsum('bhqd,bhkd->bhqk', qblk, k).astype(jnp.float32)
        logits = logits + cblk[..., None] - c[:, :, None, :]
        qpos = j * BLOCK + jnp.arange(BLOCK)
        logits = jnp.where(kpos[None, :] <= qpos[:, None], logits, -jnp.inf)
        p = jax.nn.softmax(logits, axis=-1)
        return jnp.einsum('bhqk,bhkd->bhqd', p.astype(v.dtype), v)

    o = lax.map(one_block, (qb, cb, jnp.arange(nq)))
    return o.transpose(1, 2, 0, 3, 4).reshape(B_, H_, S_, Dh)

def _hgrn2_chunkwise(q, k, v, logf):
    B_, H_, S_, dk = q.shape
    dv = v.shape[-1]
    nc = S_ // HGRN_CHUNK

    def chunks(t):
        return t.reshape(B_, H_, nc, HGRN_CHUNK, t.shape[-1]).transpose(2, 0, 1, 3, 4)

    causal = jnp.tril(jnp.ones((HGRN_CHUNK, HGRN_CHUNK), dtype=bool))[:, :, None]

    def step(state, xs):
        qc, kc, vc, gc = xs
        b = jnp.cumsum(gc, axis=-2)
        o_inter = jnp.einsum('bhtd,bhde->bhte', qc * jnp.exp(b), state)
        rel = jnp.where(causal, b[:, :, :, None, :] - b[:, :, None, :, :], -jnp.inf)
        scores = jnp.einsum('bhtd,bhtsd,bhsd->bhts', qc, jnp.exp(rel), kc)
        o_intra = jnp.einsum('bhts,bhse->bhte', scores, vc)
        b_last = b[:, :, -1, :]
        new_state = jnp.exp(b_last)[..., None] * state + jnp.einsum(
            'bhsd,bhse->bhde', kc * jnp.exp(b_last[:, :, None, :] - b), vc)
        return new_state, o_inter + o_intra

    state0 = jnp.zeros((B_, H_, dk, dv), jnp.float32)
    _, o = lax.scan(step, state0, (chunks(q), chunks(k), chunks(v), chunks(logf)))
    return o.transpose(1, 2, 0, 3, 4).reshape(B_, H_, S_, dv)

def _mixer_ab(h, positions, w_in, f_bias, w_out):
    B_, S_, _ = h.shape
    proj = h @ w_in
    wa = N_HEADS_A * HEAD_DIM
    wb = N_HEADS_B * HEAD_DIM
    splits = np.cumsum([wa, wa, wa, wb, wb, wb]).tolist()
    qa, ka, va, qb, kb, vb, f_logit = jnp.split(proj, splits, axis=-1)
    scale = HEAD_DIM ** -0.5

    def heads(t, n):
        return t.reshape(B_, S_, n, HEAD_DIM)

    def bhsd(t):
        return t.transpose(0, 2, 1, 3)

    qa = bhsd(_partial_rope(heads(qa, N_HEADS_A), positions) * scale)
    ka = bhsd(_partial_rope(heads(ka, N_HEADS_A), positions))
    va = bhsd(heads(va, N_HEADS_A))
    outs, lses = [], []
    for window, dilation in DILATED_CONFIGS:
        o_i, lse_i = _dilated_branch(qa, ka, va, window, dilation)
        outs.append(o_i.astype(jnp.float32))
        lses.append(lse_i)
    mix = jax.nn.softmax(jnp.stack(lses, axis=0), axis=0)
    out_a = jnp.sum(mix[..., None] * jnp.stack(outs, axis=0), axis=0).astype(h.dtype)

    logf = jax.nn.log_sigmoid((f_logit + f_bias).astype(jnp.float32)).transpose(0, 2, 1)
    out_b = _forgetting_attention(bhsd(heads(qb, N_HEADS_B)) * scale,
                                  bhsd(heads(kb, N_HEADS_B)),
                                  bhsd(heads(vb, N_HEADS_B)), logf).astype(h.dtype)

    o = jnp.concatenate([out_a, out_b], axis=1)
    o = o.transpose(0, 2, 1, 3).reshape(B_, S_, WIDTH_AB)
    return o @ w_out

def _mixer_c(h, w_in, lower_bound, gnorm, w_out):
    B_, S_, _ = h.shape
    proj = h @ w_in
    q, f_logit, i_in, g = jnp.split(proj, 4, axis=-1)

    def bhsd(t, d):
        return t.reshape(B_, S_, N_HEADS_C, d).transpose(0, 2, 1, 3).astype(jnp.float32)

    lb = lower_bound.astype(jnp.float32).reshape(N_HEADS_C, HGRN_DK)[None, :, None, :]
    f = lb + (1.0 - lb) * jax.nn.sigmoid(bhsd(f_logit, HGRN_DK))
    logf = jnp.log(f)
    k = 1.0 - f
    o = _hgrn2_chunkwise(bhsd(q, HGRN_DK) * (HGRN_DK ** -0.5), k, bhsd(i_in, HGRN_DV), logf)
    o = _rmsnorm(o, gnorm)
    o = o.transpose(0, 2, 1, 3).reshape(B_, S_, D_MODEL).astype(h.dtype)
    return (o * jax.nn.silu(g)) @ w_out

def _swiglu(h, w_gate, w_up, w_down):
    return (jax.nn.silu(h @ w_gate) * (h @ w_up)) @ w_down

def _moe_swiglu(h, router, w_gate, w_up, w_down):
    logits = (h @ router).astype(jnp.float32)
    top_vals, top_idx = lax.top_k(logits, TOP_K)
    gates = jax.nn.softmax(top_vals, axis=-1)
    combine = jnp.sum(jax.nn.one_hot(top_idx, N_EXPERTS, dtype=jnp.float32) * gates[..., None], axis=-2)
    y = jnp.zeros(h.shape, jnp.float32)
    for e in range(N_EXPERTS):
        y = y + combine[..., e:e + 1] * _swiglu(h, w_gate[e], w_up[e], w_down[e]).astype(jnp.float32)
    return y.astype(h.dtype)

def setup_inputs(seed: int = 0) -> dict:
    key = jax.random.key(seed)
    ks = jax.random.split(key, 20)

    def w(k, shape, fan_in):
        return jax.random.normal(k, shape, jnp.float32) * fan_in ** -0.5

    def gain(k, shape):
        return 1.0 + 0.02 * jax.random.normal(k, shape, jnp.float32)

    x = jax.random.normal(ks[0], (BATCH, SEQ, D_MODEL), jnp.float32)
    offsets = jax.random.randint(ks[1], (BATCH, 1), 0, 4096, dtype=jnp.int32)
    positions = offsets + jnp.arange(SEQ, dtype=jnp.int32)[None, :]
    return {
        "x": x,
        "positions": positions,
        "norm_mix": gain(ks[2], (DEPTH, D_MODEL)),
        "norm_ffn": gain(ks[3], (DEPTH, D_MODEL)),
        "w_in_ab": w(ks[4], (N_EVEN, D_MODEL, IN_AB), D_MODEL),
        "fgate_bias": 3.0 + 0.5 * jax.random.normal(ks[5], (N_EVEN, N_HEADS_B), jnp.float32),
        "w_out_ab": w(ks[6], (N_EVEN, WIDTH_AB, D_MODEL), WIDTH_AB),
        "w_in_c": w(ks[7], (N_ODD, D_MODEL, 4 * D_MODEL), D_MODEL),
        "lower_bounds": 0.1 * jax.random.normal(ks[8], (DEPTH, D_MODEL), jnp.float32),
        "gnorm_c": gain(ks[9], (N_ODD, HGRN_DV)),
        "w_out_c": w(ks[10], (N_ODD, D_MODEL, D_MODEL), D_MODEL),
        "w_gate_ffn": w(ks[11], (N_EVEN, D_MODEL, D_FF), D_MODEL),
        "w_up_ffn": w(ks[12], (N_EVEN, D_MODEL, D_FF), D_MODEL),
        "w_down_ffn": w(ks[13], (N_EVEN, D_FF, D_MODEL), D_FF),
        "router": w(ks[14], (N_ODD, D_MODEL, N_EXPERTS), D_MODEL),
        "w_gate_moe": w(ks[15], (N_ODD, N_EXPERTS, D_MODEL, D_FF_EXPERT), D_MODEL),
        "w_up_moe": w(ks[16], (N_ODD, N_EXPERTS, D_MODEL, D_FF_EXPERT), D_MODEL),
        "w_down_moe": w(ks[17], (N_ODD, N_EXPERTS, D_FF_EXPERT, D_MODEL), D_FF_EXPERT),
        "norm_final": gain(ks[18], (D_MODEL,)),
    }

def reference(x, positions, norm_mix, norm_ffn, w_in_ab, fgate_bias, w_out_ab, w_in_c,
              lower_bounds, gnorm_c, w_out_c, w_gate_ffn, w_up_ffn, w_down_ffn, router,
              w_gate_moe, w_up_moe, w_down_moe, norm_final):
    lb_all = jnp.cumsum(jax.nn.softmax(lower_bounds.astype(jnp.float32), axis=0), axis=0)
    lb_all = lb_all - lb_all[0:1]
    for i in range(DEPTH):
        j = i // 2
        h = _rmsnorm(x, norm_mix[i])
        if i % 2 == 0:
            x = x + _mixer_ab(h, positions, w_in_ab[j], fgate_bias[j], w_out_ab[j])
            h = _rmsnorm(x, norm_ffn[i])
            x = x + _swiglu(h, w_gate_ffn[j], w_up_ffn[j], w_down_ffn[j])
        else:
            x = x + _mixer_c(h, w_in_c[j], lb_all[i], gnorm_c[j], w_out_c[j])
            h = _rmsnorm(x, norm_ffn[i])
            x = x + _moe_swiglu(h, router[j], w_gate_moe[j], w_up_moe[j], w_down_moe[j])
    return _rmsnorm(x, norm_final)


_drawn_inputs = setup_inputs


def setup_inputs(seed=0):
    import zlib

    import numpy as np

    out = dict(_drawn_inputs(seed))
    spreads = {}
    factors = {}
    for name, (base, spread) in spreads.items():
        noise = np.random.default_rng([zlib.crc32(name.encode()), seed]).standard_normal(out[name].shape)
        drawn = base * np.exp(spread * noise) if base else spread * noise
        out[name] = __import__('jax').numpy.asarray(drawn.astype(out[name].dtype))
    for name, factor in factors.items():
        out[name] = (out[name] * factor).astype(out[name].dtype)
    return out
```

```python
from contextlib import ExitStack

import numpy as np
import concourse.bass as bass
from concourse import mybir

ALU = mybir.AluOpType
ACT = mybir.ActivationFunctionType
F32 = mybir.dt.float32
I32 = mybir.dt.int32
U32 = mybir.dt.uint32
AX_X = mybir.AxisListType.X

P = 128
SEQ = 256
T = SEQ // P
D = 1024
KD = D // P
HD = 64
NHA = 8
NHB = 8
NH = NHA + NHB
ROPE_DIM = HD // 4
ROPE_THETA = 500000.0
DILATED = ((128, 1), (512, 4), (2048, 16))
NHC = 8
CHUNK = 64
FF = 2816
NE = 8
FFE = 3584
EPS = 1e-6
NEG = -1.0e30

SLOTS = 7
SLOT = 2048
WORK = 4
LEVELS = (64, 32, 16, 8, 4, 2, 1)

C_ID, C_PERM, C_MA, C_MB, C_RST, C_FREQ, C_DIAG, C_IOTA, C_END = np.cumsum(
    [0, P, P, 3 * P, 3 * P, SEQ, 1, P, NE]).tolist()


def shape_constants():
    c = np.zeros((P, C_END), np.float32)
    c[:, C_ID:C_ID + P] = np.eye(P)
    half = ROPE_DIM // 2
    for base in range(0, P, HD):
        for i in range(half):
            c[base + half + i, C_PERM + base + i] = -1.0
            c[base + i, C_PERM + base + half + i] = 1.0
            f = np.power(np.float32(ROPE_THETA), -np.float32(i) / np.float32(half), dtype=np.float32)
            c[base + i, C_FREQ] = c[base + half + i, C_FREQ] = f
    q = np.arange(SEQ)[:, None]
    k = np.arange(SEQ)[None, :]
    count = np.zeros((SEQ, SEQ))
    for window, dilation in DILATED:
        count += (q >= k) & (q - k <= window) & ((q - k) % dilation == 0)
    dilated = np.where(count > 0, np.log(np.maximum(count, 1)), NEG)
    causal = np.where(q >= k, 0.0, NEG)
    for off, m in ((C_MA, dilated), (C_MB, causal)):
        c[:, off:off + P] = m[:P, :P]
        c[:, off + P:off + 3 * P] = m[P:, :]
    c[:, C_RST:C_RST + SEQ] = (np.arange(SEQ) % CHUNK != 0)[None, :]
    c[:, C_DIAG:C_DIAG + P] = np.eye(P)
    c[:, C_IOTA:C_IOTA + NE] = np.arange(NE)[None, :]
    onehot = np.zeros((NHB, NHB, SEQ), np.float32)
    for h in range(NHB):
        onehot[h, h, :] = 1.0
    s = np.arange(P)[:, None]
    t = np.arange(P)[None, :]
    level = np.zeros((P, len(LEVELS), P), np.int32)
    for n, w in enumerate(LEVELS):
        level[:, n, :] = (s // (2 * w) == t // (2 * w)) & (s % (2 * w) < w) & (t % (2 * w) >= w)
    return {"c_float": c, "c_onehot": onehot, "c_level": level}


class Turns:

    def __init__(self, n):
        self.n, self.at, self.used, self.where = n, 0, [0] * n, {}

    def take(self, key):
        place = self.at % self.n
        self.at += 1
        self.used[place] += 1
        self.where[key] = (place, self.used[place])
        return self.where[key]


def trunk(nc, x, positions, norm_mix, norm_ffn, w_in_ab, fgate_bias, w_out_ab, w_in_c, lower_bounds,
          gnorm_c, w_out_c, w_gate_ffn, w_up_ffn, w_down_ffn, router, w_gate_moe, w_up_moe,
          w_down_moe, norm_final, c_float, c_onehot, c_level, out):
    FG = FF // 256
    GE = FFE // 256

    ring = Turns(SLOTS)
    chunks = []

    def chunk(key, src, view):
        ring.take(key)
        chunks.append((key, src, view))

    def cols(w, c0, n):
        return w[:, c0:c0 + n].rearrange("(k p) n -> p k n", p=P)

    w_ab, w_oab, w_c, w_oc = w_in_ab[0], w_out_ab[0], w_in_c[0], w_out_c[0]
    def chunk_pair(name, c, w):
        for r in range(2):
            chunk((name, c, r), cols(w[512 * r:512 * r + 512, :], 512 * c, 512), (KD // 2, 512))

    for c in range(6):
        chunk_pair("ab", c, w_ab)
    for c in range(2):
        chunk_pair("oab", c, w_oab)
    for g in range(FG):
        chunk(("wg", g), cols(w_gate_ffn[0], 256 * g, 256), (KD, 256))
        chunk(("wu", g), cols(w_up_ffn[0], 256 * g, 256), (KD, 256))
        chunk(("wd", g), w_down_ffn[0][256 * g:256 * g + 256, :].rearrange("(k p) n -> p k n", p=P), (2, D))
    for c in (2, 3, 0, 1, 4, 5, 6, 7):
        chunk_pair("c", c, w_c)
    for c in range(2):
        chunk_pair("oc", c, w_oc)
    moe_slot0 = ring.at % SLOTS
    moe_used = list(ring.used)
    MOE_CHUNKS = 3 * GE
    assert MOE_CHUNKS % SLOTS == 0
    PER_SLOT = MOE_CHUNKS // SLOTS

    work = Turns(WORK)

    with ExitStack() as ctx:
        def sb(name, shape, dt=F32):
            return ctx.enter_context(nc.sbuf_tensor(name, shape, dt))

        sems = {}

        def sem(name):
            if name not in sems:
                sems[name] = ctx.enter_context(nc.semaphore(name))
            return sems[name]

        consts = sb("consts", [P, C_END])
        arena = sb("arena", [P, 5120])
        onehot = arena[0:NHB, 0:2048].rearrange("p (h q) -> p h q", h=NHB)
        rope = arena[:, 2048:2048 + 6 * SEQ].rearrange("p (a q) -> p a q", a=6)
        fox = arena[0:NHB, 3584:3584 + 6 * SEQ].rearrange("p (a q) -> p a q", a=6)
        level_mask = sb("level_mask", [P, len(LEVELS), P], I32)
        vec_rows = sb("vec_rows", [6 * KD, P])
        vec_cols = sb("vec_cols", [P, 6 * KD])
        wf = sb("wf", [P, KD, NHB])
        wr = sb("wr", [P, KD, NE])
        fbias = sb("fbias", [NHB, 1])
        gnorm = sb("gnorm", [P, P])
        pos_i = sb("pos_i", [P, SEQ], I32)
        ring_sb = sb("ring_sb", [P, SLOTS, SLOT])
        X = sb("X", [P, T, D])
        XN = sb("XN", [P, T, D])
        HT = sb("HT", [P, KD, SEQ])
        A = [sb(f"A{i}", [P, 2048]) for i in range(5)]
        small = sb("small", [P, 128])
        hs_sg = sb("hs_sg", [P, 8 * SEQ])
        hs = hs_sg[:, 0:4 * SEQ].rearrange("p (a q) -> p a q", a=4)
        sg = hs_sg[:, 4 * SEQ:].rearrange("p (a q) -> p a q", a=4)
        zeros = sb("zeros", [P, P])
        final_gain = sb("final_gain", [P, D])
        combine = sb("combine", [P, T, NE])
        route = sb("route", [P, T, 64])

        psum = [ctx.enter_context(nc.psum_tensor(f"work{i}", [P, 512], F32)) for i in range(WORK)]
        acc = [ctx.enter_context(nc.psum_tensor(f"acc{i}", [P, 512], F32)) for i in range(4)]

        ident = consts[:, C_ID:C_ID + P]
        perm = consts[:, C_PERM:C_PERM + P]
        score_mask = {"a": consts[:, C_MA:C_MA + 3 * P], "b": consts[:, C_MB:C_MB + 3 * P]}
        gain = {"mix0": 0, "mix1": KD, "ffn0": 2 * KD, "ffn1": 3 * KD}
        NORMS = ["mix0", "ffn0", "mix1", "ffn1", "final"]

        SS, MS, RS = 0, 2, 4
        MX, SM, RI = 8, 40, 72
        LBC, OML = 104, 112

        QK = {"qa": A[0][:, 0:1024], "ka": A[0][:, 1024:2048], "qb": A[1][:, 0:1024], "kb": A[1][:, 1024:2048]}
        QK = {n: v.rearrange("p (j q) -> p j q", j=4) for n, v in QK.items()}
        V = A[2][:, :].rearrange("p (t n) -> p t n", t=T)
        OT = A[3][:, :].rearrange("p (k q) -> p k q", k=KD)
        SRING = 4
        S = [A[4][:, 384 * i:384 * i + 384] for i in range(SRING)]
        PT = [XN[:, 0, 0:384], XN[:, 0, 384:768], XN[:, 1, 0:384]]
        cosT, sinT = rope[:, 0, :], rope[:, 1, :]
        rtmp = hs[:, :, :].rearrange("p a b -> p (a b)")

        def full(i):
            return sem(f"chunk_full{i}")

        def free(i):
            return sem(f"chunk_free{i}")

        def bank_full(i):
            return sem(f"bank_full{i}")

        def bank_free(i):
            return sem(f"bank_free{i}")

        def evacuated(eng, key):
            b, use = work.where[key]
            eng.wait_ge(bank_free(b), use)

        def product(eng, key):
            b, use = work.where[key]
            eng.wait_ge(bank_full(b), use)
            return psum[b], b

        NLV = len(LEVELS) + 1
        n_ff, n_e = FF // P, FFE // P
        PB = n_e // WORK
        CB = A[0][:, :].rearrange("p (e q) -> p e q", e=NE)

        def filled(b):
            return bank_full(b), work.used[b]

        done_at = {}
        moe = {}

        BC, KC, QC = (A[i][:, :].rearrange("p (h q) -> p h q", h=NHC) for i in range(3))
        VC = A[3][:, :].rearrange("p (t n) -> p t n", t=T)
        SG = A[4][:, :].rearrange("p (t n) -> p t n", t=T)
        LV = arena[:, 0:4096].rearrange("p (b side h q) -> p b side h q", b=2, side=2, h=4)
        DL = arena[:, 4096:5120].rearrange("p (h q) -> p h q", h=4)
        AT = hs_sg[:, 0:1024].rearrange("p (h t q) -> p h t q", h=4, t=T)
        AX_ = hs_sg[:, 1024:1536].rearrange("p (h q) -> p h q", h=4)

        def level_operands(half, n):
            if n == 0:
                return KC[:, 4 * half:4 * half + 4, :], QC[:, 4 * half:4 * half + 4, :]
            return LV[:, n % 2, 0], LV[:, n % 2, 1]

        block = ctx.enter_context(nc.Block())

        @block.tensor
        def _(pe):
            def claim(key):
                b, use = work.take(key)
                if use > 1:
                    pe.wait_ge(bank_free(b), use - 1)
                return psum[b], b

            def arrived(key):
                place, use = ring.where[key]
                pe.wait_ge(full(place), 16 * use)
                return ring_sb[:, place, :]

            def arrived_pair(name, c):
                views = [arrived((name, c, r)).rearrange("p (k n) -> p k n", n=512) for r in range(2)]
                return lambda k: views[k // 4][:, k % 4, :]

            def transposed(src, name, ready):
                pe.wait_ge(*ready)
                for j in range(KD // 2):
                    ps, b = claim((name, j))
                    for kk in range(2):
                        for t in range(T):
                            k = 2 * j + kk
                            last = nc.tensor.transpose(ps[:, 256 * kk + P * t:256 * kk + P * t + P],
                                                       src[:, t, P * k:P * k + P], ident)
                    last.then_inc(bank_full(b), 1)
                for j in range(KD // 2):
                    evacuated(pe, (name, j))

            def project_T(name, c, out_name):
                w = arrived_pair(name, c)
                for jj in range(2):
                    ps, b = claim((out_name, jj))
                    for u in range(2):
                        for k in range(KD):
                            j = 2 * jj + u
                            last = nc.tensor.matmul(ps[:, 256 * u:256 * u + 256], w(k)[:, P * j:P * j + P],
                                                    HT[:, k, :], start=(k == 0), stop=(k == KD - 1))
                    last.then_inc(bank_full(b), 1)
                for r in range(2):
                    done_at[(name, c, r)] = filled(b)

            def project(name, c, out_name):
                w = arrived_pair(name, c)
                for t in range(T):
                    ps, b = claim((out_name, t))
                    for k in range(KD):
                        last = nc.tensor.matmul(ps[:, :], HT[:, k, P * t:P * t + P], w(k),
                                                start=(k == 0), stop=(k == KD - 1))
                    last.then_inc(bank_full(b), 1)
                for r in range(2):
                    done_at[(name, c, r)] = filled(b)

            def out_project(name, src, frees, sums):
                if frees:
                    pe.wait_ge(sem("acc_free"), frees)
                for c in range(2):
                    w = arrived_pair(name, c)
                    for t in range(T):
                        for k in range(KD):
                            last = nc.tensor.matmul(acc[2 * t + c][:, :], src[:, k, P * t:P * t + P], w(k),
                                                    start=(k == 0), stop=(k == KD - 1))
                        last.then_inc(sem("acc_full"), 1)
                    for r in range(2):
                        done_at[(name, c, r)] = (sem("acc_full"), sums + 2 * c + 2)

            def gate_up(ps, wg, wu, j):
                for u, w in enumerate((wg, wu)):
                    for k in range(KD):
                        last = nc.tensor.matmul(ps[:, 256 * u:256 * u + 256], w[:, k, P * j:P * j + P],
                                                HT[:, k, :], start=(k == 0), stop=(k == KD - 1))
                return last

            def down(wd, j, i, first, last_group):
                for t in range(T):
                    for c in range(2):
                        last = nc.tensor.matmul(acc[2 * t + c][:, :], hs[:, i % 4, P * t:P * t + P],
                                                wd[:, j, 512 * c:512 * c + 512], start=first, stop=last_group,
                                                skip_group_check=True)
                return last

            pe.wait_ge(sem("consts_in"), 16)
            pe.wait_ge(sem("vecs_in"), 16 * 3)
            ps, b = claim("vecs")
            nc.tensor.transpose(ps[:, 0:6 * KD], vec_rows[:, :], consts[0:6 * KD, C_ID:C_ID + 6 * KD])\
                .then_inc(bank_full(b), 1)

            transposed(XN, "mix0", (sem("xn_ready"), 2))
            pe.wait_ge(sem("wf_in"), 16)
            ps, b = claim("flogit")
            for k in range(KD):
                last = nc.tensor.matmul(ps[0:NHB, 0:SEQ], wf[:, k, :], HT[:, k, :], start=(k == 0), stop=(k == KD - 1))
            last.then_inc(bank_full(b), 1)
            project_T("ab", 0, "qa")
            project_T("ab", 1, "ka")
            project("ab", 2, "va")
            for n, name in enumerate(("qa", "ka")):
                for jj in range(2):
                    evacuated(pe, (name, jj))
                    ps, b = claim(("rot", name, jj))
                    nc.tensor.matmul(ps[:, :], perm, QK[name][:, 2 * jj:2 * jj + 2, :],
                                     start=True, stop=True).then_inc(bank_full(b), 1)
            project_T("ab", 3, "qb")
            project_T("ab", 4, "kb")
            project("ab", 5, "vb")

            def scores(h):
                kind, j, r = ("a" if h < NHA else "b"), (h % NHA) // 2, HD * (h % 2)
                q, k = QK["q" + kind][r:r + HD, j, :], QK["k" + kind][r:r + HD, j, :]
                if h == 0:
                    pe.wait_ge(sem("rope_ready"), 4)
                if h == NHA:
                    for n in ("qb", "kb"):
                        for jj in range(2):
                            evacuated(pe, (n, jj))
                    pe.wait_ge(sem("fox_ready"), 1)
                ps, b = claim(("s", h))
                for t in range(T):
                    o = ps[:, P * t:P * t + P * (t + 1)]
                    last = nc.tensor.matmul(o, q[:, P * t:P * t + P], k[:, 0:P * (t + 1)],
                                            start=True, stop=(kind == "a"))
                    if kind == "b":
                        e = onehot[:, h - NHA, :]
                        nc.tensor.matmul(o, fox[:, 0, P * t:P * t + P], e[:, 0:P * (t + 1)], start=False, stop=False)
                        last = nc.tensor.matmul(o, e[:, 0:P], fox[:, 1, 0:P * (t + 1)], start=False, stop=True)
                last.then_inc(bank_full(b), 1)

            def probs_T(h):
                pe.wait_ge(sem("probs_ready"), h + 1)
                ps, b = claim(("p", h))
                s = S[h % SRING]
                for n, blk in enumerate((s[:, 0:P], s[:, P:2 * P], s[:, 2 * P:3 * P])):
                    last = nc.tensor.transpose(ps[:, P * n:P * n + P], blk, ident)
                last.then_inc(bank_full(b), 1)

            def values(h):
                evacuated(pe, ("p", h))
                if h % NHA == 0:
                    for t in range(T):
                        evacuated(pe, ("va" if h < NHA else "vb", t))
                pair = h // 2
                if h % 2 == 0 and pair >= 4:
                    pe.wait_ge(sem("ot_ready"), pair - 3)
                o = acc[pair % 4][HD * (h % 2):HD * (h % 2) + HD, 0:SEQ]
                pt = PT[h % 3]
                nc.tensor.matmul(o, V[:, 0, HD * h:HD * h + HD], pt[:, 0:2 * P], start=True, stop=False)
                nc.tensor.matmul(o[:, P:2 * P], V[:, 1, HD * h:HD * h + HD], pt[:, 2 * P:3 * P],
                                 start=False, stop=True).then_inc(sem("values_done"), 1)

            for i in range(NH + 3):
                if i < NH:
                    scores(i)
                if 2 <= i < NH + 2:
                    probs_T(i - 2)
                if i >= 3:
                    values(i - 3)

            pe.wait_ge(sem("ot_ready"), NH // 2)
            out_project("oab", OT, 0, 0)

            transposed(XN, "ffn0", (sem("xn_ready"), 4))
            pe.wait_ge(sem("acc_free"), 4)
            for j in range(n_ff + 2):
                if j < n_ff:
                    wg, wu = (arrived((n, j // 2)).rearrange("p (k n) -> p k n", k=KD) for n in ("wg", "wu"))
                    ps, b = claim(("gu", j))
                    gate_up(ps, wg, wu, j % 2).then_inc(bank_full(b), 1)
                    done_at[("wg", j // 2)] = done_at[("wu", j // 2)] = filled(b)
                if j >= 2:
                    i = j - 2
                    w = arrived(("wd", i // 2)).rearrange("p (k n) -> p k n", k=2)
                    evacuated(pe, ("gu", i))
                    down(w, i % 2, i, i == 0, i == n_ff - 1).then_inc(sem("hs_used"), 1)
                    done_at[("wd", i // 2)] = (sem("hs_used"), i + 1)

            transposed(XN, "mix1", (sem("xn_ready"), 6))
            for c, name in ((2, "f0"), (3, "f1"), (0, "q0"), (1, "q1")):
                project_T("c", c, name)
            for c, name in ((4, "v0"), (5, "v1"), (6, "g0"), (7, "g1")):
                project("c", c, name)

            for half in range(2):
                for n in range(len(LEVELS) + 2):
                    if n == 0:
                        for jj in range(2):
                            evacuated(pe, (f"q{half}", jj))
                        pe.wait_ge(sem("kc_ready"), 1)
                    else:
                        pe.wait_ge(sem("level_ready"), half * NLV + n)
                    kk, qq = level_operands(half, n)
                    for g in range(1 if n == 1 else 2):
                        ps, b = claim(("lv", half, n, g))
                        for i in range(4):
                            if n == 1:
                                lhs, rhs = kk[:, i, 0:P], qq[:, i, P:2 * P]
                            else:
                                hh, t = 2 * g + i // 2, i % 2
                                lhs, rhs = kk[:, hh, P * t:P * t + P], qq[:, hh, P * t:P * t + P]
                            last = nc.tensor.matmul(ps[:, P * i:P * i + P], lhs, rhs, start=True, stop=True)
                        last.then_inc(bank_full(b), 1)
                    done_at[("level", half, n)] = filled(b)
                evacuated(pe, ("lv", half, 1, 0))
                for g in range(2):
                    evacuated(pe, ("lv", half, NLV, g))
                for t in range(T):
                    evacuated(pe, (f"v{half}", t))
                for t in range(T):
                    ps, b = claim(("hgrn_o", half, t))
                    for i in range(4):
                        o = ps[:, P * i:P * i + P]
                        h = 4 * half + i
                        if t == 0:
                            last = nc.tensor.matmul(o, AT[:, i, 0, :], VC[:, 0, P * h:P * h + P], start=True, stop=True)
                        else:
                            nc.tensor.matmul(o, AX_[:, i, :], VC[:, 0, P * h:P * h + P], start=True, stop=False)
                            last = nc.tensor.matmul(o, AT[:, i, 1, :], VC[:, 1, P * h:P * h + P], start=False, stop=True)
                    last.then_inc(bank_full(b), 1)
                done_at[("at", half)] = filled(b)
            transposed(XN, "hgrn_out", (sem("hgrn_ready"), 1))
            out_project("oc", OT, 8, 4)

            transposed(XN, "ffn1", (sem("xn_ready"), 8))
            pe.wait_ge(sem("wr_in"), 16)
            ps, b = claim("router")
            for t in range(T):
                for k in range(KD):
                    last = nc.tensor.matmul(ps[:, NE * t:NE * t + NE], HT[:, k, P * t:P * t + P], wr[:, k, :],
                                            start=(k == 0), stop=(k == KD - 1))
            last.then_inc(bank_full(b), 1)
            pe.wait_ge(sem("combine_ready"), 1)
            pe.wait_ge(sem("zeros_ready"), 1)
            for e in range(NE):
                if e % 2 == 0:
                    ps, b = claim(("cb", e // 2))
                for t in range(T):
                    last = nc.tensor.matmul(ps[:, 256 * (e % 2) + P * t:256 * (e % 2) + P * t + P],
                                            combine[:, t, e:e + 1].to_broadcast([P, P]), ident, start=True, stop=True)
                if e % 2:
                    last.then_inc(bank_full(b), 1)
            pe.wait_ge(sem("acc_free"), 12)
            for t in range(T):
                for c in range(2):
                    nc.tensor.matmul(acc[2 * t + c][:, :], ident, X[:, t, 512 * c:512 * c + 512],
                                     start=True, stop=False, skip_group_check=True)
            moe_bank0 = work.at % WORK
            moe_bank_used = list(work.used)
            moe["bank"] = (moe_bank0 % WORK, moe_bank_used)
            with pe.Fori(0, NE) as e:
                def landed(n):
                    sl = (moe_slot0 + n) % SLOTS
                    pe.wait_ge(full(sl), (e * PER_SLOT + (n // SLOTS + 1 + moe_used[sl])) * 16)
                    return sl

                for j in range(n_e + 2):
                    if j < n_e:
                        g = j // 2
                        if j % 2 == 0:
                            sg_, su_ = landed(3 * g), landed(3 * g + 1)
                            wg, wu = (ring_sb[:, i, :].rearrange("p (k n) -> p k n", k=KD) for i in (sg_, su_))
                        b = (moe_bank0 + j) % WORK
                        pe.wait_ge(bank_free(b), e * PB + (moe_bank_used[b] + j // WORK))
                        gate_up(psum[b], wg, wu, j % 2).then_inc(bank_full(b), 1)
                    if j >= 2:
                        i = j - 2
                        if i % 2 == 0:
                            sd_ = landed(3 * (i // 2) + 2)
                            wd = ring_sb[:, sd_, :].rearrange("p (k n) -> p k n", k=2)
                        bi = (moe_bank0 + i) % WORK
                        pe.wait_ge(bank_free(bi), e * PB + (moe_bank_used[bi] + i // WORK + 1))
                        down(wd, i % 2, i + n_ff, False, False).then_inc(sem("hs_used"), 1)
            for t in range(T):
                for c in range(2):
                    last = nc.tensor.matmul(acc[2 * t + c][:, :], zeros[:, 0:P], X[:, t, 512 * c:512 * c + 512],
                                            start=False, stop=True, skip_group_check=True)
            last.then_inc(sem("acc_full"), 1)

        @block.sync
        def _(sp):
            sp.dma_start(X[:, :, :], x[0].rearrange("(t p) n -> p t n", p=P)).then_inc(sem("x_in"), 16)

            def load(place, src, view):
                dst = ring_sb[:, place, 0:view[0] * view[1]].rearrange("p (k n) -> p k n", k=view[0])
                sp.dma_start(dst, src).then_inc(full(place), 16)

            last_in = {}
            for key, src, view in chunks:
                place, use = ring.where[key]
                if place in last_in:
                    sp.wait_ge(*done_at[last_in[place]])
                last_in[place] = key
                load(place, src, view)

            def expert_chunk(e, n):
                g, m = divmod(n, 3)
                if m == 2:
                    return w_down_moe[0][e, 256 * g:256 * g + 256, :].rearrange("(k p) n -> p k n", p=P), (2, D)
                w = (w_gate_moe, w_up_moe)[m]
                return w[0][e, :, 256 * g:256 * g + 256].rearrange("(k p) n -> p k n", p=P), (KD, 256)

            def expert_load(e, n, eprev, nprev):
                g, m = divmod(nprev, 3)
                if m == 2:
                    sp.wait_ge(sem("hs_used"), eprev * n_e + (n_ff + 2 * g + 2))
                else:
                    j = 2 * g + 1
                    b = (moe["bank"][0] + j) % WORK
                    sp.wait_ge(bank_full(b), eprev * PB + (moe["bank"][1][b] + j // WORK + 1))
                load((moe_slot0 + n) % SLOTS, *expert_chunk(e, n))

            for n in range(SLOTS):
                place = (moe_slot0 + n) % SLOTS
                sp.wait_ge(*done_at[last_in[place]])
                load(place, *expert_chunk(0, n))
            with sp.Fori(0, NE - 1) as e:
                for n in range(SLOTS, MOE_CHUNKS):
                    expert_load(e, n, e, n - SLOTS)
                for n in range(SLOTS):
                    expert_load(e + 1, n, e, MOE_CHUNKS - SLOTS + n)
            for n in range(SLOTS, MOE_CHUNKS):
                expert_load(NE - 1, n, NE - 1, n - SLOTS)

            for t in range(T):
                sp.wait_ge(sem("out_ready"), t + 1)
                sp.dma_start(out[0, P * t:P * t + P, :], XN[:, t, :]).then_inc(sem("out_done"), 16)
            sp.wait_ge(sem("out_done"), 16 * T)

        @block.gpsimd
        def _(pool):
            nc.gpsimd.memset(zeros[:, :], 0.0).then_inc(sem("zeros_ready"), 1)
            pool.wait_ge(sem("ot_ready"), NH // 2)
            nc.gpsimd.memset(arena[:, 0:4096], 0.0).then_inc(sem("levels_cleared"), 1)
            pool.wait_ge(sem("gnorm_in"), 16)
            for c in range(2):
                for t in range(T):
                    evacuated(pool, (f"g{c}", t))
                    sgv = SG[:, t, 512 * c:512 * c + 512].rearrange("p (h n) -> p h n", h=4)
                    nc.gpsimd.tensor_tensor(sgv, sgv, gnorm[:, :].unsqueeze(1).to_broadcast([P, 4, P]),
                                            ALU.mult).then_inc(sem("gate_ready"), 1)

        @block.scalar
        def _(act):
            act.dma_start(consts[:, :], c_float).then_inc(sem("consts_in"), 16)
            act.dma_start(vec_rows[0:2 * KD, :], norm_mix.rearrange("l (k p) -> (l k) p", p=P)).then_inc(sem("vecs_in"), 16)
            act.dma_start(vec_rows[2 * KD:4 * KD, :], norm_ffn.rearrange("l (k p) -> (l k) p", p=P)).then_inc(sem("vecs_in"), 16)
            act.dma_start(vec_rows[4 * KD:6 * KD, :], lower_bounds.rearrange("l (k p) -> (l k) p", p=P)).then_inc(sem("vecs_in"), 16)
            act.dma_start(wf[:, :, :], w_ab[:, 3072:3072 + NHB].rearrange("(k p) n -> p k n", p=P)).then_inc(sem("wf_in"), 16)
            act.dma_start(pos_i[:, :], positions[0:1, :].partition_broadcast(P)).then_inc(sem("pos_in"), 16)
            act.dma_start(fbias[:, :], fgate_bias[0:1, :].rearrange("a h -> h a")).then_inc(sem("fox_in"), 16)
            act.dma_start(onehot, c_onehot).then_inc(sem("onehot_in"), 16)
            act.dma_start(level_mask[:, :, :], c_level).then_inc(sem("level_in"), 16)
            act.dma_start(wr[:, :, :], router[0].rearrange("(k p) n -> p k n", p=P)).then_inc(sem("wr_in"), 16)
            act.dma_start(gnorm[:, :], gnorm_c[0:1, :].partition_broadcast(P)).then_inc(sem("gnorm_in"), 16)
            act.dma_start(final_gain[:, :], norm_final.rearrange("(a n) -> a n", a=1).partition_broadcast(P)).then_inc(sem("final_in"), 16)

            def norm(n, x_ready):
                act.wait_ge(*x_ready)
                for t in range(T):
                    nc.scalar.activation(XN[:, t, :], X[:, t, :], ACT.Square,
                                         accum_out=small[:, SS + t:SS + t + 1]).then_inc(sem("squares"), 1)
                act.wait_ge(sem("ms_ready"), n + 1)
                nc.scalar.activation(small[:, MS:MS + 2], small[:, MS:MS + 2], ACT.Sqrt).then_inc(sem("rms_ready"), 1)
                act.wait_ge(sem("rs_ready"), n + 1)
                nc.scalar.activation(XN[:, 1, :], X[:, 1, :], ACT.Copy, scale=small[:, RS + 1:RS + 2])\
                    .then_inc(sem("xn_ready"), 1)

            def evacuate_T(name, g):
                for j in (1, 3):
                    ps, b = product(act, (name, j))
                    for kk in range(2):
                        k = 2 * j + kk
                        if g is None:
                            last = nc.scalar.activation(OT[:, k, :], ps[:, 256 * kk:256 * kk + 256], ACT.Copy)
                        else:
                            last = nc.scalar.activation(HT[:, k, :], ps[:, 256 * kk:256 * kk + 256], ACT.Copy,
                                                        scale=vec_cols[:, g + k:g + k + 1])
                    last.then_inc(bank_free(b), 1)

            norm(0, (sem("x_in"), 16))
            evacuated(act, "vecs")
            evacuate_T("mix0", gain["mix0"])

            def copy_T(name, dst, scale, func=ACT.Copy):
                for jj in range(2):
                    ps, b = product(act, (name, jj))
                    nc.scalar.activation(dst[:, 2 * jj:2 * jj + 2, :], ps[:, :].rearrange("p (u q) -> p u q", u=2),
                                         func, scale=scale).then_inc(bank_free(b), 1)

            act.wait_ge(sem("angle_ready"), 1)
            nc.scalar.activation(rope[:, 0:2, :], rope[:, 2:4, :], ACT.Sin).then_inc(sem("trig_ready"), 1)
            copy_T("qa", QK["qa"], HD ** -0.5)
            copy_T("ka", QK["ka"], 1.0)
            act.wait_ge(sem("fox_abs"), 1)
            nc.scalar.activation(fox[:, 3, :], fox[:, 3, :], ACT.Exp, scale=-1.0).then_inc(sem("fox_exp"), 1)
            act.wait_ge(sem("fox_exp"), 1)
            nc.scalar.activation(fox[:, 3, :], fox[:, 3, :], ACT.Ln, bias=1.0).then_inc(sem("fox_ln"), 1)
            copy_T("qb", QK["qb"], HD ** -0.5)
            copy_T("kb", QK["kb"], 1.0)

            for i in range(NH + 2):
                if i < NH:
                    h = i
                    act.wait_ge(sem("max_ready"), h + 1)
                    for t in range(T):
                        s_ = S[h % SRING][:, P * t:P * t + P * (t + 1)]
                        nc.scalar.activation(s_, s_, ACT.Exp, bias=small[:, MX + 2 * h + t:MX + 2 * h + t + 1],
                                             accum_out=small[:, SM + 2 * h + t:SM + 2 * h + t + 1])\
                            .then_inc(sem("exp_ready"), 1)
                if i >= 2:
                    h = i - 2
                    if h >= 3:
                        act.wait_ge(sem("values_done"), h - 2)
                    ps, b = product(act, ("p", h))
                    nc.scalar.activation(PT[h % 3], ps[:, 0:3 * P], ACT.Copy).then_inc(bank_free(b), 1)

            norm(1, (sem("acc_free"), 4))
            evacuate_T("ffn0", gain["ffn0"])
            for j in range(n_ff):
                ps, b = product(act, ("gu", j))
                nc.scalar.activation(sg[:, j % 4, :], ps[:, 0:SEQ], ACT.Silu).then_inc(sem("sg_ready"), 1)

            norm(2, (sem("acc_free"), 8))
            act.wait_ge(sem("lb_max"), 1)
            nc.scalar.activation(small[:, LBC:LBC + 16], small[:, LBC:LBC + 16], ACT.Exp).then_inc(sem("lb_exp"), 1)
            evacuate_T("mix1", gain["mix1"])
            copy_T("f0", BC[:, 0:4, :], 1.0, ACT.Sigmoid)
            copy_T("f1", BC[:, 4:8, :], 1.0, ACT.Sigmoid)
            copy_T("q0", QC[:, 0:4, :], P ** -0.5)
            copy_T("q1", QC[:, 4:8, :], P ** -0.5)
            act.wait_ge(sem("f_ready"), 1)
            nc.scalar.activation(BC[:, :, :], BC[:, :, :], ACT.Ln).then_inc(sem("logf_ready"), 1)
            for c in range(2):
                for t in range(T):
                    ps, b = product(act, (f"g{c}", t))
                    nc.scalar.activation(SG[:, t, 512 * c:512 * c + 512], ps[:, :], ACT.Silu).then_inc(bank_free(b), 1)
            for half in range(2):
                for n in range(1, NLV + 1):
                    if half == 0 and n == 1:
                        act.wait_ge(sem("levels_cleared"), 1)
                    act.wait_ge(sem("delta_ready"), half * NLV + n)
                    if n >= 3:
                        act.wait_ge(*done_at[("level", half, n - 2)])
                    elif half == 1:
                        act.wait_ge(*done_at[("level", 0, NLV - (1 if (NLV - n) % 2 else 0))])
                    for r in range(2):
                        width = P if n == 1 else LEVELS[n - 2]
                        dst, src = (v.rearrange("p h (m side z) -> p (h m) side z", side=2, z=width)[:, :, r, :]
                                    for v in (LV[:, n % 2, r], DL))
                        last = nc.scalar.activation(dst, src, ACT.Exp, scale=(-1.0, 1.0)[r])
                    last.then_inc(sem("decay_ready"), 1)
                for t in range(T):
                    ps, b = product(act, ("hgrn_o", half, t))
                    nc.scalar.activation(XN[:, t, 512 * half:512 * half + 512], ps[:, :], ACT.Copy).then_inc(bank_free(b), 1)
            act.wait_ge(sem("head_ms"), 1)
            nc.scalar.activation(small[:, MX:MX + 16], small[:, MX:MX + 16], ACT.Sqrt).then_inc(sem("head_rms"), 1)
            evacuate_T("hgrn_out", None)

            norm(3, (sem("acc_free"), 12))
            evacuate_T("ffn1", gain["ffn1"])
            act.wait_ge(sem("top_gap"), 1)
            nc.scalar.activation(route[:, :, 32:33], route[:, :, 32:33], ACT.Exp).then_inc(sem("gap_exp"), 1)
            for i in range(NE // 2):
                ps, b = product(act, ("cb", i))
                nc.scalar.activation(CB[:, 2 * i:2 * i + 2, :], ps[:, :].rearrange("p (u q) -> p u q", u=2),
                                     ACT.Copy).then_inc(bank_free(b), 1)
            with act.Fori(0, NE) as e:
                for j in range(n_e):
                    b = (moe["bank"][0] + j) % WORK
                    act.wait_ge(bank_full(b), e * PB + (moe["bank"][1][b] + j // WORK + 1))
                    nc.scalar.activation(sg[:, (n_ff + j) % 4, :], psum[b][:, 0:SEQ], ACT.Silu).then_inc(sem("sg_ready"), 1)
            norm(4, (sem("acc_free"), 16))

        @block.vector
        def _(dve):
            count = [0]

            def link(ins):
                count[0] += 1
                ins.then_inc(sem("dve_chain"), 1)
                dve.wait_ge(sem("dve_chain"), count[0])

            def norm(n):
                dve.wait_ge(sem("squares"), 2 * n + 2)
                nc.vector.tensor_scalar(small[:, MS:MS + 2], small[:, SS:SS + 2], 1.0 / D, EPS, ALU.mult, ALU.add)\
                    .then_inc(sem("ms_ready"), 1)
                dve.wait_ge(sem("rms_ready"), n + 1)
                nc.vector.reciprocal(small[:, RS:RS + 2], small[:, MS:MS + 2]).then_inc(sem("rs_ready"), 1)
                dve.wait_ge(sem("rs_ready"), n + 1)
                nc.vector.tensor_scalar(XN[:, 0, :], X[:, 0, :], small[:, RS:RS + 1], None, ALU.mult)\
                    .then_inc(sem("xn_ready"), 1)

            def evacuate_T(name, g):
                for j in (0, 2):
                    ps, b = product(dve, (name, j))
                    for kk in range(2):
                        k = 2 * j + kk
                        if g is None:
                            last = nc.vector.tensor_copy(OT[:, k, :], ps[:, 256 * kk:256 * kk + 256])
                        else:
                            last = nc.vector.tensor_scalar(HT[:, k, :], ps[:, 256 * kk:256 * kk + 256],
                                                           vec_cols[:, g + k:g + k + 1], None, ALU.mult)
                    last.then_inc(bank_free(b), 1)

            def residual(wait, already):
                for n in range(4):
                    c, t = divmod(n, 2)
                    dve.wait_ge(wait[0], wait[1] + (n + 1 if already is None else 0))
                    xs = X[:, t, 512 * c:512 * c + 512]
                    nc.vector.tensor_tensor(xs, xs, acc[2 * t + c][:, :], ALU.add).then_inc(sem("acc_free"), 1)

            two_pi = 2.0 * np.pi
            C1 = 6.28125
            C2 = float(np.float32(two_pi - C1))
            C3 = float(two_pi - C1 - C2)
            ROUND = 12582912.0
            PI_IN = float(np.nextafter(np.float32(np.pi), np.float32(0)))
            dve.wait_ge(sem("pos_in"), 16)
            dve.wait_ge(sem("consts_in"), 16)
            link(nc.vector.tensor_copy(rope[:, 4, :], pos_i[:, :]))
            link(nc.vector.tensor_scalar(rope[:, 4, :], rope[:, 4, :], consts[:, C_FREQ:C_FREQ + 1], None, ALU.mult))
            link(nc.vector.tensor_scalar(rope[:, 5, :], rope[:, 4, :], 1.0 / two_pi, ROUND, ALU.mult, ALU.add))
            link(nc.vector.tensor_scalar(rope[:, 5, :], rope[:, 5, :], ROUND, None, ALU.subtract))
            for part in (C1, C2, C3):
                link(nc.vector.scalar_tensor_tensor(rope[:, 4, :], rope[:, 5, :], -part, rope[:, 4, :], ALU.mult, ALU.add))
            link(nc.vector.tensor_scalar(rope[:, 3, :], rope[:, 4, :], PI_IN, -PI_IN, ALU.min, ALU.max))
            link(nc.vector.tensor_scalar(rope[:, 2, :], rope[:, 4, :], np.pi / 2, None, ALU.add))
            link(nc.vector.tensor_scalar(rope[:, 5, :], rope[:, 2, :], np.pi, -two_pi, ALU.is_gt, ALU.mult))
            link(nc.vector.tensor_tensor(rope[:, 2, :], rope[:, 2, :], rope[:, 5, :], ALU.add))
            nc.vector.tensor_scalar(rope[:, 2, :], rope[:, 2, :], PI_IN, -PI_IN, ALU.min, ALU.max)\
                .then_inc(sem("angle_ready"), 1)

            ps, b = product(dve, "vecs")
            nc.vector.tensor_copy(vec_cols[:, :], ps[:, 0:6 * KD]).then_inc(bank_free(b), 1)
            evacuated(dve, "vecs")
            norm(0)
            evacuate_T("mix0", gain["mix0"])

            dve.wait_ge(sem("fox_in"), 16)
            dve.wait_ge(sem("onehot_in"), 16)
            ps, b = product(dve, "flogit")
            nc.vector.tensor_scalar(fox[:, 2, :], ps[0:NHB, 0:SEQ], fbias[:, 0:1], None, ALU.add).then_inc(bank_free(b), 1)
            evacuated(dve, "flogit")
            nc.vector.scalar_tensor_tensor(fox[:, 3, :], fox[:, 2, :], -1.0, fox[:, 2, :], ALU.mult, ALU.max)\
                .then_inc(sem("fox_abs"), 1)
            link(nc.vector.tensor_scalar(fox[:, 2, :], fox[:, 2, :], 0.0, None, ALU.min))
            link(nc.vector.memset(fox[:, 4, :], 1.0))

            def rotate(name, n):
                for jj in range(2):
                    ps, b = product(dve, ("rot", name, jj))
                    raw = QK[name][:, 2 * jj:2 * jj + 2, :]
                    rt = rtmp[:, 0:512].rearrange("p (u q) -> p u q", u=2)
                    if n == jj == 0:
                        dve.wait_ge(sem("trig_ready"), 1)
                    link(nc.vector.tensor_tensor(raw, raw, cosT.unsqueeze(1).to_broadcast([P, 2, SEQ]), ALU.mult))
                    nc.vector.tensor_tensor(rt, ps[:, :].rearrange("p (u q) -> p u q", u=2),
                                            sinT.unsqueeze(1).to_broadcast([P, 2, SEQ]), ALU.mult).then_inc(bank_free(b), 1)
                    evacuated(dve, ("rot", name, jj))
                    nc.vector.tensor_tensor(raw, raw, rt, ALU.add).then_inc(sem("rope_ready"), 1)
                    dve.wait_ge(sem("rope_ready"), 2 * n + jj + 1)

            def copy_tokens(name, dst, c0):
                for t in range(T):
                    ps, b = product(dve, (name, t))
                    nc.vector.tensor_copy(dst[:, t, c0:c0 + 512], ps[:, :]).then_inc(bank_free(b), 1)

            copy_tokens("va", V, 0)
            rotate("qa", 0)
            rotate("ka", 1)
            dve.wait_ge(sem("fox_ln"), 1)
            link(nc.vector.tensor_tensor(fox[:, 2, :], fox[:, 2, :], fox[:, 3, :], ALU.subtract))
            link(nc.vector.tensor_tensor_scan(fox[:, 0, :], fox[:, 4, :], fox[:, 2, :], 0.0, ALU.mult, ALU.add))
            nc.vector.tensor_scalar(fox[:, 1, :], fox[:, 0, :], -1.0, None, ALU.mult).then_inc(sem("fox_ready"), 1)
            copy_tokens("vb", V, 512)

            for i in range(NH + 5):
                if i < NH:
                    h = i
                    if h >= SRING:
                        dve.wait_ge(bank_full(work.where[("p", h - SRING)][0]), work.where[("p", h - SRING)][1])
                    ps, b = product(dve, ("s", h))
                    m = score_mask["a" if h < NHA else "b"]
                    for t in range(T):
                        at = slice(P * t, P * t + P * (t + 1))
                        last = nc.vector.tensor_tensor_reduce(
                            out=S[h % SRING][:, at], in0=ps[:, at], in1=m[:, at], scale=1.0, scalar=-3.0e38,
                            op0=ALU.add, op1=ALU.max, accum_out=small[:, MX + 2 * h + t:MX + 2 * h + t + 1])
                    last.then_inc(bank_free(b), 1)
                    evacuated(dve, ("s", h))
                    nc.vector.tensor_scalar(small[:, MX + 2 * h:MX + 2 * h + 2], small[:, MX + 2 * h:MX + 2 * h + 2],
                                            -1.0, None, ALU.mult).then_inc(sem("max_ready"), 1)
                if 1 <= i <= NH:
                    h = i - 1
                    dve.wait_ge(sem("exp_ready"), 2 * h + 2)
                    link(nc.vector.reciprocal(small[:, RI + 2 * h:RI + 2 * h + 2], small[:, SM + 2 * h:SM + 2 * h + 2]))
                    for t in range(T):
                        s_ = S[h % SRING][:, P * t:P * t + P * (t + 1)]
                        last = nc.vector.tensor_scalar(s_, s_, small[:, RI + 2 * h + t:RI + 2 * h + t + 1], None, ALU.mult)
                    last.then_inc(sem("probs_ready"), 1)
                if i >= 4 and (i - 4) % 2 == 1:
                    pair = (i - 4) // 2
                    dve.wait_ge(sem("values_done"), 2 * pair + 2)
                    nc.vector.tensor_copy(OT[:, pair, :], acc[pair % 4][:, 0:SEQ]).then_inc(sem("ot_ready"), 1)

            residual((sem("acc_full"), 0), None)
            norm(1)
            evacuate_T("ffn0", gain["ffn0"])
            for j in range(n_ff):
                ps, b = product(dve, ("gu", j))
                dve.wait_ge(sem("sg_ready"), j + 1)
                if j >= 4:
                    dve.wait_ge(sem("hs_used"), j - 3)
                nc.vector.tensor_tensor(hs[:, j % 4, :], sg[:, j % 4, :], ps[:, SEQ:2 * SEQ], ALU.mult)\
                    .then_inc(bank_free(b), 1)
            residual((sem("hs_used"), n_ff), 0)

            l0, l1 = vec_cols[:, 4 * KD:5 * KD], vec_cols[:, 5 * KD:6 * KD]
            lb, oml = small[:, LBC:LBC + 8], small[:, OML:OML + 8]
            link(nc.vector.tensor_tensor(small[:, 120:128], l0, l1, ALU.max))
            link(nc.vector.tensor_tensor(lb, l1, small[:, 120:128], ALU.subtract))
            nc.vector.tensor_tensor(oml, l0, small[:, 120:128], ALU.subtract).then_inc(sem("lb_max"), 1)
            norm(2)
            dve.wait_ge(sem("lb_exp"), 1)
            link(nc.vector.tensor_tensor(oml, oml, lb, ALU.add))
            link(nc.vector.reciprocal(oml, oml))
            link(nc.vector.tensor_tensor(lb, lb, oml, ALU.mult))
            link(nc.vector.tensor_scalar(oml, lb, -1.0, 1.0, ALU.mult, ALU.add))
            evacuate_T("mix1", gain["mix1"])
            for c in range(2):
                for jj in range(2):
                    evacuated(dve, (f"f{c}", jj))
            for h in range(NHC):
                last = nc.vector.tensor_scalar(BC[:, h, :], BC[:, h, :], oml[:, h:h + 1], lb[:, h:h + 1], ALU.mult, ALU.add)
            link(last)
            nc.vector.tensor_scalar(KC[:, :, :], BC[:, :, :], -1.0, 1.0, ALU.mult, ALU.add).then_inc(sem("kc_ready"), 1)
            dve.wait_ge(sem("kc_ready"), 1)
            nc.vector.tensor_scalar(BC[:, :, :], BC[:, :, :], 2.0 ** -63, None, ALU.max).then_inc(sem("f_ready"), 1)
            copy_tokens("v0", VC, 0)
            copy_tokens("v1", VC, 512)
            dve.wait_ge(sem("logf_ready"), 1)
            for h in range(NHC):
                last = nc.vector.tensor_tensor_scan(BC[:, h, :], consts[:, C_RST:C_RST + SEQ], BC[:, h, :], 0.0,
                                                    ALU.mult, ALU.add)
            link(last)

            def delta(half, n):
                bh = BC[:, 4 * half:4 * half + 4, :]
                if n == 1:
                    ends = [bh[:, :, CHUNK * c + CHUNK - 1:CHUNK * c + CHUNK] for c in range(4)]
                    wide = [P, 4, CHUNK]
                    d = [DL[:, :, CHUNK * c:CHUNK * c + CHUNK] for c in range(4)]
                    s4 = [bh[:, :, CHUNK * c:CHUNK * c + CHUNK] for c in range(4)]
                    nc.vector.tensor_tensor(d[1], s4[1], ends[1].to_broadcast(wide), ALU.subtract)
                    link(nc.vector.tensor_tensor(d[0], s4[0], ends[0].to_broadcast(wide), ALU.subtract))
                    nc.vector.tensor_tensor(d[0], d[0], ends[1].to_broadcast(wide), ALU.subtract)
                    nc.vector.tensor_copy(d[2], s4[2])
                    last = nc.vector.tensor_tensor(d[3], s4[3], ends[2].to_broadcast(wide), ALU.add)
                elif LEVELS[n - 2] == CHUNK:
                    v, dv = (u.rearrange("p h (m side z) -> p (h m) side z", side=2, z=CHUNK) for u in (bh, DL))
                    nc.vector.tensor_tensor(dv[:, :, 0, :], v[:, :, 0, :],
                                            v[:, :, 0, CHUNK - 1:CHUNK].to_broadcast([P, 8, CHUNK]), ALU.subtract)
                    last = nc.vector.tensor_copy(dv[:, :, 1, :], v[:, :, 1, :])
                else:
                    width = LEVELS[n - 2]
                    v, dv = (u.rearrange("p h (m z) -> p (h m) z", z=2 * width) for u in (bh, DL))
                    last = nc.vector.tensor_tensor(dv, v, v[:, :, width - 1:width].to_broadcast([P, 4 * SEQ // (2 * width), 2 * width]),
                                                   ALU.subtract)
                last.then_inc(sem("delta_ready"), 1)

            def scale_operands(half, n):
                width = P if n == 1 else LEVELS[n - 2]
                for r, src in enumerate((KC, QC)):
                    dst, sv = (v.rearrange("p h (m side z) -> p (h m) side z", side=2, z=width)[:, :, r, :]
                               for v in (LV[:, n % 2, r], src[:, 4 * half:4 * half + 4, :]))
                    last = nc.vector.tensor_tensor(dst, dst, sv, ALU.mult)
                last.then_inc(sem("level_ready"), 1)

            def select(half, n):
                if n == 1:
                    ps, b = product(dve, ("lv", half, 1, 0))
                    nc.vector.tensor_copy(AX_, ps[:, :].rearrange("p (h q) -> p h q", h=4)).then_inc(bank_free(b), 1)
                    return
                for g in range(2):
                    ps, b = product(dve, ("lv", half, n, g))
                    dst = AT[:, 2 * g:2 * g + 2].rearrange("p h t q -> p (h t) q")
                    pv = ps[:, :].rearrange("p (h q) -> p h q", h=4)
                    if n == 0:
                        last = nc.vector.tensor_tensor(dst, pv, consts[:, C_DIAG:C_DIAG + P].unsqueeze(1)
                                                       .to_broadcast([P, 4, P]), ALU.mult)
                    else:
                        last = nc.vector.copy_predicated(dst, level_mask[:, n - 2, :].unsqueeze(1)
                                                         .to_broadcast([P, 4, P]), pv)
                    last.then_inc(bank_free(b), 1)
                evacuated(dve, ("lv", half, n, 1))

            dve.wait_ge(sem("level_in"), 16)
            for half in range(2):
                for jj in range(2):
                    evacuated(dve, (f"q{half}", jj))
                if half == 1:
                    dve.wait_ge(*done_at[("at", 0)])
                    dve.wait_ge(sem("decay_ready"), NLV)
                delta(half, 1)
                for n in range(1, NLV + 1):
                    dve.wait_ge(sem("decay_ready"), half * NLV + n)
                    if n < NLV:
                        delta(half, n + 1)
                    scale_operands(half, n)
                    select(half, n - 1)
                select(half, NLV)

            for half in range(2):
                for t in range(T):
                    evacuated(dve, ("hgrn_o", half, t))
            heads = XN[:, :, :].rearrange("p t (h n) -> p (t h) n", n=P)
            sq = A[0][:, :].rearrange("p (g n) -> p g n", n=P)
            link(nc.vector.tensor_tensor(sq, heads, heads, ALU.mult))
            hm = small[:, MX:MX + 16]
            link(nc.vector.tensor_reduce(hm, sq, AX_X, ALU.add))
            nc.vector.tensor_scalar(hm, hm, 1.0 / P, EPS, ALU.mult, ALU.add).then_inc(sem("head_ms"), 1)
            dve.wait_ge(sem("head_rms"), 1)
            link(nc.vector.reciprocal(hm, hm))
            link(nc.vector.tensor_tensor(heads, heads, hm.unsqueeze(2).to_broadcast([P, 16, P]), ALU.mult))
            dve.wait_ge(sem("gate_ready"), 4)
            nc.vector.tensor_tensor(XN[:, :, :], XN[:, :, :], SG, ALU.mult).then_inc(sem("hgrn_ready"), 1)
            evacuate_T("hgrn_out", None)
            residual((sem("acc_full"), 4), None)
            norm(3)
            evacuate_T("ffn1", gain["ffn1"])

            ps, b = product(dve, "router")
            nc.vector.tensor_copy(route[:, :, 0:NE], ps[:, 0:2 * NE].rearrange("p (t e) -> p t e", t=T)).then_inc(bank_free(b), 1)
            evacuated(dve, "router")
            for t in range(T):
                link(nc.vector.max(route[:, t, 8:16], route[:, t, 0:NE]))
                link(nc.vector.max_index(route[:, t, 16:24].bitcast(U32), route[:, t, 8:16], route[:, t, 0:NE]))
            link(nc.vector.tensor_copy(route[:, :, 24:32], route[:, :, 16:24].bitcast(U32)))
            nc.vector.tensor_tensor(route[:, :, 32:33], route[:, :, 9:10], route[:, :, 8:9], ALU.subtract)\
                .then_inc(sem("top_gap"), 1)
            dve.wait_ge(sem("gap_exp"), 1)
            link(nc.vector.tensor_scalar(route[:, :, 33:34], route[:, :, 32:33], 1.0, None, ALU.add))
            link(nc.vector.reciprocal(route[:, :, 34:35], route[:, :, 33:34]))
            link(nc.vector.tensor_tensor(route[:, :, 35:36], route[:, :, 32:33], route[:, :, 34:35], ALU.mult))
            iota = consts[:, C_IOTA:C_IOTA + NE]
            for t in range(T):
                link(nc.vector.tensor_scalar(route[:, t, 40:48], iota, route[:, t, 24:25], route[:, t, 34:35],
                                             ALU.is_equal, ALU.mult))
                link(nc.vector.tensor_scalar(route[:, t, 48:56], iota, route[:, t, 25:26], route[:, t, 35:36],
                                             ALU.is_equal, ALU.mult))
            nc.vector.tensor_tensor(combine[:, :, :], route[:, :, 40:48], route[:, :, 48:56], ALU.add)\
                .then_inc(sem("combine_ready"), 1)

            evacuated(dve, ("cb", NE // 2 - 1))
            with dve.Fori(0, NE) as e:
                for j in range(n_e):
                    b = (moe["bank"][0] + j) % WORK
                    i = n_ff + j
                    dve.wait_ge(sem("sg_ready"), e * n_e + (i + 1))
                    nc.vector.tensor_tensor(sg[:, i % 4, :], sg[:, i % 4, :], CB[:, e, :], ALU.mult)\
                        .then_inc(sem("sg_scaled"), 1)
                    dve.wait_ge(sem("sg_scaled"), e * n_e + (j + 1))
                    dve.wait_ge(sem("hs_used"), e * n_e + (i - 3))
                    nc.vector.tensor_tensor(hs[:, i % 4, :], sg[:, i % 4, :], psum[b][:, SEQ:2 * SEQ], ALU.mult)\
                        .then_inc(bank_free(b), 1)
            dve.wait_ge(sem("acc_full"), 9)
            for n in range(4):
                c, t = divmod(n, 2)
                nc.vector.tensor_copy(X[:, t, 512 * c:512 * c + 512], acc[2 * t + c][:, :]).then_inc(sem("acc_free"), 1)
            norm(4)
            dve.wait_ge(sem("xn_ready"), 10)
            dve.wait_ge(sem("final_in"), 16)
            for t in range(T):
                nc.vector.tensor_tensor(XN[:, t, :], XN[:, t, :], final_gain[:, :], ALU.mult).then_inc(sem("out_ready"), 1)


_INS = ["x", "positions", "norm_mix", "norm_ffn", "w_in_ab", "fgate_bias", "w_out_ab", "w_in_c",
        "lower_bounds", "gnorm_c", "w_out_c", "w_gate_ffn", "w_up_ffn", "w_down_ffn", "router",
        "w_gate_moe", "w_up_moe", "w_down_moe", "norm_final"]


def kernel(**inputs):
    import numpy as _np
    import concourse.bacc as _bacc
    from concourse import mybir as _mybir
    from concourse.bass_utils import run_bass_kernel_spmd as _run

    nc = _bacc.Bacc("TRN2", target_bir_lowering=False, num_devices=1)
    arrays, args = {}, []
    every = {n: _np.ascontiguousarray(inputs[n]) for n in _INS}
    every.update(shape_constants())
    for name, a in every.items():
        arrays[f"in_{name}"] = a
        args.append(nc.dram_tensor(f"in_{name}", a.shape, _mybir.dt.from_np(a.dtype), kind="ExternalInput").ap())
    args.append(nc.dram_tensor("out_0", (1, SEQ, D), F32, kind="ExternalOutput").ap())
    trunk(nc, *args)
    r = _run(nc, [arrays], core_ids=[0])
    return r.results[0]["out_0"]
```

```python
from contextlib import ExitStack

import numpy as np
import concourse.bass as bass
from concourse import mybir

ALU = mybir.AluOpType
ACT = mybir.ActivationFunctionType
F32 = mybir.dt.float32
F32R = mybir.dt.float32r
I32 = mybir.dt.int32
U32 = mybir.dt.uint32
AX_X = mybir.AxisListType.X

P = 128
SEQ = 256
T = SEQ // P
D = 1024
KD = D // P
HD = 64
NHA = 8
NHB = 8
NH = NHA + NHB
ROPE_DIM = HD // 4
ROPE_THETA = 500000.0
DILATED = ((128, 1), (512, 4), (2048, 16))
NHC = 8
CHUNK = 64
FF = 2816
NE = 8
FFE = 3584
EPS = 1e-6
NEG = -1.0e30

RAW = 6
SPLIT = 3
CHUNK_F = 2048
WORK = 4
BANKS_E = 6
LEVELS = (64, 32, 16, 8, 4, 2, 1)

C_ID, C_PERM, C_MA, C_MB, C_RST, C_FREQ, C_TRI, C_ONE, C_SLOT, C_IOTA, C_END = np.cumsum(
    [0, P, P, 3 * P, 3 * P, SEQ, 1, P, P, P, NE]).tolist()


def shape_constants():
    c = np.zeros((P, C_END), np.float32)
    c[:, C_ID:C_ID + P] = np.eye(P)
    half = ROPE_DIM // 2
    for base in range(0, P, HD):
        for i in range(half):
            c[base + half + i, C_PERM + base + i] = -1.0
            c[base + i, C_PERM + base + half + i] = 1.0
            f = np.power(np.float32(ROPE_THETA), -np.float32(i) / np.float32(half), dtype=np.float32)
            c[base + i, C_FREQ] = c[base + half + i, C_FREQ] = f
    q = np.arange(SEQ)[:, None]
    k = np.arange(SEQ)[None, :]
    count = np.zeros((SEQ, SEQ))
    for window, dilation in DILATED:
        count += (q >= k) & (q - k <= window) & ((q - k) % dilation == 0)
    dilated = np.where(count > 0, np.log(np.maximum(count, 1)), NEG)
    causal = np.where(q >= k, 0.0, NEG)
    for off, m in ((C_MA, dilated), (C_MB, causal)):
        c[:, off:off + P] = m[:P, :P]
        c[:, off + P:off + 3 * P] = m[P:, :]
    c[:, C_RST:C_RST + SEQ] = (np.arange(SEQ) % CHUNK != 0)[None, :]
    c[:, C_TRI:C_TRI + P] = np.arange(P)[:, None] < np.arange(P)[None, :]
    c[:, C_ONE:C_ONE + P] = 1.0
    c[:, C_SLOT:C_SLOT + P] = np.arange(P)[None, :]
    c[:, C_IOTA:C_IOTA + NE] = np.arange(NE)[None, :]
    onehot = np.zeros((NHB, NHB, SEQ), np.float32)
    for h in range(NHB):
        onehot[h, h, :] = 1.0
    s = np.arange(P)[:, None]
    t = np.arange(P)[None, :]
    level = np.zeros((P, len(LEVELS), P), np.int32)
    for n, w in enumerate(LEVELS):
        level[:, n, :] = (s // (2 * w) == t // (2 * w)) & (s % (2 * w) < w) & (t % (2 * w) >= w)
    return {"c_float": c, "c_onehot": onehot, "c_level": level}


class Turns:

    def __init__(self, n):
        self.n, self.at, self.used, self.where = n, 0, [0] * n, {}

    def take(self, key):
        place = self.at % self.n
        self.at += 1
        self.used[place] += 1
        self.where[key] = (place, self.used[place])
        return self.where[key]


def trunk(nc, x, positions, norm_mix, norm_ffn, w_in_ab, fgate_bias, w_out_ab, w_in_c, lower_bounds,
          gnorm_c, w_out_c, w_gate_ffn, w_up_ffn, w_down_ffn, router, w_gate_moe, w_up_moe,
          w_down_moe, norm_final, c_float, c_onehot, c_level, out):
    FG = FF // 256
    GE = FFE // 256

    stream = []
    split_slot, before_in_slot, in_slot = {}, {}, {}

    def cols(w, row, c0, n):
        return w[row:row + 256, c0:c0 + n].rearrange("(k p) n -> p k n", p=P)

    def enqueue(key, slot, parts):
        split_slot[key] = slot
        before_in_slot[key] = in_slot.get(slot)
        in_slot[slot] = key
        stream.append((key, parts))

    def plain_parts(w, half, c0):
        return [(1024 * m, 2, 512, 512, cols(w, 512 * half + 256 * m, c0, 512)) for m in range(2)]

    def gate_up_parts(wg, wu, half, g):
        return [(256 * m, 4, 256, 512, w[512 * half:512 * half + 512, 256 * g:256 * g + 256]
                 .rearrange("(k p) n -> p k n", p=P)) for m, w in enumerate((wg, wu))]

    def down_parts(w, g):
        return [(1024 * m, 1, 1024, 1024, w[256 * g + P * m:256 * g + P * m + P, :]
                 .rearrange("(k p) n -> p k n", p=P)) for m in range(2)]

    turn = [0]

    def enqueue_pair(name, c, w):
        for half in range(2):
            enqueue((name, c, half), turn[0] % SPLIT, plain_parts(w, half, 512 * c))
            turn[0] += 1

    w_ab, w_oab, w_c, w_oc = w_in_ab[0], w_out_ab[0], w_in_c[0], w_out_c[0]
    C_ORDER = (2, 3, 0, 1, 4, 5, 6, 7)
    for c in range(6):
        enqueue_pair("ab", c, w_ab)
    for c in range(2):
        enqueue_pair("oab", c, w_oab)
    sa, sb_, sd = (turn[0] % SPLIT, (turn[0] + 1) % SPLIT, (turn[0] + 2) % SPLIT)

    def enqueue_ff(kind, g):
        if kind == 2:
            enqueue(("ff", g, 2), sd, down_parts(w_down_ffn[0], g))
        else:
            enqueue(("ff", g, kind), (sa, sb_)[kind], gate_up_parts(w_gate_ffn[0], w_up_ffn[0], kind, g))

    enqueue_ff(0, 0)
    enqueue_ff(1, 0)
    for g in range(FG - 1):
        enqueue_ff(0, g + 1)
        enqueue_ff(1, g + 1)
        enqueue_ff(2, g)
    enqueue_pair("c", C_ORDER[0], w_c)
    enqueue_ff(2, FG - 1)
    for c in C_ORDER[1:]:
        enqueue_pair("c", c, w_c)
    for c in range(2):
        enqueue_pair("oc", c, w_oc)
    assert turn[0] % SPLIT == 0
    position = {key: n for n, (key, _) in enumerate(stream)}
    N0 = len(stream)
    PER_ITEM = 3 * GE
    assert PER_ITEM % RAW == 0
    ITEM_POS = 5

    work = Turns(WORK)

    with ExitStack() as ctx:
        def sb(name, shape, dt=F32):
            return ctx.enter_context(nc.sbuf_tensor(name, shape, dt))

        sems = {}

        def sem(name):
            if name not in sems:
                sems[name] = ctx.enter_context(nc.semaphore(name))
            return sems[name]

        consts = sb("consts", [P, C_END])
        level_mask = sb("level_mask", [P, len(LEVELS), P], mybir.dt.uint8)
        vec_rows = sb("vec_rows", [6 * KD, P])
        vec_cols = sb("vec_cols", [P, 6 * KD])
        wf = sb("wf", [P, KD, NHB])
        wr = sb("wr", [P, KD, NE])
        fbias = sb("fbias", [NHB, 1])
        gnorm = sb("gnorm", [P, P])
        gain_row = sb("gain_row", [P, D])
        small = sb("small", [P, 128])
        route = sb("route", [P, T, 64])
        rank_of = sb("rank_of", [P, T, 2 * NE + 1])
        combine = sb("combine", [P, T, 2 * NE + 1])
        slot_gate = sb("slot_gate", [P, 2])
        overflow = sb("overflow", [P, 2], I32)
        X = sb("X", [P, T, D])
        XN = sb("XN", [P, T, D])
        raw = sb("raw", [P, RAW, CHUNK_F])
        hi_lo = sb("hi_lo", [P, SPLIT, 2, CHUNK_F], F32R)
        xt = sb("xt", [P, 4096], F32R)
        hT = sb("hT", [P, 2, 2, 512], F32R)

        with ExitStack() as before:
            def sb1(name, shape, dt=F32):
                return before.enter_context(nc.sbuf_tensor(name, shape, dt))

            A = [sb1(f"A{i}", [P, 2048]) for i in range(5)]
            arena = sb1("arena", [P, 3072])
            hbuf = sb1("hbuf", [P, 2, T * 256])
        hi_lo_e = sb("hi_lo_e", [P, SPLIT, 2, CHUNK_F], F32R)
        sel = sb("sel", [P, T, P])
        selT = sb("selT", [P, 2, T * P])
        ye = sb("ye", [P, D])
        hexp = sb("hexp", [P, 2, 256])

        HTH, HTL = (xt[:, 2048 * m:2048 * m + 2048].rearrange("p (k q) -> p k q", k=KD) for m in range(2))
        XE = xt[:, :].rearrange("p (par m k q) -> p par m k q", par=2, m=2, k=KD)
        onehot = A[3][0:NHB, 0:2048].rearrange("p (h q) -> p h q", h=NHB)
        rope = arena[:, 0:6 * SEQ].rearrange("p (a q) -> p a q", a=6)
        fox = arena[0:NHB, 6 * SEQ:12 * SEQ].rearrange("p (a q) -> p a q", a=6)
        level_words = A[4][:, 0:len(LEVELS) * P].bitcast(I32).rearrange("p (n q) -> p n q", q=P)
        pos_i = A[4][:, 0:SEQ].bitcast(I32)

        psum = [ctx.enter_context(nc.psum_tensor(f"work{i}", [P, 512], F32)) for i in range(WORK)]
        acc = [ctx.enter_context(nc.psum_tensor(f"acc{i}", [P, 512], F32)) for i in range(4)]

        ident = consts[:, C_ID:C_ID + P]
        perm = consts[:, C_PERM:C_PERM + P]
        score_mask = {"a": consts[:, C_MA:C_MA + 3 * P], "b": consts[:, C_MB:C_MB + 3 * P]}
        gain = {"mix0": 0, "mix1": KD, "ffn0": 2 * KD, "ffn1": 3 * KD}
        NORMS = ["mix0", "ffn0", "mix1", "ffn1", "final"]

        SS, MS, RS = 0, 2, 4
        MX, SM, RI = 8, 40, 72
        LBC, OML = 104, 112

        QK = {"qa": A[0][:, 0:1024], "ka": A[0][:, 1024:2048], "qb": A[1][:, 0:1024], "kb": A[1][:, 1024:2048]}
        QK = {n: v.rearrange("p (j q) -> p j q", j=4) for n, v in QK.items()}
        V = A[2][:, :].rearrange("p (t n) -> p t n", t=T)
        SRING = 4
        S = [A[4][:, 384 * i:384 * i + 384] for i in range(SRING)]
        PT = [XN[:, 0, 0:384], XN[:, 0, 384:768], XN[:, 1, 0:384]]
        cosT, sinT = rope[:, 0, :], rope[:, 1, :]
        rtmp = hbuf[:, 0, :]

        def full(i):
            return sem(f"raw_full{i}")

        def bank_full(i):
            return sem(f"bank_full{i}")

        def bank_free(i):
            return sem(f"bank_free{i}")

        def evacuated(eng, key):
            b, use = work.where[key]
            eng.wait_ge(bank_free(b), use)

        def product(eng, key):
            b, use = work.where[key]
            eng.wait_ge(bank_full(b), use)
            return psum[b], b

        NLV = len(LEVELS) + 1

        def parts_of(key):
            return hi_lo[:, split_slot[key], 0, :], hi_lo[:, split_slot[key], 1, :]

        def split_high(act, key):
            n = position[key]
            act.wait_ge(full(n % RAW), 32 * (n // RAW + 1))
            if before_in_slot[key] is not None:
                act.wait_ge(*done_at[before_in_slot[key]])
            nc.scalar.activation(parts_of(key)[0], raw[:, n % RAW, :], ACT.Copy).then_inc(sem("split_hi"), 1)

        def split_low(dve, key):
            n = position[key]
            dve.wait_ge(sem("split_hi"), n + 1)
            nc.vector.tensor_tensor(parts_of(key)[1], raw[:, n % RAW, :], parts_of(key)[0].bitcast(F32),
                                    ALU.subtract).then_inc(sem("split_lo"), 1)

        item_keys = [("gu", 0)]
        for g in range(1, GE):
            item_keys += [("gu", g), ("ht", g - 1)]
            if g == GE // 2:
                item_keys += [("x", 0), ("x", 1), ("selT",), ("gate",)]
        item_keys += [("ht", GE - 1)] + [("y", n) for n in range(4)]
        assert len(item_keys) % BANKS_E == 0
        USES = len(item_keys) // BANKS_E
        item_at = {key: n for n, key in enumerate(item_keys)}
        ebank = psum + [acc[2], acc[3]]
        ybank = [acc[0], acc[1]]

        def e_full(key, i):
            n = item_at[key]
            return sem(f"expert_full{n % BANKS_E}"), i * USES + (n // BANKS_E + 1)

        def e_free(key, i):
            n = item_at[key]
            return sem(f"expert_free{n % BANKS_E}"), i * USES + (n // BANKS_E + 1)

        def e_read(key, i):
            n = item_at[key]
            return sem(f"expert_free{n % BANKS_E}"), i * USES + (n // BANKS_E + 2)

        def e_split(kind, g):
            slots = hi_lo if g % 2 == 0 else hi_lo_e
            return slots[:, kind, 0, :], slots[:, kind, 1, :]

        def item_splits(i, g, last):
            base = i * PER_ITEM + (ITEM_POS + 3 * g)
            if not last or g + 2 < GE:
                return [(0, g + 2, base), (1, g + 2, base + 1), (2, g + 1, base + 2)]
            return [(2, g + 1, base)] if g + 1 < GE else []

        def split_ready(i, kind, g, last):
            if g == 0 and kind < 2:
                return i * PER_ITEM + (N0 + 2)
            if g == 0:
                return i * PER_ITEM + (N0 + 5)
            if g == 1 and kind < 2:
                return i * PER_ITEM + (N0 + 3 + kind)
            if last and g == GE - 1 and kind == 2:
                return i * PER_ITEM + (N0 + ITEM_POS + 3 * (GE - 2) + 1)
            n = 3 * (g - 2) + kind if kind < 2 else 3 * (g - 1) + 2
            return i * PER_ITEM + (N0 + ITEM_POS + n + 1)

        PASS_START = [(0, 0, 0), (1, 0, 1), (0, 1, 2), (1, 1, 3), (2, 0, 4)]

        def passes(eng, items):
            items(0)
            eng.wait_ge(sem("overflow_ready"), 1)
            more = eng.value_load(overflow[0:1, 0:1], min_val=0, max_val=1)
            with eng.If(more > 0):
                items(1)

        def filled(b):
            return bank_full(b), work.used[b]

        done_at = {}
        moe = {}

        BC, KC, QC = (A[i][:, :].rearrange("p (h q) -> p h q", h=NHC) for i in range(3))
        VC = A[3][:, :].rearrange("p (t n) -> p t n", t=T)
        SG = A[4][:, :].rearrange("p (t n) -> p t n", t=T)
        LV = arena[:, 0:2048].rearrange("p (b h q) -> p b h q", b=2, h=4)
        DL = arena[:, 2048:3072].rearrange("p (h q) -> p h q", h=4)
        AT = hbuf[:, :, :].rearrange("p a (h t q) -> p (a h) t q", h=2, t=T)
        AX_ = XN[:, 1, 512:1024].rearrange("p (h q) -> p h q", h=4)

        def level_operands(half, n):
            if n == 0:
                return KC[:, 4 * half:4 * half + 4, :], QC[:, 4 * half:4 * half + 4, :]
            return LV[:, n % 2], LV[:, n % 2]

        block = ctx.enter_context(nc.Block())

        @block.tensor
        def _(pe):
            def claim(key):
                b, use = work.take(key)
                if use > 1:
                    pe.wait_ge(bank_free(b), use - 1)
                return psum[b], b

            def transposed(src, name, ready):
                pe.wait_ge(*ready)
                for j in range(KD // 2):
                    ps, b = claim((name, j))
                    for kk in range(2):
                        for t in range(T):
                            k = 2 * j + kk
                            last = nc.tensor.transpose(ps[:, 256 * kk + P * t:256 * kk + P * t + P],
                                                       src[:, t, P * k:P * k + P], ident)
                    last.then_inc(bank_full(b), 1)
                for j in range(KD // 2):
                    evacuated(pe, (name, j))

            def split(key):
                pe.wait_ge(sem("split_lo"), position[key] + 1)
                return parts_of(key)

            halves_used = [0]

            def half_used(last, key):
                halves_used[0] += 1
                last.then_inc(sem("half_used"), 1)
                done_at[key] = (sem("half_used"), halves_used[0])

            def three(out, stationary, moving, start, stop):
                (sh, sl), (mh, ml) = stationary, moving
                nc.tensor.matmul(out, sh, mh, start=start, stop=False, skip_group_check=True)
                nc.tensor.matmul(out, sh, ml, start=False, stop=False, skip_group_check=True)
                return nc.tensor.matmul(out, sl, mh, start=False, stop=stop, skip_group_check=True)

            def project_T(name, c, out_name):
                banks = [claim((out_name, j)) for j in range(4)]
                for half in range(2):
                    key = (name, c, half)
                    w = [v.rearrange("p (k n) -> p k n", k=4) for v in split(key)]
                    for j in range(4):
                        for k in range(4):
                            x_ = [v[:, 4 * half + k, :] for v in (HTH, HTL)]
                            last = three(banks[j][0][:, 0:SEQ], [v[:, k, P * j:P * j + P] for v in w], x_,
                                         half == k == 0, half == 1 and k == 3)
                        if half:
                            last.then_inc(bank_full(banks[j][1]), 1)
                    if not half:
                        half_used(last, key)
                done_at[key] = filled(banks[3][1])

            def token_product(key, half, outs, start_k, stop):
                w = [v.rearrange("p (k n) -> p k n", k=4) for v in split(key)]
                lasts = []
                for t in range(T):
                    for k in range(4):
                        x_ = [v[:, 4 * half + k, P * t:P * t + P] for v in (HTH, HTL)]
                        last = three(outs[t], x_, [v[:, k, :] for v in w], half == k == 0, half == 1 and k == 3)
                    yield last

            def project(name, c, out_name):
                banks = [claim((out_name, t)) for t in range(T)]
                for half in range(2):
                    key = (name, c, half)
                    for t, last in enumerate(token_product(key, half, [b[0][:, :] for b in banks], 0, 0)):
                        if half:
                            last.then_inc(bank_full(banks[t][1]), 1)
                    if not half:
                        half_used(last, key)
                done_at[key] = filled(banks[1][1])

            def out_project(name, frees, sums):
                if frees:
                    pe.wait_ge(sem("acc_free"), frees)
                for c in range(2):
                    for half in range(2):
                        key = (name, c, half)
                        for t, last in enumerate(token_product(key, half, [acc[2 * t + c][:, :] for t in range(T)], 0, 0)):
                            if half:
                                last.then_inc(sem("acc_full"), 1)
                        if not half:
                            half_used(last, key)
                    done_at[key] = (sem("acc_full"), sums + 2 * c + 2)

            pe.wait_ge(sem("consts_in"), 16)
            pe.wait_ge(sem("vecs_in"), 16 * 3)
            ps, b = claim("vecs")
            nc.tensor.transpose(ps[:, 0:6 * KD], vec_rows[:, :], consts[0:6 * KD, C_ID:C_ID + 6 * KD])\
                .then_inc(bank_full(b), 1)

            transposed(XN, "mix0", (sem("xn_ready"), 2))
            pe.wait_ge(sem("wf_in"), 16)
            ps, b = claim("flogit")
            for k in range(KD):
                for m, v in enumerate((HTH, HTL)):
                    last = nc.tensor.matmul(ps[0:NHB, 0:SEQ], wf[:, k, :], v[:, k, :].bitcast(F32),
                                            start=(k == m == 0), stop=(k == KD - 1 and m == 1))
            last.then_inc(bank_full(b), 1)
            project_T("ab", 0, "qa")
            project_T("ab", 1, "ka")
            project("ab", 2, "va")
            for n, name in enumerate(("qa", "ka")):
                for jj in range(2):
                    evacuated(pe, (name, 2 * jj))
                    evacuated(pe, (name, 2 * jj + 1))
                    ps, b = claim(("rot", name, jj))
                    nc.tensor.matmul(ps[:, :], perm, QK[name][:, 2 * jj:2 * jj + 2, :],
                                     start=True, stop=True).then_inc(bank_full(b), 1)
            project_T("ab", 3, "qb")
            project_T("ab", 4, "kb")
            project("ab", 5, "vb")

            def scores(h):
                kind, j, r = ("a" if h < NHA else "b"), (h % NHA) // 2, HD * (h % 2)
                q, k = QK["q" + kind][r:r + HD, j, :], QK["k" + kind][r:r + HD, j, :]
                if h == 0:
                    pe.wait_ge(sem("rope_ready"), 4)
                if h == NHA:
                    for n in ("qb", "kb"):
                        for jj in range(4):
                            evacuated(pe, (n, jj))
                    pe.wait_ge(sem("fox_ready"), 1)
                ps, b = claim(("s", h))
                for t in range(T):
                    o = ps[:, P * t:P * t + P * (t + 1)]
                    last = nc.tensor.matmul(o, q[:, P * t:P * t + P], k[:, 0:P * (t + 1)],
                                            start=True, stop=(kind == "a"))
                    if kind == "b":
                        e = onehot[:, h - NHA, :]
                        nc.tensor.matmul(o, fox[:, 0, P * t:P * t + P], e[:, 0:P * (t + 1)], start=False, stop=False)
                        last = nc.tensor.matmul(o, e[:, 0:P], fox[:, 1, 0:P * (t + 1)], start=False, stop=True)
                last.then_inc(bank_full(b), 1)

            def probs_T(h):
                pe.wait_ge(sem("probs_ready"), h + 1)
                ps, b = claim(("p", h))
                s = S[h % SRING]
                for n, blk in enumerate((s[:, 0:P], s[:, P:2 * P], s[:, 2 * P:3 * P])):
                    last = nc.tensor.transpose(ps[:, P * n:P * n + P], blk, ident)
                last.then_inc(bank_full(b), 1)

            def values(h):
                evacuated(pe, ("p", h))
                if h % NHA == 0:
                    for t in range(T):
                        evacuated(pe, ("va" if h < NHA else "vb", t))
                pair = h // 2
                if h % 2 == 0 and pair >= 4:
                    pe.wait_ge(sem("ot_ready"), pair - 3)
                o = acc[pair % 4][HD * (h % 2):HD * (h % 2) + HD, 0:SEQ]
                pt = PT[h % 3]
                nc.tensor.matmul(o, V[:, 0, HD * h:HD * h + HD], pt[:, 0:2 * P], start=True, stop=False)
                nc.tensor.matmul(o[:, P:2 * P], V[:, 1, HD * h:HD * h + HD], pt[:, 2 * P:3 * P],
                                 start=False, stop=True).then_inc(sem("values_done"), 1)

            for i in range(NH + 3):
                if i < NH:
                    scores(i)
                if 2 <= i < NH + 2:
                    probs_T(i - 2)
                if i >= 3:
                    values(i - 3)

            pe.wait_ge(sem("ot_ready"), NH // 2)
            out_project("oab", 0, 0)

            transposed(XN, "ffn0", (sem("xn_ready"), 4))
            pe.wait_ge(sem("acc_free"), 4)
            for g in range(FG + 1):
                if g < FG:
                    banks = [claim(("gu", g, t)) for t in range(T)]
                    for last in token_product(("ff", g, 0), 0, [b[0][:, :] for b in banks], 0, 0):
                        pass
                    half_used(last, ("ff", g, 0))
                if g > 0:
                    for t in range(T):
                        evacuated(pe, ("gu", g - 1, t))
                    ps, b = claim(("ht", g - 1))
                    for f in range(2):
                        for t in range(T):
                            last = nc.tensor.transpose(ps[:, 256 * f + P * t:256 * f + P * t + P],
                                                       hbuf[:, (g - 1) % 2, 256 * t + P * f:256 * t + P * f + P], ident)
                    last.then_inc(bank_full(b), 1)
                if g < FG:
                    for t, last in enumerate(token_product(("ff", g, 1), 1, [b[0][:, :] for b in banks], 0, 0)):
                        last.then_inc(bank_full(banks[t][1]), 1)
                    done_at[("ff", g, 1)] = filled(banks[1][1])
                if g > 0:
                    i = g - 1
                    w = [v.rearrange("p (f n) -> p f n", f=2) for v in split(("ff", i, 2))]
                    evacuated(pe, ("ht", i))
                    for f in range(2):
                        for t in range(T):
                            for c in range(2):
                                h_ = [hT[:, i % 2, m, 256 * f + P * t:256 * f + P * t + P] for m in range(2)]
                                last = three(acc[2 * t + c][:, :], h_, [v[:, f, 512 * c:512 * c + 512] for v in w],
                                             i == f == 0, i == FG - 1 and f == 1)
                    last.then_inc(sem("down_used"), 1)
                    done_at[("ff", i, 2)] = (sem("down_used"), i + 1)

            transposed(XN, "mix1", (sem("xn_ready"), 6))
            for c, name in ((2, "f0"), (3, "f1"), (0, "q0"), (1, "q1")):
                project_T("c", c, name)
            for c, name in ((4, "v0"), (5, "v1"), (6, "g0"), (7, "g1")):
                project("c", c, name)

            for half in range(2):
                for n in range(len(LEVELS) + 2):
                    if n == 0:
                        for jj in range(4):
                            evacuated(pe, (f"q{half}", jj))
                        pe.wait_ge(sem("kc_ready"), 1)
                    else:
                        pe.wait_ge(sem("level_ready"), half * NLV + n)
                    kk, qq = level_operands(half, n)
                    for g in range(1 if n == 1 else 2):
                        ps, b = claim(("lv", half, n, g))
                        for i in range(4):
                            if n == 1:
                                lhs, rhs = kk[:, i, 0:P], qq[:, i, P:2 * P]
                            else:
                                hh, t = 2 * g + i // 2, i % 2
                                lhs, rhs = kk[:, hh, P * t:P * t + P], qq[:, hh, P * t:P * t + P]
                            last = nc.tensor.matmul(ps[:, P * i:P * i + P], lhs, rhs, start=True, stop=True)
                        last.then_inc(bank_full(b), 1)
                    done_at[("level", half, n)] = filled(b)
                evacuated(pe, ("lv", half, 1, 0))
                for g in range(2):
                    evacuated(pe, ("lv", half, NLV, g))
                for t in range(T):
                    evacuated(pe, (f"v{half}", t))
                for t in range(T):
                    ps, b = claim(("hgrn_o", half, t))
                    for i in range(4):
                        o = ps[:, P * i:P * i + P]
                        h = 4 * half + i
                        if t == 0:
                            last = nc.tensor.matmul(o, AT[:, i, 0, :], VC[:, 0, P * h:P * h + P], start=True, stop=True)
                        else:
                            nc.tensor.matmul(o, AX_[:, i, :], VC[:, 0, P * h:P * h + P], start=True, stop=False)
                            last = nc.tensor.matmul(o, AT[:, i, 1, :], VC[:, 1, P * h:P * h + P], start=False, stop=True)
                    last.then_inc(bank_full(b), 1)
                done_at[("at", half)] = filled(b)
            transposed(XN, "hgrn_out", (sem("hgrn_ready"), 1))
            out_project("oc", 8, 4)

            transposed(XN, "ffn1", (sem("xg_ready"), 1))
            pe.wait_ge(sem("wr_in"), 16)
            ps, b = claim("router")
            for t in range(T):
                for k in range(KD):
                    for m, v in enumerate((HTH, HTL)):
                        last = nc.tensor.matmul(ps[:, NE * t:NE * t + NE], v[:, k, P * t:P * t + P].bitcast(F32), wr[:, k, :],
                                                start=(k == m == 0), stop=(k == KD - 1 and m == 1))
            last.then_inc(bank_full(b), 1)
            pe.wait_ge(sem("chosen_ready"), 1)
            ps, b = claim("rank")
            tri, ones = consts[:, C_TRI:C_TRI + P], consts[:, C_ONE:C_ONE + P]
            chosen = [route[:, t, 56:64] for t in range(T)]
            nc.tensor.matmul(ps[:, 0:NE], tri, chosen[0], start=True, stop=True)
            nc.tensor.matmul(ps[:, NE:2 * NE], tri, chosen[1], start=True, stop=False)
            nc.tensor.matmul(ps[:, NE:2 * NE], ones, chosen[0], start=False, stop=True)
            nc.tensor.matmul(ps[:, 2 * NE:3 * NE], ones, chosen[0], start=True, stop=False)
            nc.tensor.matmul(ps[:, 2 * NE:3 * NE], ones, chosen[1], start=False, stop=True).then_inc(bank_full(b), 1)

            def gather(nxt, banks):
                for h in range(2):
                    ps = banks(("x", h))
                    for k in range(4):
                        for t in range(T):
                            kk = P * (4 * h + k)
                            last = nc.tensor.matmul(ps[:, P * k:P * k + P], XN[:, t, kk:kk + P], sel[:, t, :],
                                                    start=(t == 0), stop=(t == T - 1))
                    yield ("x", h), last
                ps = banks(("selT",))
                for t in range(T):
                    last = nc.tensor.transpose(ps[:, P * t:P * t + P], sel[:, t, :], ident)
                yield ("selT",), last
                ps = banks(("gate",))
                for t in range(T):
                    last = nc.tensor.matmul(ps[:, 0:1], sel[:, t, :], combine[:, t, bass.ds(nxt, 1)],
                                            start=(t == 0), stop=(t == T - 1))
                yield ("gate",), last

            pe.wait_ge(sem("sel_ready"), 1)
            for key, last in gather(0, lambda key: claim(("first",) + key)[0]):
                last.then_inc(bank_full(work.where[("first",) + key][0]), 1)
            for key in (("x", 0), ("x", 1), ("selT",), ("gate",)):
                evacuated(pe, ("first",) + key)
            pe.wait_ge(sem("acc_free"), 12)

            def item(i, par, last_item):
                def claim_e(key):
                    pe.wait_ge(*e_free(key, i))
                    return ebank[item_at[key] % BANKS_E]

                def there(key, last):
                    last.then_inc(e_full(key, i)[0], 1)

                def ready(kind, g):
                    pe.wait_ge(sem("split_lo"), split_ready(i, kind, g, last_item))
                    return e_split(kind, g)

                def gate_up_half(ps, g, half):
                    w = [v.rearrange("p (k n) -> p k n", k=4) for v in ready(half, g)]
                    for k in range(4):
                        x_ = [XE[:, par, m, 4 * half + k, :] for m in range(2)]
                        last = three(ps[:, :], x_, [v[:, k, :] for v in w], half == k == 0, half == 1 and k == 3)
                    return last

                for g in range(GE + 1):
                    if g < GE:
                        ps_gu = claim_e(("gu", g))
                        gate_up_half(ps_gu, g, 0).then_inc(sem("expert_half_used"), 1)
                    if g > 0:
                        pe.wait_ge(*e_read(("gu", g - 1), i))
                        ps = claim_e(("ht", g - 1))
                        for f in range(2):
                            last = nc.tensor.transpose(ps[:, P * f:P * f + P], hexp[:, (g - 1) % 2, P * f:P * f + P], ident)
                        there(("ht", g - 1), last)
                    if g < GE:
                        there(("gu", g), gate_up_half(ps_gu, g, 1))
                    if g > 0:
                        w = [v.rearrange("p (f n) -> p f n", f=2) for v in ready(2, g - 1)]
                        pe.wait_ge(*e_read(("ht", g - 1), i))
                        for f in range(2):
                            for c in range(2):
                                h_ = [hT[:, (g - 1) % 2, m, P * f:P * f + P] for m in range(2)]
                                last = three(ybank[c][:, :], h_, [v[:, f, 512 * c:512 * c + 512] for v in w],
                                             g == 1 and f == 0, g == GE and f == 1)
                        last.then_inc(sem("expert_down_used"), 1)
                    if g == GE // 2:
                        pe.wait_ge(sem("sel_ready"), i + 2)
                        for key, last in gather(i + 1, claim_e):
                            there(key, last)
                pe.wait_ge(sem("ye_ready"), 2 * i + 2)
                for n in range(4):
                    t, c = divmod(n, 2)
                    ps = claim_e(("y", n))
                    there(("y", n), nc.tensor.matmul(ps[:, :], selT[:, par, P * t:P * t + P],
                                                     ye[:, 512 * c:512 * c + 512], start=True, stop=True))
                pe.wait_ge(*e_read(("gate",), i))
                for h in range(2):
                    pe.wait_ge(*e_read(("x", h), i))
                pe.wait_ge(*e_read(("selT",), i))

            def items(p):
                with pe.Fori(0, NE // 2 - 1) as m:
                    for u in range(2):
                        item(m * 2 + (NE * p + u), u, False)
                item(NE * p + NE - 2, 0, False)
                item(NE * p + NE - 1, 1, True)

            passes(pe, items)

        @block.sync
        def _(sp):
            sp.dma_start(X[:, :, :], x[0].rearrange("(t p) n -> p t n", p=P)).then_inc(sem("x_in"), 16)

            def load(n, parts):
                for off, blocks, width, stride, src in parts:
                    dst = raw[:, n % RAW, :].rearrange("p (k n) -> p k n", n=stride)
                    k0, c0 = divmod(off, stride)
                    sp.dma_start(dst[:, k0:k0 + blocks, c0:c0 + width], src).then_inc(full(n % RAW), 16)

            for n, (key, parts) in enumerate(stream):
                if n >= RAW:
                    sp.wait_ge(sem("split_lo"), n - RAW + 1)
                load(n, parts)

            def expert_parts(kind, e, g):
                if kind == 2:
                    return down_parts(w_down_moe[0][e], g)
                return gate_up_parts(w_gate_moe[0][e], w_up_moe[0][e], kind, g)

            def items(p):
                for kind, g, n in PASS_START:
                    sp.wait_ge(sem("split_lo"), p * NE * PER_ITEM + N0 + n - RAW + 1)
                    load(N0 + n, expert_parts(kind, 0, g))

                def item(i, e, last):
                    for g in range(GE):
                        for kind, gg, n in item_splits(i, g, last):
                            sp.wait_ge(sem("split_lo"), n + (N0 - RAW + 1))
                            off = item_splits(0, g, last)
                            place = N0 + [q for k_, g_, q in off if (k_, g_) == (kind, gg)][0]
                            load(place, expert_parts(kind, e + gg // GE, gg % GE))

                with sp.Fori(0, NE // 2 - 1) as m:
                    for u in range(2):
                        item(m * 2 + (NE * p + u), m * 2 + u, False)
                item(NE * p + NE - 2, NE - 2, False)
                item(NE * p + NE - 1, NE - 1, True)

            passes(sp, items)

            for t in range(T):
                sp.wait_ge(sem("out_ready"), t + 1)
                sp.dma_start(out[0, P * t:P * t + P, :], XN[:, t, :]).then_inc(sem("out_done"), 16)
            sp.wait_ge(sem("out_done"), 16 * T)

        @block.gpsimd
        def _(pool):
            for b in range(BANKS_E):
                pool.sem_inc(sem(f"expert_free{b}"), 1)
            pool.wait_ge(sem("gnorm_in"), 16)
            for c in range(2):
                for t in range(T):
                    evacuated(pool, (f"g{c}", t))
                    sgv = SG[:, t, 512 * c:512 * c + 512].rearrange("p (h n) -> p h n", h=4)
                    nc.gpsimd.tensor_tensor(sgv, sgv, gnorm[:, :].unsqueeze(1).to_broadcast([P, 4, P]),
                                            ALU.mult).then_inc(sem("gate_ready"), 1)

        @block.scalar
        def _(act):
            act.dma_start(consts[:, :], c_float).then_inc(sem("consts_in"), 16)
            act.dma_start(vec_rows[0:2 * KD, :], norm_mix.rearrange("l (k p) -> (l k) p", p=P)).then_inc(sem("vecs_in"), 16)
            act.dma_start(vec_rows[2 * KD:4 * KD, :], norm_ffn.rearrange("l (k p) -> (l k) p", p=P)).then_inc(sem("vecs_in"), 16)
            act.dma_start(vec_rows[4 * KD:6 * KD, :], lower_bounds.rearrange("l (k p) -> (l k) p", p=P)).then_inc(sem("vecs_in"), 16)
            act.dma_start(wf[:, :, :], w_ab[:, 3072:3072 + NHB].rearrange("(k p) n -> p k n", p=P)).then_inc(sem("wf_in"), 16)
            act.dma_start(pos_i[:, :], positions[0:1, :].partition_broadcast(P)).then_inc(sem("pos_in"), 16)
            act.dma_start(fbias[:, :], fgate_bias[0:1, :].rearrange("a h -> h a")).then_inc(sem("fox_in"), 16)
            act.dma_start(onehot, c_onehot).then_inc(sem("onehot_in"), 16)
            act.dma_start(wr[:, :, :], router[0].rearrange("(k p) n -> p k n", p=P)).then_inc(sem("wr_in"), 16)
            act.dma_start(gnorm[:, :], gnorm_c[0:1, :].partition_broadcast(P)).then_inc(sem("gnorm_in"), 16)
            act.dma_start(gain_row[:, :], norm_ffn[1:2, :].partition_broadcast(P)).then_inc(sem("gain_row_in"), 16)

            def norm(n, x_ready):
                act.wait_ge(*x_ready)
                for t in range(T):
                    nc.scalar.activation(XN[:, t, :], X[:, t, :], ACT.Square,
                                         accum_out=small[:, SS + t:SS + t + 1]).then_inc(sem("squares"), 1)
                act.wait_ge(sem("ms_ready"), n + 1)
                nc.scalar.activation(small[:, MS:MS + 2], small[:, MS:MS + 2], ACT.Sqrt).then_inc(sem("rms_ready"), 1)
                act.wait_ge(sem("rs_ready"), n + 1)
                nc.scalar.activation(XN[:, 1, :], X[:, 1, :], ACT.Copy, scale=small[:, RS + 1:RS + 2])\
                    .then_inc(sem("xn_ready"), 1)

            def evacuate_T(name, g):
                for j in range(KD // 2):
                    ps, b = product(act, (name, j))
                    if g is None:
                        nc.scalar.activation(HTH[:, 2 * j:2 * j + 2, :], ps[:, :].rearrange("p (u q) -> p u q", u=2),
                                             ACT.Copy).then_inc(sem("xt_high"), 1)
                    else:
                        for kk in range(2):
                            k = 2 * j + kk
                            last = nc.scalar.activation(HTH[:, k, :], ps[:, 256 * kk:256 * kk + 256], ACT.Copy,
                                                        scale=vec_cols[:, g + k:g + k + 1])
                        last.then_inc(sem("xt_high"), 1)

            def high(*key):
                split_high(act, key)

            high("ab", 0, 0)
            high("ab", 0, 1)
            high("ab", 1, 0)
            norm(0, (sem("x_in"), 16))
            evacuated(act, "vecs")
            evacuate_T("mix0", gain["mix0"])

            def copy_T(name, dst, scale, func=ACT.Copy):
                for j in range(4):
                    ps, b = product(act, (name, j))
                    nc.scalar.activation(dst[:, j, :], ps[:, 0:SEQ], func, scale=scale).then_inc(bank_free(b), 1)

            high("ab", 1, 1)
            copy_T("qa", QK["qa"], HD ** -0.5)
            high("ab", 2, 0)
            high("ab", 2, 1)
            copy_T("ka", QK["ka"], 1.0)
            high("ab", 3, 0)
            act.wait_ge(sem("angle_ready"), 1)
            nc.scalar.activation(rope[:, 0:2, :], rope[:, 2:4, :], ACT.Sin).then_inc(sem("trig_ready"), 1)
            act.wait_ge(sem("fox_abs"), 1)
            nc.scalar.activation(fox[:, 3, :], fox[:, 3, :], ACT.Exp, scale=-1.0).then_inc(sem("fox_exp"), 1)
            act.wait_ge(sem("fox_exp"), 1)
            nc.scalar.activation(fox[:, 3, :], fox[:, 3, :], ACT.Ln, bias=1.0).then_inc(sem("fox_ln"), 1)
            high("ab", 3, 1)
            high("ab", 4, 0)
            high("ab", 4, 1)
            copy_T("qb", QK["qb"], HD ** -0.5)
            high("ab", 5, 0)
            high("ab", 5, 1)
            copy_T("kb", QK["kb"], 1.0)
            high("oab", 0, 0)
            high("oab", 0, 1)
            high("oab", 1, 0)

            def head_pair_out(pair):
                act.wait_ge(sem("values_done"), 2 * pair + 2)
                nc.scalar.activation(HTH[:, pair, :], acc[pair % 4][:, 0:SEQ], ACT.Copy).then_inc(sem("out_high"), 1)

            for i in range(NH + 5):
                if i < NH:
                    h = i
                    act.wait_ge(sem("max_ready"), h + 1)
                    for t in range(T):
                        s_ = S[h % SRING][:, P * t:P * t + P * (t + 1)]
                        nc.scalar.activation(s_, s_, ACT.Exp, bias=small[:, MX + 2 * h + t:MX + 2 * h + t + 1],
                                             accum_out=small[:, SM + 2 * h + t:SM + 2 * h + t + 1])\
                            .then_inc(sem("exp_ready"), 1)
                if 2 <= i < NH + 2:
                    h = i - 2
                    if h >= 3:
                        act.wait_ge(sem("values_done"), h - 2)
                    ps, b = product(act, ("p", h))
                    nc.scalar.activation(PT[h % 3], ps[:, 0:3 * P], ACT.Copy).then_inc(bank_free(b), 1)
                if i >= 5 and i % 2 == 1:
                    head_pair_out((i - 5) // 2)

            act.dma_start(level_words, c_level).then_inc(sem("level_in"), 16)
            high("oab", 1, 1)
            high("ff", 0, 0)
            high("ff", 0, 1)
            norm(1, (sem("acc_free"), 4))
            evacuate_T("ffn0", gain["ffn0"])
            for g in range(FG + 1):
                if g > 0:
                    ps, b = product(act, ("ht", g - 1))
                    nc.scalar.activation(hT[:, (g - 1) % 2, 0, :], ps[:, :], ACT.Copy).then_inc(sem("hT_high"), 1)
                if g < FG - 1:
                    high("ff", g + 1, 0)
                elif g == FG - 1:
                    high("c", C_ORDER[0], 0)
                if g < FG:
                    for t in range(T):
                        ps, b = product(act, ("gu", g, t))
                        nc.scalar.activation(hbuf[:, g % 2, 256 * t:256 * t + 256], ps[:, 0:256], ACT.Silu)\
                            .then_inc(sem("silu_ready"), 1)
                    if g < FG - 1:
                        high("ff", g + 1, 1)
                    else:
                        high("c", C_ORDER[0], 1)
                    high("ff", g, 2)

            high("c", C_ORDER[1], 0)
            norm(2, (sem("acc_free"), 8))
            act.wait_ge(sem("lb_max"), 1)
            nc.scalar.activation(small[:, LBC:LBC + 16], small[:, LBC:LBC + 16], ACT.Exp).then_inc(sem("lb_exp"), 1)
            evacuate_T("mix1", gain["mix1"])
            high("c", C_ORDER[1], 1)
            copy_T("f0", BC[:, 0:4, :], 1.0, ACT.Sigmoid)
            high("c", C_ORDER[2], 0)
            high("c", C_ORDER[2], 1)
            copy_T("f1", BC[:, 4:8, :], 1.0, ACT.Sigmoid)
            high("c", C_ORDER[3], 0)
            high("c", C_ORDER[3], 1)
            copy_T("q0", QC[:, 0:4, :], P ** -0.5)
            high("c", C_ORDER[4], 0)
            act.wait_ge(sem("f_ready"), 1)
            nc.scalar.activation(BC[:, :, :], BC[:, :, :], ACT.Ln).then_inc(sem("logf_ready"), 1)
            high("c", C_ORDER[4], 1)
            copy_T("q1", QC[:, 4:8, :], P ** -0.5)
            high("c", C_ORDER[5], 0)
            high("c", C_ORDER[5], 1)
            high("c", C_ORDER[6], 0)
            high("c", C_ORDER[6], 1)
            high("c", C_ORDER[7], 0)
            high("c", C_ORDER[7], 1)
            for c in range(2):
                for t in range(T):
                    ps, b = product(act, (f"g{c}", t))
                    nc.scalar.activation(SG[:, t, 512 * c:512 * c + 512], ps[:, :], ACT.Silu).then_inc(bank_free(b), 1)
                if c == 0:
                    high("oc", 0, 0)
                    high("oc", 0, 1)
            high("oc", 1, 0)
            for half in range(2):
                for n in range(1, NLV + 1):
                    act.wait_ge(sem("delta_ready"), half * NLV + n)
                    if n >= 3:
                        act.wait_ge(*done_at[("level", half, n - 2)])
                    elif half == 1:
                        act.wait_ge(*done_at[("level", 0, NLV - (1 if (NLV - n) % 2 else 0))])
                    for r in range(2):
                        width = P if n == 1 else LEVELS[n - 2]
                        dst, src = (v.rearrange("p h (m side z) -> p (h m) side z", side=2, z=width)[:, :, r, :]
                                    for v in (LV[:, n % 2], DL))
                        last = nc.scalar.activation(dst, src, ACT.Exp, scale=(-1.0, 1.0)[r])
                    last.then_inc(sem("decay_ready"), 1)
                for t in range(T):
                    ps, b = product(act, ("hgrn_o", half, t))
                    nc.scalar.activation(XN[:, t, 512 * half:512 * half + 512], ps[:, :], ACT.Copy).then_inc(bank_free(b), 1)
            act.wait_ge(sem("head_ms"), 1)
            nc.scalar.activation(small[:, MX:MX + 16], small[:, MX:MX + 16], ACT.Sqrt).then_inc(sem("head_rms"), 1)
            evacuate_T("hgrn_out", None)

            high("oc", 1, 1)

            def high_e(kind, g, slot, value, arrived, free_wait):
                act.wait_ge(full(slot), arrived)
                act.wait_ge(*free_wait)
                nc.scalar.activation(e_split(kind, g)[0], raw[:, slot, :], ACT.Copy).then_inc(sem("split_hi"), 1)

            def raw_place(n0, i):
                n = N0 + n0
                return n % RAW, i * (32 * PER_ITEM // RAW) + 32 * (n // RAW + 1)

            def pass_start(p, which):
                for kind, g, n in which:
                    slot, arrived = raw_place(n, NE * p)
                    if p == 0 and g == 0:
                        wait = done_at[("oc", (kind + 1) // 2, (kind + 1) % 2)]
                    elif p == 0:
                        wait = (sem("acc_full"), 8)
                    elif kind == 0:
                        wait = (sem("expert_half_used"), GE * NE * p + g - 1)
                    elif kind == 1:
                        wait = e_full(("gu", GE - 2 + g), NE * p - 1)
                    else:
                        wait = (sem("expert_down_used"), GE * NE * p + g - 1)
                    high_e(kind, g, slot, None, arrived, wait)

            norm(3, (sem("acc_free"), 12))
            pass_start(0, PASS_START[0:2])
            evacuate_T("ffn1", None)
            act.wait_ge(sem("top_gap"), 1)
            nc.scalar.activation(route[:, :, 32:33], route[:, :, 32:33], ACT.Exp).then_inc(sem("gap_exp"), 1)

            def place_x(par, wait):
                for h in range(2):
                    ps = wait(("x", h))
                    nc.scalar.activation(XE[:, par, 0, 4 * h:4 * h + 4, :], ps[:, :].rearrange("p (k q) -> p k q", k=4),
                                         ACT.Copy).then_inc(sem("xe_high"), 1)
                ps = wait(("selT",))
                return nc.scalar.activation(selT[:, par, :], ps[:, 0:T * P], ACT.Copy)

            b = work.where[("first", "selT")][0]
            place_x(0, lambda key: product(act, ("first",) + key)[0]).then_inc(bank_free(b), 1)
            pass_start(0, PASS_START[2:])

            def item(i, par, last):
                def there(key):
                    act.wait_ge(*e_full(key, i))
                    return ebank[item_at[key] % BANKS_E]

                def split_step(g, which):
                    for (kind, gg, n), (_, _, n0) in zip(item_splits(i, g, last), item_splits(0, g, last)):
                        if kind not in which:
                            continue
                        slot, arrived = raw_place(n0, i)
                        if kind == 0:
                            wait = (sem("expert_half_used"), i * GE + (gg - 2 + 1))
                        elif kind == 1:
                            wait = e_full(("gu", gg - 2), i)
                        elif gg >= 2:
                            wait = (sem("expert_down_used"), i * GE + (gg - 2 + 1))
                        else:
                            wait = (sem("expert_half_used"), i * GE + 1)
                        high_e(kind, gg, slot, None, arrived, wait)

                for g in range(GE + 1):
                    if g > 0:
                        nc_ = there(("ht", g - 1))
                        nc.scalar.activation(hT[:, (g - 1) % 2, 0, 0:256], nc_[:, 0:256], ACT.Copy)\
                            .then_inc(sem("hT_high"), 1)
                    if g == GE // 2 + 1:
                        place_x(1 - par, there).then_inc(e_read(("selT",), i)[0], 1)
                    if g < GE:
                        split_step(g, (0,))
                        ps = there(("gu", g))
                        nc.scalar.activation(hexp[:, g % 2, :], ps[:, 0:256], ACT.Silu).then_inc(sem("silu_ready"), 1)
                        split_step(g, (1, 2))
                act.wait_ge(sem("expert_down_used"), i * GE + GE)
                for c in range(2):
                    nc.scalar.activation(ye[:, 512 * c:512 * c + 512], ybank[c][:, :], ACT.Copy,
                                         scale=slot_gate[:, par:par + 1]).then_inc(sem("ye_ready"), 1)

            def items(p):
                if p:
                    pass_start(p, PASS_START)
                with act.Fori(0, NE // 2 - 1) as m:
                    for u in range(2):
                        item(m * 2 + (NE * p + u), u, False)
                item(NE * p + NE - 2, 0, False)
                item(NE * p + NE - 1, 1, True)

            passes(act, items)
            act.dma_start(gain_row[:, :], norm_final.rearrange("(a n) -> a n", a=1).partition_broadcast(P)).then_inc(sem("final_in"), 16)
            norm(4, (sem("x_final"), 1))


        @block.vector
        def _(dve):
            count = [0]

            def link(ins):
                count[0] += 1
                ins.then_inc(sem("dve_chain"), 1)
                dve.wait_ge(sem("dve_chain"), count[0])

            def norm(n):
                dve.wait_ge(sem("squares"), 2 * n + 2)
                nc.vector.tensor_scalar(small[:, MS:MS + 2], small[:, SS:SS + 2], 1.0 / D, EPS, ALU.mult, ALU.add)\
                    .then_inc(sem("ms_ready"), 1)
                dve.wait_ge(sem("rms_ready"), n + 1)
                nc.vector.reciprocal(small[:, RS:RS + 2], small[:, MS:MS + 2]).then_inc(sem("rs_ready"), 1)
                dve.wait_ge(sem("rs_ready"), n + 1)
                nc.vector.tensor_scalar(XN[:, 0, :], X[:, 0, :], small[:, RS:RS + 1], None, ALU.mult)\
                    .then_inc(sem("xn_ready"), 1)

            highs = [0]

            def evacuate_T(name, g):
                for j in range(KD // 2):
                    b, _ = work.where[(name, j)]
                    ps = psum[b]
                    highs[0] += 1
                    dve.wait_ge(sem("xt_high"), highs[0])
                    if g is None:
                        last = nc.vector.tensor_tensor(HTL[:, 2 * j:2 * j + 2, :], ps[:, :].rearrange("p (u q) -> p u q", u=2),
                                                       HTH[:, 2 * j:2 * j + 2, :].bitcast(F32), ALU.subtract)
                    else:
                        for kk in range(2):
                            k = 2 * j + kk
                            last = nc.vector.scalar_tensor_tensor(HTL[:, k, :], ps[:, 256 * kk:256 * kk + 256],
                                                                  vec_cols[:, g + k:g + k + 1], HTH[:, k, :].bitcast(F32),
                                                                  ALU.mult, ALU.subtract)
                    last.then_inc(bank_free(b), 1)

            def low(*key):
                split_low(dve, key)

            def residual(wait, already):
                for n in range(4):
                    c, t = divmod(n, 2)
                    dve.wait_ge(wait[0], wait[1] + (n + 1 if already is None else 0))
                    xs = X[:, t, 512 * c:512 * c + 512]
                    nc.vector.tensor_tensor(xs, xs, acc[2 * t + c][:, :], ALU.add).then_inc(sem("acc_free"), 1)

            two_pi = 2.0 * np.pi
            C1 = 6.28125
            C2 = float(np.float32(two_pi - C1))
            C3 = float(two_pi - C1 - C2)
            ROUND = 12582912.0
            PI_IN = float(np.nextafter(np.float32(np.pi), np.float32(0)))
            dve.wait_ge(sem("pos_in"), 16)
            dve.wait_ge(sem("consts_in"), 16)
            link(nc.vector.tensor_copy(rope[:, 4, :], pos_i[:, :]))
            link(nc.vector.tensor_scalar(rope[:, 4, :], rope[:, 4, :], consts[:, C_FREQ:C_FREQ + 1], None, ALU.mult))
            link(nc.vector.tensor_scalar(rope[:, 5, :], rope[:, 4, :], 1.0 / two_pi, ROUND, ALU.mult, ALU.add))
            link(nc.vector.tensor_scalar(rope[:, 5, :], rope[:, 5, :], ROUND, None, ALU.subtract))
            for part in (C1, C2, C3):
                link(nc.vector.scalar_tensor_tensor(rope[:, 4, :], rope[:, 5, :], -part, rope[:, 4, :], ALU.mult, ALU.add))
            link(nc.vector.tensor_scalar(rope[:, 3, :], rope[:, 4, :], PI_IN, -PI_IN, ALU.min, ALU.max))
            link(nc.vector.tensor_scalar(rope[:, 2, :], rope[:, 4, :], np.pi / 2, None, ALU.add))
            link(nc.vector.tensor_scalar(rope[:, 5, :], rope[:, 2, :], np.pi, -two_pi, ALU.is_gt, ALU.mult))
            link(nc.vector.tensor_tensor(rope[:, 2, :], rope[:, 2, :], rope[:, 5, :], ALU.add))
            nc.vector.tensor_scalar(rope[:, 2, :], rope[:, 2, :], PI_IN, -PI_IN, ALU.min, ALU.max)\
                .then_inc(sem("angle_ready"), 1)

            low("ab", 0, 0)
            low("ab", 0, 1)
            ps, b = product(dve, "vecs")
            nc.vector.tensor_copy(vec_cols[:, :], ps[:, 0:6 * KD]).then_inc(bank_free(b), 1)
            evacuated(dve, "vecs")
            norm(0)
            low("ab", 1, 0)
            evacuate_T("mix0", gain["mix0"])

            dve.wait_ge(sem("fox_in"), 16)
            dve.wait_ge(sem("onehot_in"), 16)
            ps, b = product(dve, "flogit")
            nc.vector.tensor_scalar(fox[:, 2, :], ps[0:NHB, 0:SEQ], fbias[:, 0:1], None, ALU.add).then_inc(bank_free(b), 1)
            evacuated(dve, "flogit")
            nc.vector.scalar_tensor_tensor(fox[:, 3, :], fox[:, 2, :], -1.0, fox[:, 2, :], ALU.mult, ALU.max)\
                .then_inc(sem("fox_abs"), 1)
            link(nc.vector.tensor_scalar(fox[:, 2, :], fox[:, 2, :], 0.0, None, ALU.min))
            link(nc.vector.memset(fox[:, 4, :], 1.0))

            def rotate(name, n):
                for jj in range(2):
                    ps, b = product(dve, ("rot", name, jj))
                    raw = QK[name][:, 2 * jj:2 * jj + 2, :]
                    rt = rtmp[:, 0:512].rearrange("p (u q) -> p u q", u=2)
                    if n == jj == 0:
                        dve.wait_ge(sem("trig_ready"), 1)
                    link(nc.vector.tensor_tensor(raw, raw, cosT.unsqueeze(1).to_broadcast([P, 2, SEQ]), ALU.mult))
                    nc.vector.tensor_tensor(rt, ps[:, :].rearrange("p (u q) -> p u q", u=2),
                                            sinT.unsqueeze(1).to_broadcast([P, 2, SEQ]), ALU.mult).then_inc(bank_free(b), 1)
                    evacuated(dve, ("rot", name, jj))
                    nc.vector.tensor_tensor(raw, raw, rt, ALU.add).then_inc(sem("rope_ready"), 1)
                    dve.wait_ge(sem("rope_ready"), 2 * n + jj + 1)

            def copy_tokens(name, dst, c0):
                for t in range(T):
                    ps, b = product(dve, (name, t))
                    nc.vector.tensor_copy(dst[:, t, c0:c0 + 512], ps[:, :]).then_inc(bank_free(b), 1)

            low("ab", 1, 1)
            low("ab", 2, 0)
            low("ab", 2, 1)
            low("ab", 3, 0)
            copy_tokens("va", V, 0)
            rotate("qa", 0)
            rotate("ka", 1)
            low("ab", 3, 1)
            low("ab", 4, 0)
            low("ab", 4, 1)
            dve.wait_ge(sem("fox_ln"), 1)
            link(nc.vector.tensor_tensor(fox[:, 2, :], fox[:, 2, :], fox[:, 3, :], ALU.subtract))
            link(nc.vector.tensor_tensor_scan(fox[:, 0, :], fox[:, 4, :], fox[:, 2, :], 0.0, ALU.mult, ALU.add))
            nc.vector.tensor_scalar(fox[:, 1, :], fox[:, 0, :], -1.0, None, ALU.mult).then_inc(sem("fox_ready"), 1)
            low("ab", 5, 0)
            low("ab", 5, 1)
            low("oab", 0, 0)
            low("oab", 0, 1)
            copy_tokens("vb", V, 512)
            low("oab", 1, 0)

            for i in range(NH + 5):
                if i < NH:
                    h = i
                    if h >= SRING:
                        dve.wait_ge(bank_full(work.where[("p", h - SRING)][0]), work.where[("p", h - SRING)][1])
                    ps, b = product(dve, ("s", h))
                    m = score_mask["a" if h < NHA else "b"]
                    for t in range(T):
                        at = slice(P * t, P * t + P * (t + 1))
                        last = nc.vector.tensor_tensor_reduce(
                            out=S[h % SRING][:, at], in0=ps[:, at], in1=m[:, at], scale=1.0, scalar=-3.0e38,
                            op0=ALU.add, op1=ALU.max, accum_out=small[:, MX + 2 * h + t:MX + 2 * h + t + 1])
                    last.then_inc(bank_free(b), 1)
                    evacuated(dve, ("s", h))
                    nc.vector.tensor_scalar(small[:, MX + 2 * h:MX + 2 * h + 2], small[:, MX + 2 * h:MX + 2 * h + 2],
                                            -1.0, None, ALU.mult).then_inc(sem("max_ready"), 1)
                if 1 <= i <= NH:
                    h = i - 1
                    dve.wait_ge(sem("exp_ready"), 2 * h + 2)
                    link(nc.vector.reciprocal(small[:, RI + 2 * h:RI + 2 * h + 2], small[:, SM + 2 * h:SM + 2 * h + 2]))
                    for t in range(T):
                        s_ = S[h % SRING][:, P * t:P * t + P * (t + 1)]
                        last = nc.vector.tensor_scalar(s_, s_, small[:, RI + 2 * h + t:RI + 2 * h + t + 1], None, ALU.mult)
                    last.then_inc(sem("probs_ready"), 1)
                if i >= 4 and (i - 4) % 2 == 1:
                    pair = (i - 4) // 2
                    dve.wait_ge(sem("out_high"), pair + 1)
                    nc.vector.tensor_tensor(HTL[:, pair, :], acc[pair % 4][:, 0:SEQ], HTH[:, pair, :].bitcast(F32),
                                            ALU.subtract).then_inc(sem("ot_ready"), 1)

            low("oab", 1, 1)
            low("ff", 0, 0)
            dve.wait_ge(sem("level_in"), 16)
            nc.vector.tensor_copy(level_mask[:, :, :], level_words).then_inc(sem("level_masks"), 1)
            residual((sem("acc_full"), 0), None)
            low("ff", 0, 1)
            norm(1)
            evacuate_T("ffn0", gain["ffn0"])
            for g in range(FG + 1):
                if g > 0:
                    b, _ = work.where[("ht", g - 1)]
                    dve.wait_ge(sem("hT_high"), g)
                    nc.vector.tensor_tensor(hT[:, (g - 1) % 2, 1, :], psum[b][:, :],
                                            hT[:, (g - 1) % 2, 0, :].bitcast(F32), ALU.subtract).then_inc(bank_free(b), 1)
                if g < FG - 1:
                    low("ff", g + 1, 0)
                elif g == FG - 1:
                    low("c", C_ORDER[0], 0)
                if g < FG:
                    for t in range(T):
                        b, _ = work.where[("gu", g, t)]
                        dve.wait_ge(sem("silu_ready"), 2 * g + t + 1)
                        ht_ = hbuf[:, g % 2, 256 * t:256 * t + 256]
                        nc.vector.tensor_tensor(ht_, ht_, psum[b][:, 256:512], ALU.mult).then_inc(bank_free(b), 1)
                    if g < FG - 1:
                        low("ff", g + 1, 1)
                    else:
                        low("c", C_ORDER[0], 1)
                    low("ff", g, 2)
            residual((sem("down_used"), FG), 0)
            low("c", C_ORDER[1], 0)

            l0, l1 = vec_cols[:, 4 * KD:5 * KD], vec_cols[:, 5 * KD:6 * KD]
            lb, oml = small[:, LBC:LBC + 8], small[:, OML:OML + 8]
            link(nc.vector.tensor_tensor(small[:, 120:128], l0, l1, ALU.max))
            link(nc.vector.tensor_tensor(lb, l1, small[:, 120:128], ALU.subtract))
            nc.vector.tensor_tensor(oml, l0, small[:, 120:128], ALU.subtract).then_inc(sem("lb_max"), 1)
            norm(2)
            dve.wait_ge(sem("lb_exp"), 1)
            link(nc.vector.tensor_tensor(oml, oml, lb, ALU.add))
            link(nc.vector.reciprocal(oml, oml))
            link(nc.vector.tensor_tensor(lb, lb, oml, ALU.mult))
            link(nc.vector.tensor_scalar(oml, lb, -1.0, 1.0, ALU.mult, ALU.add))
            evacuate_T("mix1", gain["mix1"])
            low("c", C_ORDER[1], 1)
            low("c", C_ORDER[2], 0)
            low("c", C_ORDER[2], 1)
            low("c", C_ORDER[3], 0)
            for c in range(2):
                for jj in range(4):
                    evacuated(dve, (f"f{c}", jj))
            for h in range(NHC):
                last = nc.vector.tensor_scalar(BC[:, h, :], BC[:, h, :], oml[:, h:h + 1], lb[:, h:h + 1], ALU.mult, ALU.add)
            link(last)
            nc.vector.tensor_scalar(KC[:, :, :], BC[:, :, :], -1.0, 1.0, ALU.mult, ALU.add).then_inc(sem("kc_ready"), 1)
            dve.wait_ge(sem("kc_ready"), 1)
            nc.vector.tensor_scalar(BC[:, :, :], BC[:, :, :], 2.0 ** -63, None, ALU.max).then_inc(sem("f_ready"), 1)
            low("c", C_ORDER[3], 1)
            low("c", C_ORDER[4], 0)
            low("c", C_ORDER[4], 1)
            low("c", C_ORDER[5], 0)
            low("c", C_ORDER[5], 1)
            low("c", C_ORDER[6], 0)
            copy_tokens("v0", VC, 0)
            low("c", C_ORDER[6], 1)
            low("c", C_ORDER[7], 0)
            copy_tokens("v1", VC, 512)
            low("c", C_ORDER[7], 1)
            low("oc", 0, 0)
            low("oc", 0, 1)
            low("oc", 1, 0)
            dve.wait_ge(sem("logf_ready"), 1)
            for h in range(NHC):
                last = nc.vector.tensor_tensor_scan(BC[:, h, :], consts[:, C_RST:C_RST + SEQ], BC[:, h, :], 0.0,
                                                    ALU.mult, ALU.add)
            link(last)

            def delta(half, n):
                bh = BC[:, 4 * half:4 * half + 4, :]
                if n == 1:
                    ends = [bh[:, :, CHUNK * c + CHUNK - 1:CHUNK * c + CHUNK] for c in range(4)]
                    wide = [P, 4, CHUNK]
                    d = [DL[:, :, CHUNK * c:CHUNK * c + CHUNK] for c in range(4)]
                    s4 = [bh[:, :, CHUNK * c:CHUNK * c + CHUNK] for c in range(4)]
                    nc.vector.tensor_tensor(d[1], s4[1], ends[1].to_broadcast(wide), ALU.subtract)
                    link(nc.vector.tensor_tensor(d[0], s4[0], ends[0].to_broadcast(wide), ALU.subtract))
                    nc.vector.tensor_tensor(d[0], d[0], ends[1].to_broadcast(wide), ALU.subtract)
                    nc.vector.tensor_copy(d[2], s4[2])
                    last = nc.vector.tensor_tensor(d[3], s4[3], ends[2].to_broadcast(wide), ALU.add)
                elif LEVELS[n - 2] == CHUNK:
                    v, dv = (u.rearrange("p h (m side z) -> p (h m) side z", side=2, z=CHUNK) for u in (bh, DL))
                    nc.vector.tensor_tensor(dv[:, :, 0, :], v[:, :, 0, :],
                                            v[:, :, 0, CHUNK - 1:CHUNK].to_broadcast([P, 8, CHUNK]), ALU.subtract)
                    last = nc.vector.tensor_copy(dv[:, :, 1, :], v[:, :, 1, :])
                else:
                    width = LEVELS[n - 2]
                    v, dv = (u.rearrange("p h (m z) -> p (h m) z", z=2 * width) for u in (bh, DL))
                    last = nc.vector.tensor_tensor(dv, v, v[:, :, width - 1:width].to_broadcast([P, 4 * SEQ // (2 * width), 2 * width]),
                                                   ALU.subtract)
                last.then_inc(sem("delta_ready"), 1)

            def scale_operands(half, n):
                width = P if n == 1 else LEVELS[n - 2]
                for r, src in enumerate((KC, QC)):
                    dst, sv = (v.rearrange("p h (m side z) -> p (h m) side z", side=2, z=width)[:, :, r, :]
                               for v in (LV[:, n % 2], src[:, 4 * half:4 * half + 4, :]))
                    last = nc.vector.tensor_tensor(dst, dst, sv, ALU.mult)
                last.then_inc(sem("level_ready"), 1)

            def select(half, n):
                if n == 1:
                    ps, b = product(dve, ("lv", half, 1, 0))
                    nc.vector.tensor_copy(AX_, ps[:, :].rearrange("p (h q) -> p h q", h=4)).then_inc(bank_free(b), 1)
                    return
                for g in range(2):
                    ps, b = product(dve, ("lv", half, n, g))
                    dst = AT[:, 2 * g:2 * g + 2].rearrange("p h t q -> p (h t) q")
                    pv = ps[:, :].rearrange("p (h q) -> p h q", h=4)
                    if n == 0:
                        last = nc.vector.tensor_tensor(dst, pv, consts[:, C_ID:C_ID + P].unsqueeze(1)
                                                       .to_broadcast([P, 4, P]), ALU.mult)
                    else:
                        last = nc.vector.copy_predicated(dst, level_mask[:, n - 2, :].unsqueeze(1)
                                                         .to_broadcast([P, 4, P]), pv)
                    last.then_inc(bank_free(b), 1)
                evacuated(dve, ("lv", half, n, 1))

            dve.wait_ge(sem("level_masks"), 1)
            for half in range(2):
                for jj in range(4):
                    evacuated(dve, (f"q{half}", jj))
                if half == 1:
                    dve.wait_ge(*done_at[("at", 0)])
                    dve.wait_ge(sem("decay_ready"), NLV)
                delta(half, 1)
                for n in range(1, NLV + 1):
                    dve.wait_ge(sem("decay_ready"), half * NLV + n)
                    if n < NLV:
                        delta(half, n + 1)
                    scale_operands(half, n)
                    select(half, n - 1)
                select(half, NLV)

            for half in range(2):
                for t in range(T):
                    evacuated(dve, ("hgrn_o", half, t))
            heads = XN[:, :, :].rearrange("p t (h n) -> p (t h) n", n=P)
            sq = A[0][:, :].rearrange("p (g n) -> p g n", n=P)
            link(nc.vector.tensor_tensor(sq, heads, heads, ALU.mult))
            hm = small[:, MX:MX + 16]
            link(nc.vector.tensor_reduce(hm, sq, AX_X, ALU.add))
            nc.vector.tensor_scalar(hm, hm, 1.0 / P, EPS, ALU.mult, ALU.add).then_inc(sem("head_ms"), 1)
            dve.wait_ge(sem("head_rms"), 1)
            link(nc.vector.reciprocal(hm, hm))
            link(nc.vector.tensor_tensor(heads, heads, hm.unsqueeze(2).to_broadcast([P, 16, P]), ALU.mult))
            dve.wait_ge(sem("gate_ready"), 4)
            nc.vector.tensor_tensor(XN[:, :, :], XN[:, :, :], SG, ALU.mult).then_inc(sem("hgrn_ready"), 1)
            evacuate_T("hgrn_out", None)
            low("oc", 1, 1)
            residual((sem("acc_full"), 4), None)

            def low_e(kind, g, slot, value):
                dve.wait_ge(sem("split_hi"), value)
                high_, low_ = e_split(kind, g)
                nc.vector.tensor_tensor(low_, raw[:, slot, :], high_.bitcast(F32), ALU.subtract).then_inc(sem("split_lo"), 1)

            def pass_start(p, which):
                for kind, g, n in which:
                    low_e(kind, g, (N0 + n) % RAW, p * NE * PER_ITEM + N0 + n + 1)

            norm(3)
            dve.wait_ge(sem("gain_row_in"), 16)
            dve.wait_ge(sem("xn_ready"), 8)
            nc.vector.tensor_tensor(XN[:, :, :], XN[:, :, :], gain_row[:, :].unsqueeze(1).to_broadcast([P, T, D]),
                                    ALU.mult).then_inc(sem("xg_ready"), 1)
            pass_start(0, PASS_START[0:2])
            evacuate_T("ffn1", None)

            ps, b = product(dve, "router")
            nc.vector.tensor_copy(route[:, :, 0:NE], ps[:, 0:2 * NE].rearrange("p (t e) -> p t e", t=T)).then_inc(bank_free(b), 1)
            evacuated(dve, "router")
            for t in range(T):
                link(nc.vector.max(route[:, t, 8:16], route[:, t, 0:NE]))
                link(nc.vector.max_index(route[:, t, 16:24].bitcast(U32), route[:, t, 8:16], route[:, t, 0:NE]))
            link(nc.vector.tensor_copy(route[:, :, 24:32], route[:, :, 16:24].bitcast(U32)))
            nc.vector.tensor_tensor(route[:, :, 32:33], route[:, :, 9:10], route[:, :, 8:9], ALU.subtract)\
                .then_inc(sem("top_gap"), 1)
            dve.wait_ge(sem("gap_exp"), 1)
            link(nc.vector.tensor_scalar(route[:, :, 33:34], route[:, :, 32:33], 1.0, None, ALU.add))
            link(nc.vector.reciprocal(route[:, :, 34:35], route[:, :, 33:34]))
            link(nc.vector.tensor_tensor(route[:, :, 35:36], route[:, :, 32:33], route[:, :, 34:35], ALU.mult))
            iota = consts[:, C_IOTA:C_IOTA + NE]
            for t in range(T):
                nc.vector.tensor_scalar(route[:, t, 40:48], iota, route[:, t, 24:25], None, ALU.is_equal)
                link(nc.vector.tensor_scalar(route[:, t, 48:56], iota, route[:, t, 25:26], None, ALU.is_equal))
            nc.vector.tensor_tensor(route[:, :, 56:64], route[:, :, 40:48], route[:, :, 48:56], ALU.add)\
                .then_inc(sem("chosen_ready"), 1)
            link(nc.vector.memset(rank_of[:, :, :], -1.0))
            link(nc.vector.memset(combine[:, :, :], 0.0))
            for t in range(T):
                link(nc.vector.tensor_scalar(route[:, t, 40:48], iota, route[:, t, 24:25], route[:, t, 34:35],
                                             ALU.is_equal, ALU.mult))
                link(nc.vector.tensor_scalar(route[:, t, 48:56], iota, route[:, t, 25:26], route[:, t, 35:36],
                                             ALU.is_equal, ALU.mult))
            for p in range(2):
                last = nc.vector.tensor_tensor(combine[:, :, NE * p:NE * p + NE], route[:, :, 40:48], route[:, :, 48:56], ALU.add)
            link(last)

            ps, b = product(dve, "rank")
            rank = rank_of[:, :, 0:NE]
            link(nc.vector.tensor_scalar(rank, ps[:, 0:2 * NE].rearrange("p (t e) -> p t e", t=T), 1.0, None, ALU.add))
            nc.vector.reduce_max(small[:, 120:121], ps[:, 2 * NE:3 * NE], AX_X).then_inc(bank_free(b), 1)
            evacuated(dve, "rank")
            link(nc.vector.tensor_tensor(rank, rank, route[:, :, 56:64], ALU.mult))
            link(nc.vector.tensor_scalar(rank, rank, -1.0, None, ALU.add))
            link(nc.vector.tensor_scalar(rank_of[:, :, NE:2 * NE], rank, -float(P), None, ALU.add))
            nc.vector.tensor_scalar(overflow[:, 0:1], small[:, 120:121], float(P), None, ALU.is_gt)\
                .then_inc(sem("overflow_ready"), 1)

            slots = consts[:, C_SLOT:C_SLOT + P]

            def select_tokens(nxt):
                nc.vector.tensor_scalar(sel[:, 0, :], slots, rank_of[:, 0, bass.ds(nxt, 1)], None, ALU.is_equal)
                nc.vector.tensor_scalar(sel[:, 1, :], slots, rank_of[:, 1, bass.ds(nxt, 1)], None, ALU.is_equal)\
                    .then_inc(sem("sel_ready"), 1)

            def place_x(par, nxt, wait, bank, freed):
                for h in range(2):
                    dve.wait_ge(sem("xe_high"), nxt * 2 + (h + 1))
                    ps = bank(("x", h))
                    nc.vector.tensor_tensor(XE[:, par, 1, 4 * h:4 * h + 4, :], ps[:, :].rearrange("p (k q) -> p k q", k=4),
                                            XE[:, par, 0, 4 * h:4 * h + 4, :].bitcast(F32), ALU.subtract).then_inc(freed(("x", h)), 1)
                wait(("gate",))
                nc.vector.tensor_copy(slot_gate[:, par:par + 1], bank(("gate",))[:, 0:1]).then_inc(freed(("gate",)), 1)

            select_tokens(0)
            place_x(0, 0, lambda key: product(dve, ("first",) + key),
                    lambda key: psum[work.where[("first",) + key][0]],
                    lambda key: bank_free(work.where[("first",) + key][0]))
            pass_start(0, PASS_START[2:])

            def item(i, par, last):
                def bank(key):
                    return ebank[item_at[key] % BANKS_E]

                def split_step(g, which):
                    for (kind, gg, n), (_, _, n0) in zip(item_splits(i, g, last), item_splits(0, g, last)):
                        if kind in which:
                            low_e(kind, gg, (N0 + n0) % RAW, n + (N0 + 1))

                for g in range(GE + 1):
                    if g > 0:
                        dve.wait_ge(sem("hT_high"), i * GE + (FG + g))
                        nc.vector.tensor_tensor(hT[:, (g - 1) % 2, 1, 0:256], bank(("ht", g - 1))[:, 0:256],
                                                hT[:, (g - 1) % 2, 0, 0:256].bitcast(F32), ALU.subtract)\
                            .then_inc(e_read(("ht", g - 1), i)[0], 1)
                    if g == GE // 2 + 1:
                        place_x(1 - par, i + 1, lambda key: dve.wait_ge(*e_full(key, i)), bank,
                                lambda key: e_read(key, i)[0])
                    if g < GE:
                        split_step(g, (0,))
                        dve.wait_ge(sem("silu_ready"), i * GE + (2 * FG + g + 1))
                        nc.vector.tensor_tensor(hexp[:, g % 2, :], hexp[:, g % 2, :], bank(("gu", g))[:, 256:512], ALU.mult)\
                            .then_inc(e_read(("gu", g), i)[0], 1)
                        if g == GE // 2 - 1:
                            select_tokens(i + 1)
                        split_step(g, (1, 2))
                for n in range(4):
                    t, c = divmod(n, 2)
                    dve.wait_ge(*e_full(("y", n), i))
                    xs = X[:, t, 512 * c:512 * c + 512]
                    nc.vector.tensor_tensor(xs, xs, bank(("y", n))[:, :], ALU.add).then_inc(e_read(("y", n), i)[0], 1)

            def items(p):
                if p:
                    pass_start(p, PASS_START)
                with dve.Fori(0, NE // 2 - 1) as m:
                    for u in range(2):
                        item(m * 2 + (NE * p + u), u, False)
                item(NE * p + NE - 2, 0, False)
                item(NE * p + NE - 1, 1, True)
                for n in range(4):
                    dve.wait_ge(*e_read(("y", n), NE * p + NE - 1))

            passes(dve, items)
            dve.sem_inc(sem("x_final"), 1)
            norm(4)
            dve.wait_ge(sem("xn_ready"), 10)
            dve.wait_ge(sem("final_in"), 16)
            for t in range(T):
                nc.vector.tensor_tensor(XN[:, t, :], XN[:, t, :], gain_row[:, :], ALU.mult).then_inc(sem("out_ready"), 1)


_INS = ["x", "positions", "norm_mix", "norm_ffn", "w_in_ab", "fgate_bias", "w_out_ab", "w_in_c",
        "lower_bounds", "gnorm_c", "w_out_c", "w_gate_ffn", "w_up_ffn", "w_down_ffn", "router",
        "w_gate_moe", "w_up_moe", "w_down_moe", "norm_final"]


def kernel(**inputs):
    import numpy as _np
    import concourse.bacc as _bacc
    from concourse import mybir as _mybir
    from concourse.bass_utils import run_bass_kernel_spmd as _run

    nc = _bacc.Bacc("TRN2", target_bir_lowering=False, num_devices=1)
    arrays, args = {}, []
    every = {n: _np.ascontiguousarray(inputs[n]) for n in _INS}
    every.update(shape_constants())
    for name, a in every.items():
        arrays[f"in_{name}"] = a
        args.append(nc.dram_tensor(f"in_{name}", a.shape, _mybir.dt.from_np(a.dtype), kind="ExternalInput").ap())
    args.append(nc.dram_tensor("out_0", (1, SEQ, D), F32, kind="ExternalOutput").ap())
    trunk(nc, *args)
    r = _run(nc, [arrays], core_ids=[0])
    return r.results[0]["out_0"]
```

```python
from contextlib import ExitStack

import numpy as np
import concourse.bass as bass
from concourse import mybir

ALU = mybir.AluOpType
ACT = mybir.ActivationFunctionType
F32 = mybir.dt.float32
F32R = mybir.dt.float32r
I32 = mybir.dt.int32
U32 = mybir.dt.uint32
AX_X = mybir.AxisListType.X

P = 128
SEQ = 256
T = SEQ // P
D = 1024
KD = D // P
HD = 64
NHA = 8
NHB = 8
NH = NHA + NHB
ROPE_DIM = HD // 4
ROPE_THETA = 500000.0
DILATED = ((128, 1), (512, 4), (2048, 16))
NHC = 8
CHUNK = 64
FF = 2816
NE = 8
FFE = 3584
EPS = 1e-6
NEG = -1.0e30

RAW = 6
SPLIT = 3
CHUNK_F = 2048
WORK = 4
BANKS_E = 6
LEVELS = (64, 32, 16, 8, 4, 2, 1)

C_ID, C_PERM, C_MA, C_MB, C_RST, C_FREQ, C_TRI, C_ONE, C_SLOT, C_IOTA, C_END = np.cumsum(
    [0, P, P, 3 * P, 3 * P, SEQ, 1, P, P, P, NE]).tolist()


def shape_constants():
    c = np.zeros((P, C_END), np.float32)
    c[:, C_ID:C_ID + P] = np.eye(P)
    half = ROPE_DIM // 2
    for base in range(0, P, HD):
        for i in range(half):
            c[base + half + i, C_PERM + base + i] = -1.0
            c[base + i, C_PERM + base + half + i] = 1.0
            f = np.power(np.float32(ROPE_THETA), -np.float32(i) / np.float32(half), dtype=np.float32)
            c[base + i, C_FREQ] = c[base + half + i, C_FREQ] = f
    q = np.arange(SEQ)[:, None]
    k = np.arange(SEQ)[None, :]
    count = np.zeros((SEQ, SEQ))
    for window, dilation in DILATED:
        count += (q >= k) & (q - k <= window) & ((q - k) % dilation == 0)
    dilated = np.where(count > 0, np.log(np.maximum(count, 1)), NEG)
    causal = np.where(q >= k, 0.0, NEG)
    for off, m in ((C_MA, dilated), (C_MB, causal)):
        c[:, off:off + P] = m[:P, :P]
        c[:, off + P:off + 3 * P] = m[P:, :]
    c[:, C_RST:C_RST + SEQ] = (np.arange(SEQ) % CHUNK != 0)[None, :]
    c[:, C_TRI:C_TRI + P] = np.arange(P)[:, None] < np.arange(P)[None, :]
    c[:, C_ONE:C_ONE + P] = 1.0
    c[:, C_SLOT:C_SLOT + P] = np.arange(P)[None, :]
    c[:, C_IOTA:C_IOTA + NE] = np.arange(NE)[None, :]
    onehot = np.zeros((NHB, NHB, SEQ), np.float32)
    for h in range(NHB):
        onehot[h, h, :] = 1.0
    s = np.arange(P)[:, None]
    t = np.arange(P)[None, :]
    level = np.zeros((P, len(LEVELS), P), np.int32)
    for n, w in enumerate(LEVELS):
        level[:, n, :] = (s // (2 * w) == t // (2 * w)) & (s % (2 * w) < w) & (t % (2 * w) >= w)
    return {"c_float": c, "c_onehot": onehot, "c_level": level}


class Turns:

    def __init__(self, places, beside=None):
        self.places, self.at = list(places), 0
        self.used, self.where = ({}, {}) if beside is None else (beside.used, beside.where)

    def take(self, key):
        place = self.places[self.at % len(self.places)]
        self.at += 1
        self.used[place] = self.used.get(place, 0) + 1
        self.where[key] = (place, self.used[place])
        return self.where[key]


def trunk(nc, x, positions, norm_mix, norm_ffn, w_in_ab, fgate_bias, w_out_ab, w_in_c, lower_bounds,
          gnorm_c, w_out_c, w_gate_ffn, w_up_ffn, w_down_ffn, router, w_gate_moe, w_up_moe,
          w_down_moe, norm_final, c_float, c_onehot, c_level, out):
    FG = FF // 256
    GE = FFE // 256

    stream = []
    split_slot, before_in_slot, in_slot = {}, {}, {}

    def cols(w, row, c0, n):
        return w[row:row + 256, c0:c0 + n].rearrange("(k p) n -> p k n", p=P)

    def enqueue(key, slot, parts):
        split_slot[key] = slot
        before_in_slot[key] = in_slot.get(slot)
        in_slot[slot] = key
        stream.append((key, parts))

    def plain_parts(w, half, c0):
        return [(1024 * m, 2, 512, 512, cols(w, 512 * half + 256 * m, c0, 512)) for m in range(2)]

    def gate_up_parts(wg, wu, half, g):
        return [(256 * m, 4, 256, 512, w[512 * half:512 * half + 512, 256 * g:256 * g + 256]
                 .rearrange("(k p) n -> p k n", p=P)) for m, w in enumerate((wg, wu))]

    def down_parts(w, g):
        return [(1024 * m, 1, 1024, 1024, w[256 * g + P * m:256 * g + P * m + P, :]
                 .rearrange("(k p) n -> p k n", p=P)) for m in range(2)]

    turn = [0]

    def enqueue_pair(name, c, w):
        for half in range(2):
            enqueue((name, c, half), turn[0] % SPLIT, plain_parts(w, half, 512 * c))
            turn[0] += 1

    w_ab, w_oab, w_c, w_oc = w_in_ab[0], w_out_ab[0], w_in_c[0], w_out_c[0]
    C_ORDER = (2, 3, 0, 1, 4, 6, 5, 7)
    for c in range(6):
        enqueue_pair("ab", c, w_ab)
    for c in range(2):
        enqueue_pair("oab", c, w_oab)
    sa, sb_, sd = (turn[0] % SPLIT, (turn[0] + 1) % SPLIT, (turn[0] + 2) % SPLIT)

    def enqueue_ff(kind, g):
        if kind == 2:
            enqueue(("ff", g, 2), sd, down_parts(w_down_ffn[0], g))
        else:
            enqueue(("ff", g, kind), (sa, sb_)[kind], gate_up_parts(w_gate_ffn[0], w_up_ffn[0], kind, g))

    enqueue_ff(0, 0)
    enqueue_ff(1, 0)
    for g in range(FG - 1):
        enqueue_ff(0, g + 1)
        enqueue_ff(1, g + 1)
        enqueue_ff(2, g)
    enqueue_pair("c", C_ORDER[0], w_c)
    enqueue_ff(2, FG - 1)
    for c in C_ORDER[1:]:
        enqueue_pair("c", c, w_c)
    for c in range(2):
        enqueue_pair("oc", c, w_oc)
    assert turn[0] % SPLIT == 0
    position = {key: n for n, (key, _) in enumerate(stream)}
    N0 = len(stream)
    PER_ITEM = 3 * GE
    assert PER_ITEM % RAW == 0
    ITEM_POS = 5

    work = Turns(range(WORK))
    beside = Turns((0, 1), work)
    outputs = Turns((2, 3), work)
    side = Turns(range(WORK, WORK + 4), work)

    with ExitStack() as ctx:
        def sb(name, shape, dt=F32):
            return ctx.enter_context(nc.sbuf_tensor(name, shape, dt))

        sems = {}

        def sem(name):
            if name not in sems:
                sems[name] = ctx.enter_context(nc.semaphore(name))
            return sems[name]

        consts = sb("consts", [P, C_END])
        level_mask = sb("level_mask", [P, len(LEVELS), P], mybir.dt.uint8)
        vec_rows = sb("vec_rows", [6 * KD, P])
        vec_cols = sb("vec_cols", [P, 6 * KD])
        narrow = sb("narrow", [P, 2, KD, NE], F32R)
        fbias = sb("fbias", [NHB, 1])
        gnorm = sb("gnorm", [P, P])
        gain_row = sb("gain_row", [P, D])
        small = sb("small", [P, 128])
        route = sb("route", [P, T, 64])
        wf, wr = (route[:, t, :].rearrange("p (k n) -> p k n", n=NE) for t in range(T))
        rank_of = sb("rank_of", [P, T, 2 * NE + 1])
        combine = sb("combine", [P, T, 2 * NE + 1])
        slot_gate = sb("slot_gate", [P, 2])
        overflow = sb("overflow", [P, 2], I32)
        X = sb("X", [P, T, D])
        XN = sb("XN", [P, T, D])
        raw = sb("raw", [P, RAW, CHUNK_F])
        hi_lo = sb("hi_lo", [P, SPLIT, 2, CHUNK_F], F32R)
        xt = sb("xt", [P, 4096], F32R)
        hT = sb("hT", [P, 2, 2, 512], F32R)

        with ExitStack() as before:
            def sb1(name, shape, dt=F32):
                return before.enter_context(nc.sbuf_tensor(name, shape, dt))

            A = [sb1(f"A{i}", [P, 2048]) for i in range(5)]
            arena = sb1("arena", [P, 3072])
            hbuf = sb1("hbuf", [P, 2, T * 256])
            gate_rows = sb1("gate_rows", [P, SEQ], F32R)
        hi_lo_e = sb("hi_lo_e", [P, SPLIT, 2, CHUNK_F], F32R)
        sel = sb("sel", [P, T, P])
        selT = sb("selT", [P, 2, T * P])
        ye = sb("ye", [P, D])
        logits = sel[0:NE, :, :].rearrange("p t q -> p (t q)")
        hexp = sb("hexp", [P, 2, 256])

        HTH, HTL = (xt[:, 2048 * m:2048 * m + 2048].rearrange("p (k q) -> p k q", k=KD) for m in range(2))
        XE = xt[:, :].rearrange("p (par m k q) -> p par m k q", par=2, m=2, k=KD)
        onehot = A[1][0:NHB, 0:2048].rearrange("p (h q) -> p h q", h=NHB)
        gate_cols = hT[:, :, :, :].rearrange("p a b q -> p (a b q)").rearrange("p (h q) -> p h q", h=NHB)
        rope = arena[:, 0:6 * SEQ].rearrange("p (a q) -> p a q", a=6)
        fox = arena[0:NHB, 6 * SEQ:12 * SEQ].rearrange("p (a q) -> p a q", a=6)
        level_words = A[4][:, 0:len(LEVELS) * P].bitcast(I32).rearrange("p (n q) -> p n q", q=P)
        pos_i = A[4][:, 0:SEQ].bitcast(I32)

        psum = [ctx.enter_context(nc.psum_tensor(f"work{i}", [P, 512], F32)) for i in range(WORK)]
        acc = [ctx.enter_context(nc.psum_tensor(f"acc{i}", [P, 512], F32)) for i in range(4)]

        psum += acc
        ident = consts[:, C_ID:C_ID + P]
        perm = consts[:, C_PERM:C_PERM + P]
        score_mask = {"a": consts[:, C_MA:C_MA + 3 * P], "b": consts[:, C_MB:C_MB + 3 * P]}
        gain = {"mix0": 0, "mix1": KD, "ffn0": 2 * KD, "ffn1": 3 * KD}
        NORMS = ["mix0", "ffn0", "mix1", "ffn1", "final"]

        SS, MS, RS, WARM = 0, 2, 4, 6
        MX, SM, RI = 8, 40, 72
        LBC, OML = 104, 112

        Q = {"a": A[0][:, :].rearrange("p (j s q) -> p j s q", s=2, q=SEQ),
             "b": A[1][:, :].rearrange("p (j s q) -> p j s q", s=2, q=SEQ)}
        K = {"a": A[3][:, 0:1024].rearrange("p (j q) -> p j q", q=SEQ),
             "b": A[3][:, 1024:2048].rearrange("p (j q) -> p j q", q=SEQ)}
        RAW_ROT = {"qa": hbuf[:, :, :].rearrange("p a (j q) -> p (a j) q", q=SEQ), "ka": K["a"]}
        V = A[2][:, :].rearrange("p (t n) -> p t n", t=T)
        SRING = 4
        S = [A[4][:, 384 * i:384 * i + 384] for i in range(SRING)]
        PARKED = [XN[:, 0, 768:1024], XN[:, 1, 384:640], XN[:, 1, 640:896]]
        PT = [XN[:, 0, 0:384], XN[:, 0, 384:768], XN[:, 1, 0:384]]
        cosT, sinT = rope[:, 0, :], rope[:, 1, :]
        rtmp = A[4][:, 1536:2048]

        def full(i):
            return sem(f"raw_full{i}")

        def bank_full(i):
            return sem(f"bank_full{i}")

        def bank_free(i):
            return sem(f"bank_free{i}")

        def evacuated(eng, key):
            b, use = work.where[key]
            eng.wait_ge(bank_free(b), use)

        def product(eng, key):
            b, use = work.where[key]
            eng.wait_ge(bank_full(b), use)
            return psum[b], b

        def product_of(key):
            b, use = work.where[key]
            return bank_full(b), use

        NLV = len(LEVELS) + 1

        def parts_of(key):
            return hi_lo[:, split_slot[key], 0, :], hi_lo[:, split_slot[key], 1, :]

        def split_high(act, key):
            n = position[key]
            act.wait_ge(full(n % RAW), 32 * (n // RAW + 1))
            if before_in_slot[key] is not None:
                act.wait_ge(*done_at[before_in_slot[key]])
            nc.scalar.activation(parts_of(key)[0], raw[:, n % RAW, :], ACT.Copy).then_inc(sem("split_hi"), 1)

        def split_low(eng, key, tensor_tensor, handed_over=False):
            n = position[key]
            if handed_over:
                eng.wait_ge(sem("split_lo"), n)
            eng.wait_ge(sem("split_hi"), n + 1)
            tensor_tensor(parts_of(key)[1], raw[:, n % RAW, :], parts_of(key)[0].bitcast(F32),
                                    ALU.subtract).then_inc(sem("split_lo"), 1)

        item_keys = [("gu", 0)]
        for g in range(1, GE):
            item_keys += [("gu", g), ("ht", g - 1)]
            if g == GE // 2:
                item_keys += [("x", 0), ("x", 1), ("selT",), ("gate",)]
        item_keys += [("ht", GE - 1)] + [("y", n) for n in range(4)]
        assert len(item_keys) % BANKS_E == 0
        USES = len(item_keys) // BANKS_E
        item_at = {key: n for n, key in enumerate(item_keys)}
        ebank = psum[0:WORK] + [acc[2], acc[3]]
        ybank = [acc[0], acc[1]]

        def e_full(key, i):
            n = item_at[key]
            return sem(f"expert_full{n % BANKS_E}"), i * USES + (n // BANKS_E + 1)

        def e_free(key, i):
            n = item_at[key]
            return sem(f"expert_free{n % BANKS_E}"), i * USES + (n // BANKS_E + 1)

        def e_read(key, i):
            n = item_at[key]
            return sem(f"expert_free{n % BANKS_E}"), i * USES + (n // BANKS_E + 2)

        def e_split(kind, g):
            slots = hi_lo if g % 2 == 0 else hi_lo_e
            return slots[:, kind, 0, :], slots[:, kind, 1, :]

        def item_splits(i, g, last):
            base = i * PER_ITEM + (ITEM_POS + 3 * g)
            if not last or g + 2 < GE:
                return [(0, g + 2, base), (1, g + 2, base + 1), (2, g + 1, base + 2)]
            return [(2, g + 1, base)] if g + 1 < GE else []

        def split_ready(i, kind, g, last):
            if g == 0 and kind < 2:
                return i * PER_ITEM + (N0 + 2)
            if g == 0:
                return i * PER_ITEM + (N0 + 5)
            if g == 1 and kind < 2:
                return i * PER_ITEM + (N0 + 3 + kind)
            if last and g == GE - 1 and kind == 2:
                return i * PER_ITEM + (N0 + ITEM_POS + 3 * (GE - 2) + 1)
            n = 3 * (g - 2) + kind if kind < 2 else 3 * (g - 1) + 2
            return i * PER_ITEM + (N0 + ITEM_POS + n + 1)

        PASS_START = [(0, 0, 0), (1, 0, 1), (0, 1, 2), (1, 1, 3), (2, 0, 4)]

        def passes(eng, items):
            items(0)
            eng.wait_ge(sem("overflow_ready"), 1)
            more = eng.value_load(overflow[0:1, 0:1], min_val=0, max_val=1)
            with eng.If(more > 0):
                items(1)

        def filled(b):
            return bank_full(b), work.used[b]

        done_at = {}
        moe = {}

        BC, KC, QC = (A[i][:, :].rearrange("p (h q) -> p h q", h=NHC) for i in range(3))
        VC = A[3][:, :].rearrange("p (t n) -> p t n", t=T)
        SG = A[4][:, :].rearrange("p (t n) -> p t n", t=T)
        LV = arena[:, 0:2048].rearrange("p (b h q) -> p b h q", b=2, h=4)
        DL = arena[:, 2048:3072].rearrange("p (h q) -> p h q", h=4)
        AT = hbuf[:, :, :].rearrange("p a (h t q) -> p (a h) t q", h=2, t=T)
        AX_ = XN[:, 1, 512:1024].rearrange("p (h q) -> p h q", h=4)

        def level_operands(half, n):
            if n == 0:
                return KC[:, 4 * half:4 * half + 4, :], QC[:, 4 * half:4 * half + 4, :]
            return LV[:, n % 2], LV[:, n % 2]

        block = ctx.enter_context(nc.Block())

        @block.tensor
        def _(pe):
            def claim(key, turns=work):
                b, use = turns.take(key)
                if use > 1:
                    pe.wait_ge(bank_free(b), use - 1)
                return psum[b], b

            rest = []

            def transposed(src, name, ready):
                pe.wait_ge(*ready)
                for j in range(KD // 2):
                    ps, b = claim((name, j))
                    for kk in range(2):
                        for t in range(T):
                            k = 2 * j + kk
                            last = nc.tensor.transpose(ps[:, 256 * kk + P * t:256 * kk + P * t + P],
                                                       src[:, t, P * k:P * k + P], ident)
                    last.then_inc(bank_full(b), 1)
                for j in range(KD // 4):
                    evacuated(pe, (name, j))
                rest.extend((name, j) for j in range(KD // 4, KD // 2))

            def other_rows():
                while rest:
                    evacuated(pe, rest.pop(0))

            def split(key):
                pe.wait_ge(sem("split_lo"), position[key] + 1)
                return parts_of(key)

            halves_used = [0]

            def half_used(last, key):
                halves_used[0] += 1
                last.then_inc(sem("half_used"), 1)
                done_at[key] = (sem("half_used"), halves_used[0])

            def three(out, stationary, moving, start, stop):
                (sh, sl), (mh, ml) = stationary, moving
                nc.tensor.matmul(out, sh, mh, start=start, stop=False, skip_group_check=True)
                nc.tensor.matmul(out, sh, ml, start=False, stop=False, skip_group_check=True)
                return nc.tensor.matmul(out, sl, mh, start=False, stop=stop, skip_group_check=True)

            def project_T_steps(name, c, out_name, turns=work):
                banks = [claim((out_name, j), turns) for j in range(2)]
                for half in range(2):
                    key = (name, c, half)
                    w = [v.rearrange("p (k n) -> p k n", k=4) for v in split(key)]
                    if half:
                        other_rows()
                    for j in range(4):
                        for k in range(4):
                            x_ = [v[:, 4 * half + k, :] for v in (HTH, HTL)]
                            last = three(banks[j // 2][0][:, SEQ * (j % 2):SEQ * (j % 2) + SEQ], [v[:, k, P * j:P * j + P] for v in w], x_,
                                         half == k == j % 2 == 0, half == 1 and k == 3)
                        if half:
                            if j % 2:
                                last.then_inc(bank_full(banks[j // 2][1]), 1)
                            if j == 3:
                                done_at[key] = filled(banks[1][1])
                        elif j == 3:
                            half_used(last, key)
                        yield

            def token_product(key, half, outs, start_k, stop):
                w = [v.rearrange("p (k n) -> p k n", k=4) for v in split(key)]
                if half:
                    other_rows()
                for t in range(T):
                    for k in range(4):
                        x_ = [v[:, 4 * half + k, P * t:P * t + P] for v in (HTH, HTL)]
                        last = three(outs[t], x_, [v[:, k, :] for v in w], half == k == 0, half == 1 and k == 3)
                    yield last

            def project_steps(name, c, out_name, turns=work):
                banks = [claim((out_name, t), turns) for t in range(T)]
                for half in range(2):
                    key = (name, c, half)
                    for t, last in enumerate(token_product(key, half, [b[0][:, :] for b in banks], 0, 0)):
                        if half:
                            last.then_inc(bank_full(banks[t][1]), 1)
                            if t == T - 1:
                                done_at[key] = filled(banks[t][1])
                        elif t == T - 1:
                            half_used(last, key)
                        yield

            def project_T(name, c, out_name):
                for _ in project_T_steps(name, c, out_name):
                    pass

            def project(name, c, out_name):
                for _ in project_steps(name, c, out_name):
                    pass

            def out_project(name, frees, sums):
                if frees:
                    pe.wait_ge(sem("acc_free"), frees)
                for c in range(2):
                    for half in range(2):
                        key = (name, c, half)
                        for t, last in enumerate(token_product(key, half, [acc[2 * t + c][:, :] for t in range(T)], 0, 0)):
                            if half:
                                last.then_inc(sem("acc_full"), 1)
                        if not half:
                            half_used(last, key)
                    done_at[key] = (sem("acc_full"), sums + 2 * c + 2)

            pe.wait_ge(sem("consts_in"), 16)
            pe.wait_ge(sem("vecs_in"), 16 * 3)
            ps, b = claim("vecs")
            nc.tensor.transpose(ps[:, 0:6 * KD], vec_rows[:, :], consts[0:6 * KD, C_ID:C_ID + 6 * KD])\
                .then_inc(bank_full(b), 1)

            transposed(XN, "mix0", (sem("xn_ready"), 2))
            def narrow_product(key, use):
                pe.wait_ge(sem("narrow_low"), use)
                other_rows()
                ps, b = claim(key)
                for k in range(KD):
                    for m in range(2):
                        for v in (HTH, HTL):
                            last = nc.tensor.matmul(ps[0:NE, 0:SEQ], narrow[:, m, k, :], v[:, k, :],
                                                    start=(k == m == 0 and v is HTH),
                                                    stop=(k == KD - 1 and m == 1 and v is HTL))
                last.then_inc(bank_full(b), 1)

            narrow_product("flogit", 1)
            project_T("ab", 0, "qa")
            project_T("ab", 1, "ka")
            project("ab", 2, "va")
            for n, name in enumerate(("qa", "ka")):
                for jj in range(2):
                    evacuated(pe, (name, jj))
                    ps, b = claim(("rot", name, jj))
                    nc.tensor.matmul(ps[:, :], perm, RAW_ROT[name][:, 2 * jj:2 * jj + 2, :],
                                     start=True, stop=True).then_inc(bank_full(b), 1)
            def scores(h):
                kind = "a" if h < NHA else "b"
                q, k = Q[kind][:, (h % NHA) // 2, h % 2, :], K[kind][:, (h % NHA) // 2, :]
                if h == 0:
                    pe.wait_ge(sem("rope_ready"), 4)
                    pe.wait_ge(sem("queries_cleared"), 2)
                if h == NHA:
                    for n in ("qb", "kb"):
                        for jj in range(2):
                            evacuated(pe, (n, jj))
                    pe.wait_ge(sem("fox_ready"), 1)
                ps, b = claim(("s", h), side)
                for t in range(T):
                    o = ps[:, P * t:P * t + P * (t + 1)]
                    last = nc.tensor.matmul(o, q[:, P * t:P * t + P], k[:, 0:P * (t + 1)],
                                            start=True, stop=(kind == "a"))
                    if kind == "b":
                        last = nc.tensor.matmul(o, gate_rows[:, P * t:P * t + P], gate_cols[:, h - NHA, 0:P * (t + 1)],
                                                start=False, stop=True)
                last.then_inc(bank_full(b), 1)

            def probs_T(h):
                pe.wait_ge(sem("probs_ready"), h + 1)
                ps, b = claim(("p", h), side)
                s = S[h % SRING]
                for n, blk in enumerate((s[:, 0:P], s[:, P:2 * P], s[:, 2 * P:3 * P])):
                    last = nc.tensor.transpose(ps[:, P * n:P * n + P], blk, ident)
                last.then_inc(bank_full(b), 1)

            def values(h):
                evacuated(pe, ("p", h))
                if h % NHA == 0:
                    for t in range(T):
                        evacuated(pe, ("va" if h < NHA else "vb", t))
                pair = h // 2
                if h % 2 == 0:
                    claim(("o", pair), outputs)
                b = work.where[("o", pair)][0]
                o = psum[b][HD * (h % 2):HD * (h % 2) + HD, 0:SEQ]
                pt = PT[h % 3]
                nc.tensor.matmul(o, V[:, 0, HD * h:HD * h + HD], pt[:, 0:2 * P], start=True, stop=False)
                last = nc.tensor.matmul(o[:, P:2 * P], V[:, 1, HD * h:HD * h + HD], pt[:, 2 * P:3 * P],
                                        start=False, stop=True)
                last.then_inc(bank_full(b) if h % 2 else sem("even_values"), 1)

            def later_projections():
                yield from project_T_steps("ab", 3, "qb", beside)
                yield from project_T_steps("ab", 4, "kb", beside)
                yield from project_steps("ab", 5, "vb", beside)

            pieces = later_projections()
            for _ in range(8):
                next(pieces)
            for i in range(NH + 3):
                if i < NH:
                    scores(i)
                for _ in range(2 if i < 2 else 1):
                    next(pieces, None)
                if 2 <= i < NH + 2:
                    probs_T(i - 2)
                if i >= 3:
                    values(i - 3)
            assert next(pieces, "done") == "done"

            for pair in range(NH // 2):
                evacuated(pe, ("o", pair))
            out_project("oab", 0, 0)

            transposed(XN, "ffn0", (sem("xn_ready"), 4))
            pe.wait_ge(sem("acc_free"), 4)
            for g in range(FG + 1):
                if g < FG:
                    banks = [claim(("gu", g, t)) for t in range(T)]
                    for last in token_product(("ff", g, 0), 0, [b[0][:, :] for b in banks], 0, 0):
                        pass
                    half_used(last, ("ff", g, 0))
                if g > 0:
                    for t in range(T):
                        evacuated(pe, ("gu", g - 1, t))
                    ps, b = claim(("ht", g - 1))
                    for f in range(2):
                        for t in range(T):
                            last = nc.tensor.transpose(ps[:, 256 * f + P * t:256 * f + P * t + P],
                                                       hbuf[:, (g - 1) % 2, 256 * t + P * f:256 * t + P * f + P], ident)
                    last.then_inc(bank_full(b), 1)
                if g < FG:
                    for t, last in enumerate(token_product(("ff", g, 1), 1, [b[0][:, :] for b in banks], 0, 0)):
                        last.then_inc(bank_full(banks[t][1]), 1)
                    done_at[("ff", g, 1)] = filled(banks[1][1])
                if g > 0:
                    i = g - 1
                    w = [v.rearrange("p (f n) -> p f n", f=2) for v in split(("ff", i, 2))]
                    evacuated(pe, ("ht", i))
                    steps = [(f, t, c) for f in range(2) for t in range(T) for c in range(2)]
                    if i == FG - 1:
                        steps = [(f, t, c) for t in range(T) for c in range(2) for f in range(2)]
                    for f, t, c in steps:
                        h_ = [hT[:, i % 2, m, 256 * f + P * t:256 * f + P * t + P] for m in range(2)]
                        last = three(acc[2 * t + c][:, :], h_, [v[:, f, 512 * c:512 * c + 512] for v in w],
                                     i == f == 0, i == FG - 1 and f == 1)
                        if i == FG - 1 and f == 1 and (t, c) != (T - 1, 1):
                            last.then_inc(sem("ffn_sums"), 1)
                    last.then_inc(sem("down_used"), 1)
                    done_at[("ff", i, 2)] = (sem("down_used"), i + 1)

            transposed(XN, "mix1", (sem("xn_ready"), 6))
            for c, name in ((2, "f0"), (3, "f1"), (0, "q0"), (1, "q1")):
                project_T("c", c, name)

            def c_pieces():
                for c, name in ((4, "v0"), (6, "g0"), (5, "v1"), (7, "g1")):
                    yield from project_steps("c", c, name, beside)

            pieces = c_pieces()

            def hgrn_outputs(half):
                evacuated(pe, ("lv", half, 1, 0))
                for g in range(2):
                    evacuated(pe, ("lv", half, NLV, g))
                for t in range(T):
                    evacuated(pe, (f"v{half}", t))
                for t in range(T):
                    ps, b = claim(("hgrn_o", half, t), side)
                    for i in range(4):
                        o = ps[:, P * i:P * i + P]
                        h = 4 * half + i
                        if t == 0:
                            last = nc.tensor.matmul(o, AT[:, i, 0, :], VC[:, 0, P * h:P * h + P], start=True, stop=True)
                        else:
                            nc.tensor.matmul(o, AX_[:, i, :], VC[:, 0, P * h:P * h + P], start=True, stop=False)
                            last = nc.tensor.matmul(o, AT[:, i, 1, :], VC[:, 1, P * h:P * h + P], start=False, stop=True)
                    last.then_inc(bank_full(b), 1)
                done_at[("at", half)] = filled(b)

            for _ in range(4):
                next(pieces)

            for half in range(2):
                for n in range(len(LEVELS) + 2):
                    if n == 0:
                        for jj in range(2):
                            evacuated(pe, (f"q{half}", jj))
                        pe.wait_ge(sem("kc_ready"), 1)
                    else:
                        pe.wait_ge(sem("level_ready"), half * NLV + n)
                    kk, qq = level_operands(half, n)
                    for g in range(1 if n == 1 else 2):
                        ps, b = claim(("lv", half, n, g), side)
                        for i in range(4):
                            if n == 1:
                                lhs, rhs = kk[:, i, 0:P], qq[:, i, P:2 * P]
                            else:
                                hh, t = 2 * g + i // 2, i % 2
                                lhs, rhs = kk[:, hh, P * t:P * t + P], qq[:, hh, P * t:P * t + P]
                            last = nc.tensor.matmul(ps[:, P * i:P * i + P], lhs, rhs, start=True, stop=True)
                        last.then_inc(bank_full(b), 1)
                    done_at[("level", half, n)] = filled(b)
                    next(pieces, None)
                    if half == 1 and n == 0:
                        hgrn_outputs(0)
                if half == 1:
                    hgrn_outputs(1)

            assert next(pieces, "done") == "done"
            transposed(XN, "hgrn_out", (sem("hgrn_ready"), 2))
            out_project("oc", 8, 4)

            transposed(XN, "ffn1", (sem("xn_ready"), 8))
            narrow_product("router_T", 2)
            evacuated(pe, "router_T")
            ps, b = claim("router")
            for t in range(T):
                last = nc.tensor.transpose(ps[:, NE * t:NE * t + NE], logits[:, P * t:P * t + P], consts[0:NE, C_ID:C_ID + NE])
            last.then_inc(bank_full(b), 1)
            pe.wait_ge(sem("chosen_ready"), 1)
            ps, b = claim("rank")
            tri, ones = consts[:, C_TRI:C_TRI + P], consts[:, C_ONE:C_ONE + P]
            chosen = [route[:, t, 56:64] for t in range(T)]
            nc.tensor.matmul(ps[:, 0:NE], tri, chosen[0], start=True, stop=True)
            nc.tensor.matmul(ps[:, NE:2 * NE], tri, chosen[1], start=True, stop=False)
            nc.tensor.matmul(ps[:, NE:2 * NE], ones, chosen[0], start=False, stop=True)
            nc.tensor.matmul(ps[:, 2 * NE:3 * NE], ones, chosen[0], start=True, stop=False)
            nc.tensor.matmul(ps[:, 2 * NE:3 * NE], ones, chosen[1], start=False, stop=True).then_inc(bank_full(b), 1)

            def gather(nxt, banks):
                for h in range(2):
                    ps = banks(("x", h))
                    for k in range(4):
                        for t in range(T):
                            kk = P * (4 * h + k)
                            last = nc.tensor.matmul(ps[:, P * k:P * k + P], XN[:, t, kk:kk + P], sel[:, t, :],
                                                    start=(t == 0), stop=(t == T - 1))
                    yield ("x", h), last
                ps = banks(("selT",))
                for t in range(T):
                    last = nc.tensor.transpose(ps[:, P * t:P * t + P], sel[:, t, :], ident)
                yield ("selT",), last
                ps = banks(("gate",))
                for t in range(T):
                    last = nc.tensor.matmul(ps[:, 0:1], sel[:, t, :], combine[:, t, bass.ds(nxt, 1)],
                                            start=(t == 0), stop=(t == T - 1))
                yield ("gate",), last

            pe.wait_ge(sem("xg_ready"), 1)
            pe.wait_ge(sem("sel_ready"), 1)
            for key, last in gather(0, lambda key: claim(("first",) + key)[0]):
                last.then_inc(bank_full(work.where[("first",) + key][0]), 1)
            for key in (("x", 0), ("x", 1), ("selT",), ("gate",)):
                evacuated(pe, ("first",) + key)
            pe.wait_ge(sem("acc_free"), 12)

            def item(i, par, last_item):
                def claim_e(key):
                    pe.wait_ge(*e_free(key, i))
                    return ebank[item_at[key] % BANKS_E]

                def there(key, last):
                    last.then_inc(e_full(key, i)[0], 1)

                def ready(kind, g):
                    pe.wait_ge(sem("split_lo"), split_ready(i, kind, g, last_item))
                    return e_split(kind, g)

                def gate_up_half(ps, g, half):
                    w = [v.rearrange("p (k n) -> p k n", k=4) for v in ready(half, g)]
                    for k in range(4):
                        x_ = [XE[:, par, m, 4 * half + k, :] for m in range(2)]
                        last = three(ps[:, :], x_, [v[:, k, :] for v in w], half == k == 0, half == 1 and k == 3)
                    return last

                for g in range(GE + 1):
                    if g < GE:
                        ps_gu = claim_e(("gu", g))
                        gate_up_half(ps_gu, g, 0).then_inc(sem("expert_half_used"), 1)
                    if g > 0:
                        pe.wait_ge(*e_read(("gu", g - 1), i))
                        ps = claim_e(("ht", g - 1))
                        for f in range(2):
                            last = nc.tensor.transpose(ps[:, P * f:P * f + P], hexp[:, (g - 1) % 2, P * f:P * f + P], ident)
                        there(("ht", g - 1), last)
                    if g < GE:
                        there(("gu", g), gate_up_half(ps_gu, g, 1))
                    if g > 0:
                        w = [v.rearrange("p (f n) -> p f n", f=2) for v in ready(2, g - 1)]
                        pe.wait_ge(*e_read(("ht", g - 1), i))
                        steps = [(f, c) for f in range(2) for c in range(2)]
                        if g == GE:
                            steps = [(f, c) for c in range(2) for f in range(2)]
                        for f, c in steps:
                            h_ = [hT[:, (g - 1) % 2, m, P * f:P * f + P] for m in range(2)]
                            last = three(ybank[c][:, :], h_, [v[:, f, 512 * c:512 * c + 512] for v in w],
                                         g == 1 and f == 0, g == GE and f == 1)
                            if g == GE and (f, c) == (1, 0):
                                last.then_inc(sem("first_columns"), 1)
                        last.then_inc(sem("expert_down_used"), 1)
                    if g == GE // 2:
                        pe.wait_ge(sem("sel_ready"), i + 2)
                        for key, last in gather(i + 1, claim_e):
                            there(key, last)
                for n in range(4):
                    c, t = divmod(n, 2)
                    if t == 0:
                        pe.wait_ge(sem("ye_ready"), 2 * i + (1 + c))
                    ps = claim_e(("y", n))
                    there(("y", n), nc.tensor.matmul(ps[:, :], selT[:, par, P * t:P * t + P],
                                                     ye[:, 512 * c:512 * c + 512], start=True, stop=True))
                pe.wait_ge(*e_read(("gate",), i))
                for h in range(2):
                    pe.wait_ge(*e_read(("x", h), i))
                pe.wait_ge(*e_read(("selT",), i))

            def items(p):
                with pe.Fori(0, NE // 2 - 1) as m:
                    for u in range(2):
                        item(m * 2 + (NE * p + u), u, False)
                item(NE * p + NE - 2, 0, False)
                item(NE * p + NE - 1, 1, True)

            passes(pe, items)

        @block.sync
        def _(sp):
            sp.dma_start(X[:, :, :], x[0].rearrange("(t p) n -> p t n", p=P)).then_inc(sem("x_in"), 16)

            def load(n, parts):
                for off, blocks, width, stride, src in parts:
                    dst = raw[:, n % RAW, :].rearrange("p (k n) -> p k n", n=stride)
                    k0, c0 = divmod(off, stride)
                    sp.dma_start(dst[:, k0:k0 + blocks, c0:c0 + width], src).then_inc(full(n % RAW), 16)

            for n, (key, parts) in enumerate(stream):
                if n >= RAW:
                    sp.wait_ge(sem("split_lo"), n - RAW + 1)
                load(n, parts)

            def expert_parts(kind, e, g):
                if kind == 2:
                    return down_parts(w_down_moe[0][e], g)
                return gate_up_parts(w_gate_moe[0][e], w_up_moe[0][e], kind, g)

            def items(p):
                for kind, g, n in PASS_START:
                    sp.wait_ge(sem("split_lo"), p * NE * PER_ITEM + N0 + n - RAW + 1)
                    load(N0 + n, expert_parts(kind, 0, g))

                def item(i, e, last):
                    for g in range(GE):
                        for kind, gg, n in item_splits(i, g, last):
                            sp.wait_ge(sem("split_lo"), n + (N0 - RAW + 1))
                            off = item_splits(0, g, last)
                            place = N0 + [q for k_, g_, q in off if (k_, g_) == (kind, gg)][0]
                            load(place, expert_parts(kind, e + gg // GE, gg % GE))

                with sp.Fori(0, NE // 2 - 1) as m:
                    for u in range(2):
                        item(m * 2 + (NE * p + u), m * 2 + u, False)
                item(NE * p + NE - 2, NE - 2, False)
                item(NE * p + NE - 1, NE - 1, True)

            passes(sp, items)

            for t in range(T):
                sp.wait_ge(sem("out_ready"), t + 1)
                sp.dma_start(out[0, P * t:P * t + P, :], XN[:, t, :]).then_inc(sem("out_done"), 16)
            sp.wait_ge(sem("out_done"), 16 * T)

        @block.gpsimd
        def _(pool):
            for b in range(BANKS_E):
                pool.sem_inc(sem(f"expert_free{b}"), 1)
            nc.gpsimd.memset(A[0][:, :], 0.0).then_inc(sem("queries_cleared"), 1)
            nc.gpsimd.memset(gate_rows[:, :].bitcast(F32), 0.0).then_inc(sem("gates_cleared"), 1)
            nc.gpsimd.memset(hT[:, :, :, :].bitcast(F32), 0.0).then_inc(sem("gates_cleared"), 1)
            pool.wait_ge(sem("onehot_placed"), 2)
            nc.gpsimd.memset(A[1][:, :], 0.0).then_inc(sem("queries_cleared"), 1)
            pool.wait_ge(sem("gnorm_in"), 16)

            def gated(c):
                for t in range(T):
                    evacuated(pool, (f"g{c}", t))
                    sgv = SG[:, t, 512 * c:512 * c + 512].rearrange("p (h n) -> p h n", h=4)
                    nc.gpsimd.tensor_tensor(sgv, sgv, gnorm[:, :].unsqueeze(1).to_broadcast([P, 4, P]),
                                            ALU.mult).then_inc(sem("gate_ready"), 1)

            for key in (("c", C_ORDER[5], 1), ("c", C_ORDER[6], 0)):
                split_low(pool, key, nc.gpsimd.tensor_tensor, key == ("c", C_ORDER[5], 1))
            gated(0)
            for key in (("c", C_ORDER[6], 1), ("c", C_ORDER[7], 0), ("c", C_ORDER[7], 1), ("oc", 0, 0)):
                split_low(pool, key, nc.gpsimd.tensor_tensor)
            gated(1)
            for key in (("oc", 0, 1), ("oc", 1, 0)):
                split_low(pool, key, nc.gpsimd.tensor_tensor)
            pool.wait_ge(sem("split_lo"), N0)
            for kind, g, n in PASS_START:
                pool.wait_ge(sem("split_hi"), N0 + n + 1)
                high_, low_ = e_split(kind, g)
                nc.gpsimd.tensor_tensor(low_, raw[:, (N0 + n) % RAW, :], high_.bitcast(F32),
                                        ALU.subtract).then_inc(sem("split_lo"), 1)

        @block.scalar
        def _(act):
            act.dma_start(consts[:, :], c_float).then_inc(sem("consts_in"), 16)
            act.dma_start(vec_rows[0:2 * KD, :], norm_mix.rearrange("l (k p) -> (l k) p", p=P)).then_inc(sem("vecs_in"), 16)
            act.dma_start(vec_rows[2 * KD:4 * KD, :], norm_ffn.rearrange("l (k p) -> (l k) p", p=P)).then_inc(sem("vecs_in"), 16)
            act.dma_start(vec_rows[4 * KD:6 * KD, :], lower_bounds.rearrange("l (k p) -> (l k) p", p=P)).then_inc(sem("vecs_in"), 16)
            act.dma_start(wf, w_ab[:, 3072:3072 + NHB].rearrange("(k p) n -> p k n", p=P)).then_inc(sem("wf_in"), 16)
            act.dma_start(pos_i[:, :], positions[0:1, :].partition_broadcast(P)).then_inc(sem("pos_in"), 16)
            act.dma_start(fbias[:, :], fgate_bias[0:1, :].rearrange("a h -> h a")).then_inc(sem("fox_in"), 16)
            act.dma_start(onehot, c_onehot).then_inc(sem("onehot_in"), 16)
            act.dma_start(wr, router[0].rearrange("(k p) n -> p k n", p=P)).then_inc(sem("wr_in"), 16)
            act.dma_start(gnorm[:, :], gnorm_c[0:1, :].partition_broadcast(P)).then_inc(sem("gnorm_in"), 16)
            act.dma_start(gain_row[:, :], norm_ffn[1:2, :].partition_broadcast(P)).then_inc(sem("gain_row_in"), 16)

            def norm(n, *x_ready):
                act.wait_ge(sem("consts_in"), 16)
                nc.scalar.activation(small[:, WARM:WARM + 1], consts[:, C_ONE:C_ONE + 1], ACT.Sqrt)
                for t in range(T):
                    act.wait_ge(*x_ready[t])
                    nc.scalar.activation(XN[:, t, :], X[:, t, :], ACT.Square,
                                         accum_out=small[:, SS + t:SS + t + 1]).then_inc(sem("squares"), 1)
                act.wait_ge(sem("ms_ready"), n + 1)
                nc.scalar.activation(small[:, MS:MS + 2], small[:, MS:MS + 2], ACT.Sqrt).then_inc(sem("rms_ready"), 1)
                act.wait_ge(sem("rs_ready"), n + 1)
                nc.scalar.activation(XN[:, 1, :], X[:, 1, :], ACT.Copy, scale=small[:, RS + 1:RS + 2])\
                    .then_inc(sem("xn_ready"), 1)

            def evacuate_T(name, g):
                for j in range(KD // 2):
                    ps, b = product(act, (name, j))
                    if g is None:
                        nc.scalar.activation(HTH[:, 2 * j:2 * j + 2, :], ps[:, :].rearrange("p (u q) -> p u q", u=2),
                                             ACT.Copy).then_inc(sem("xt_high"), 1)
                    else:
                        for kk in range(2):
                            k = 2 * j + kk
                            last = nc.scalar.activation(HTH[:, k, :], ps[:, 256 * kk:256 * kk + 256], ACT.Copy,
                                                        scale=vec_cols[:, g + k:g + k + 1])
                        last.then_inc(sem("xt_high"), 1)

            def high(*key):
                split_high(act, key)

            norm(0, (sem("x_in"), 16), (sem("x_in"), 16))

            def narrow_high(raw_, arrived):
                act.wait_ge(arrived, 16)
                nc.scalar.activation(narrow[:, 0, :, :], raw_, ACT.Copy).then_inc(sem("narrow_high"), 1)

            narrow_high(wf, sem("wf_in"))
            high("ab", 0, 0)
            evacuated(act, "vecs")
            evacuate_T("mix0", gain["mix0"])
            high("ab", 0, 1)
            high("ab", 1, 0)
            act.wait_ge(sem("onehot_in"), 16)
            act.wait_ge(sem("gates_cleared"), 2)
            for row in (0, 32):
                nc.scalar.activation(gate_cols[row:row + NHB], onehot, ACT.Copy).then_inc(sem("onehot_placed"), 1)

            def copy_T(name, dst, scale, func=ACT.Copy):
                for j in range(2):
                    ps, b = product(act, (name, j))
                    nc.scalar.activation(dst[:, 2 * j:2 * j + 2, :], ps[:, :].rearrange("p (u q) -> p u q", u=2), func,
                                         scale=scale).then_inc(bank_free(b), 1)

            high("ab", 1, 1)
            copy_T("qa", RAW_ROT["qa"], HD ** -0.5)
            high("ab", 2, 0)
            high("ab", 2, 1)
            copy_T("ka", K["a"], 1.0)
            high("ab", 3, 0)
            act.wait_ge(sem("angle_ready"), 1)
            nc.scalar.activation(rope[:, 0:2, :], rope[:, 2:4, :], ACT.Sin).then_inc(sem("trig_ready"), 1)
            act.wait_ge(sem("fox_abs"), 1)
            nc.scalar.activation(fox[:, 3, :], fox[:, 3, :], ACT.Exp, scale=-1.0).then_inc(sem("fox_exp"), 1)
            act.wait_ge(sem("fox_exp"), 1)
            nc.scalar.activation(fox[:, 3, :], fox[:, 3, :], ACT.Ln, bias=1.0).then_inc(sem("fox_ln"), 1)
            high("ab", 3, 1)
            high("ab", 4, 0)

            high("ab", 4, 1)
            act.wait_ge(sem("queries_cleared"), 2)
            for j in range(2):
                ps, b = product(act, ("qb", j))
                both = ps[:, :].rearrange("p (u q) -> p u q", u=2)
                nc.scalar.activation(Q["b"][0:HD, 2 * j:2 * j + 2, 0, :], both[0:HD], ACT.Copy, scale=HD ** -0.5)
                nc.scalar.activation(Q["b"][HD:P, 2 * j:2 * j + 2, 1, :], both[HD:P], ACT.Copy, scale=HD ** -0.5)\
                    .then_inc(bank_free(b), 1)

            def beside_head(i):
                if i in (0, 3):
                    high("ab", 5, i // 3)
                if i == 5:
                    copy_T("kb", K["b"], 1.0)
                if i in (6, 8, 10):
                    high("oab", *((0, 0), (0, 1), (1, 0))[(i - 6) // 2])

            def head_pair_out(pair):
                ps, b = product(act, ("o", pair))
                if pair < len(PARKED):
                    nc.scalar.activation(PARKED[pair], ps[:, 0:SEQ], ACT.Copy).then_inc(bank_free(b), 1)
                    return
                if pair == len(PARKED):
                    act.wait_ge(*done_at[("ab", 5, 1)])
                    for early in range(pair):
                        evacuated(act, ("o", early))
                        nc.scalar.activation(HTH[:, early, :], PARKED[early], ACT.Copy).then_inc(sem("out_high"), 1)
                nc.scalar.activation(HTH[:, pair, :], ps[:, 0:SEQ], ACT.Copy).then_inc(sem("out_high"), 1)

            for i in range(NH + 5):
                if i < NH:
                    h = i
                    act.wait_ge(sem("max_ready"), h + 1)
                    for t in range(T):
                        s_ = S[h % SRING][:, P * t:P * t + P * (t + 1)]
                        nc.scalar.activation(s_, s_, ACT.Exp, bias=small[:, MX + 2 * h + t:MX + 2 * h + t + 1],
                                             accum_out=small[:, SM + 2 * h + t:SM + 2 * h + t + 1])\
                            .then_inc(sem("exp_ready"), 1)
                if i >= 5 and i % 2 == 1:
                    head_pair_out((i - 5) // 2)
                if 2 <= i < NH + 2:
                    h = i - 2
                    if h >= 3:
                        if h % 2:
                            act.wait_ge(sem("even_values"), (h - 3) // 2 + 1)
                        else:
                            act.wait_ge(*product_of(("o", (h - 3) // 2)))
                    ps, b = product(act, ("p", h))
                    nc.scalar.activation(PT[h % 3], ps[:, 0:3 * P], ACT.Copy).then_inc(bank_free(b), 1)
                beside_head(i)

            act.dma_start(level_words, c_level).then_inc(sem("level_in"), 16)
            act.wait_ge(*product_of("flogit"))
            narrow_high(wr, sem("wr_in"))
            high("oab", 1, 1)
            high("ff", 0, 0)
            high("ff", 0, 1)
            norm(1, (sem("acc_free"), 3), (sem("acc_free"), 4))
            evacuate_T("ffn0", gain["ffn0"])
            for g in range(FG + 1):
                if g > 0:
                    ps, b = product(act, ("ht", g - 1))
                    nc.scalar.activation(hT[:, (g - 1) % 2, 0, :], ps[:, :], ACT.Copy).then_inc(sem("hT_high"), 1)
                if g < FG - 1:
                    high("ff", g + 1, 0)
                elif g == FG - 1:
                    high("c", C_ORDER[0], 0)
                if g < FG:
                    for t in range(T):
                        ps, b = product(act, ("gu", g, t))
                        nc.scalar.activation(hbuf[:, g % 2, 256 * t:256 * t + 256], ps[:, 0:256], ACT.Silu)\
                            .then_inc(sem("silu_ready"), 1)
                    if g < FG - 1:
                        high("ff", g + 1, 1)
                    else:
                        high("c", C_ORDER[0], 1)
                    high("ff", g, 2)

            high("c", C_ORDER[1], 0)
            norm(2, (sem("acc_free"), 6), (sem("acc_free"), 8))
            act.wait_ge(sem("lb_max"), 1)
            nc.scalar.activation(small[:, LBC:LBC + 16], small[:, LBC:LBC + 16], ACT.Exp).then_inc(sem("lb_exp"), 1)
            evacuate_T("mix1", gain["mix1"])
            high("c", C_ORDER[1], 1)
            copy_T("f0", BC[:, 0:4, :], 1.0, ACT.Sigmoid)
            high("c", C_ORDER[2], 0)
            high("c", C_ORDER[2], 1)
            copy_T("f1", BC[:, 4:8, :], 1.0, ACT.Sigmoid)
            high("c", C_ORDER[3], 0)
            high("c", C_ORDER[3], 1)
            copy_T("q0", QC[:, 0:4, :], P ** -0.5)
            high("c", C_ORDER[4], 0)
            act.wait_ge(sem("f_ready"), 1)
            nc.scalar.activation(BC[:, :, :], BC[:, :, :], ACT.Ln).then_inc(sem("logf_ready"), 1)
            high("c", C_ORDER[4], 1)
            copy_T("q1", QC[:, 4:8, :], P ** -0.5)
            high("c", C_ORDER[5], 0)

            def gates(c):
                for t in range(T):
                    ps, b = product(act, (f"g{c}", t))
                    nc.scalar.activation(SG[:, t, 512 * c:512 * c + 512], ps[:, :], ACT.Silu).then_inc(bank_free(b), 1)

            def beside_level(step):
                chunk = {1: (C_ORDER[5], 1), 3: (C_ORDER[6], 0), 5: (C_ORDER[6], 1), 6: (C_ORDER[7], 0), 8: (C_ORDER[7], 1)}
                if step in chunk:
                    high("c", *chunk[step])
                if step in (11, 13, 15):
                    high("oc", *((0, 0), (0, 1), (1, 0))[(step - 11) // 2])
                if step in (4, 12):
                    gates(step // 12)

            def copy_heads(half):
                for t in range(T):
                    ps, b = product(act, ("hgrn_o", half, t))
                    nc.scalar.activation(XN[:, t, 512 * half:512 * half + 512], ps[:, :], ACT.Copy).then_inc(bank_free(b), 1)

            def head_roots(half):
                head_ms = small[:, MX + 8 * half:MX + 8 * half + 8]
                act.wait_ge(sem("head_ms"), half + 1)
                nc.scalar.activation(head_ms, head_ms, ACT.Sqrt).then_inc(sem("head_rms"), 1)

            for half in range(2):
                for n in range(1, NLV + 1):
                    act.wait_ge(sem("delta_ready"), half * NLV + n)
                    if n >= 3:
                        act.wait_ge(*done_at[("level", half, n - 2)])
                    elif half == 1:
                        act.wait_ge(*done_at[("level", 0, NLV - (1 if (NLV - n) % 2 else 0))])
                    for r in range(2):
                        width = P if n == 1 else LEVELS[n - 2]
                        dst, src = (v.rearrange("p h (m side z) -> p (h m) side z", side=2, z=width)[:, :, r, :]
                                    for v in (LV[:, n % 2], DL))
                        last = nc.scalar.activation(dst, src, ACT.Exp, scale=(-1.0, 1.0)[r])
                    last.then_inc(sem("decay_ready"), 1)
                    if half == n == 1:
                        beside_level(NLV + 1)
                        copy_heads(0)
                    beside_level(half * (NLV + 1) + n)
                if half == 1:
                    head_roots(0)
                    copy_heads(1)
            head_roots(1)
            evacuate_T("hgrn_out", None)

            high("oc", 1, 1)

            def high_e(kind, g, slot, value, arrived, free_wait):
                act.wait_ge(full(slot), arrived)
                act.wait_ge(*free_wait)
                nc.scalar.activation(e_split(kind, g)[0], raw[:, slot, :], ACT.Copy).then_inc(sem("split_hi"), 1)

            def raw_place(n0, i):
                n = N0 + n0
                return n % RAW, i * (32 * PER_ITEM // RAW) + 32 * (n // RAW + 1)

            def pass_start(p, which):
                for kind, g, n in which:
                    slot, arrived = raw_place(n, NE * p)
                    if p == 0 and g == 0:
                        wait = done_at[("oc", (kind + 1) // 2, (kind + 1) % 2)]
                    elif p == 0:
                        wait = (sem("acc_full"), 8)
                    elif kind == 0:
                        wait = (sem("expert_half_used"), GE * NE * p + g - 1)
                    elif kind == 1:
                        wait = e_full(("gu", GE - 2 + g), NE * p - 1)
                    else:
                        wait = (sem("expert_down_used"), GE * NE * p + g - 1)
                    high_e(kind, g, slot, None, arrived, wait)

            norm(3, (sem("acc_free"), 11), (sem("acc_free"), 12))
            pass_start(0, PASS_START[0:1])
            evacuate_T("ffn1", gain["ffn1"])
            pass_start(0, PASS_START[1:])
            act.wait_ge(sem("top_gap"), 1)
            nc.scalar.activation(route[:, :, 32:33], route[:, :, 32:33], ACT.Exp).then_inc(sem("gap_exp"), 1)

            def place_x(par, wait):
                for h in range(2):
                    ps = wait(("x", h))
                    nc.scalar.activation(XE[:, par, 0, 4 * h:4 * h + 4, :], ps[:, :].rearrange("p (k q) -> p k q", k=4),
                                         ACT.Copy).then_inc(sem("xe_high"), 1)
                ps = wait(("selT",))
                return nc.scalar.activation(selT[:, par, :], ps[:, 0:T * P], ACT.Copy)

            b = work.where[("first", "selT")][0]
            place_x(0, lambda key: product(act, ("first",) + key)[0]).then_inc(bank_free(b), 1)

            def item(i, par, last):
                def there(key):
                    act.wait_ge(*e_full(key, i))
                    return ebank[item_at[key] % BANKS_E]

                def split_step(g, which):
                    for (kind, gg, n), (_, _, n0) in zip(item_splits(i, g, last), item_splits(0, g, last)):
                        if kind not in which:
                            continue
                        slot, arrived = raw_place(n0, i)
                        if kind == 0:
                            wait = (sem("expert_half_used"), i * GE + (gg - 2 + 1))
                        elif kind == 1:
                            wait = e_full(("gu", gg - 2), i)
                        elif gg >= 2:
                            wait = (sem("expert_down_used"), i * GE + (gg - 2 + 1))
                        else:
                            wait = (sem("expert_half_used"), i * GE + 1)
                        high_e(kind, gg, slot, None, arrived, wait)

                for g in range(GE + 1):
                    if g > 0:
                        nc_ = there(("ht", g - 1))
                        nc.scalar.activation(hT[:, (g - 1) % 2, 0, 0:256], nc_[:, 0:256], ACT.Copy)\
                            .then_inc(sem("hT_high"), 1)
                        split_step(g - 1, (2,))
                    if g == GE // 2 + 1:
                        place_x(1 - par, there).then_inc(e_read(("selT",), i)[0], 1)
                    if g < GE:
                        split_step(g, (0,))
                        ps = there(("gu", g))
                        nc.scalar.activation(hexp[:, g % 2, :], ps[:, 0:256], ACT.Silu).then_inc(sem("silu_ready"), 1)
                        split_step(g, (1,))
                for c in range(2):
                    if c == 0:
                        act.wait_ge(sem("first_columns"), i + 1)
                    else:
                        act.wait_ge(sem("expert_down_used"), i * GE + GE)
                    nc.scalar.activation(ye[:, 512 * c:512 * c + 512], ybank[c][:, :], ACT.Copy,
                                         scale=slot_gate[:, par:par + 1]).then_inc(sem("ye_ready"), 1)

            def items(p):
                if p:
                    pass_start(p, PASS_START)
                with act.Fori(0, NE // 2 - 1) as m:
                    for u in range(2):
                        item(m * 2 + (NE * p + u), u, False)
                item(NE * p + NE - 2, 0, False)
                item(NE * p + NE - 1, 1, True)

            passes(act, items)
            act.dma_start(gain_row[:, :], norm_final.rearrange("(a n) -> a n", a=1).partition_broadcast(P)).then_inc(sem("final_in"), 16)
            norm(4, (sem("x_final"), 1), (sem("x_final"), 1))


        @block.vector
        def _(dve):
            count = [0]

            def link(ins):
                count[0] += 1
                ins.then_inc(sem("dve_chain"), 1)
                dve.wait_ge(sem("dve_chain"), count[0])

            def norm(n):
                dve.wait_ge(sem("squares"), 2 * n + 2)
                nc.vector.tensor_scalar(small[:, MS:MS + 2], small[:, SS:SS + 2], 1.0 / D, EPS, ALU.mult, ALU.add)\
                    .then_inc(sem("ms_ready"), 1)
                dve.wait_ge(sem("rms_ready"), n + 1)
                nc.vector.reciprocal(small[:, RS:RS + 2], small[:, MS:MS + 2]).then_inc(sem("rs_ready"), 1)
                dve.wait_ge(sem("rs_ready"), n + 1)
                nc.vector.tensor_scalar(XN[:, 0, :], X[:, 0, :], small[:, RS:RS + 1], None, ALU.mult)\
                    .then_inc(sem("xn_ready"), 1)

            highs = [0]

            def evacuate_T(name, g):
                for j in range(KD // 2):
                    b, _ = work.where[(name, j)]
                    ps = psum[b]
                    highs[0] += 1
                    dve.wait_ge(sem("xt_high"), highs[0])
                    if g is None:
                        last = nc.vector.tensor_tensor(HTL[:, 2 * j:2 * j + 2, :], ps[:, :].rearrange("p (u q) -> p u q", u=2),
                                                       HTH[:, 2 * j:2 * j + 2, :].bitcast(F32), ALU.subtract)
                    else:
                        for kk in range(2):
                            k = 2 * j + kk
                            last = nc.vector.scalar_tensor_tensor(HTL[:, k, :], ps[:, 256 * kk:256 * kk + 256],
                                                                  vec_cols[:, g + k:g + k + 1], HTH[:, k, :].bitcast(F32),
                                                                  ALU.mult, ALU.subtract)
                    last.then_inc(bank_free(b), 1)

            def low(*key):
                split_low(dve, key, nc.vector.tensor_tensor, key == ("oc", 1, 1))

            def residual(waits, by_tile=False):
                for n in range(4):
                    c, t = divmod(n, 2)
                    if by_tile:
                        t, c = c, t
                    dve.wait_ge(*waits[n])
                    xs = X[:, t, 512 * c:512 * c + 512]
                    nc.vector.tensor_tensor(xs, xs, acc[2 * t + c][:, :], ALU.add).then_inc(sem("acc_free"), 1)

            ps, b = product(dve, "vecs")
            nc.vector.tensor_copy(vec_cols[:, :], ps[:, 0:6 * KD]).then_inc(bank_free(b), 1)
            norm(0)

            def narrow_low(raw_, use):
                dve.wait_ge(sem("narrow_high"), use)
                nc.vector.tensor_tensor(narrow[:, 1, :, :], raw_, narrow[:, 0, :, :].bitcast(F32),
                                        ALU.subtract).then_inc(sem("narrow_low"), 1)

            narrow_low(wf, 1)
            low("ab", 0, 0)
            evacuated(dve, "vecs")
            evacuate_T("mix0", gain["mix0"])
            low("ab", 0, 1)
            low("ab", 1, 0)

            two_pi = 2.0 * np.pi
            C1 = 6.28125
            C2 = float(np.float32(two_pi - C1))
            C3 = float(two_pi - C1 - C2)
            ROUND = 12582912.0
            PI_IN = float(np.nextafter(np.float32(np.pi), np.float32(0)))
            dve.wait_ge(sem("pos_in"), 16)
            dve.wait_ge(sem("consts_in"), 16)
            link(nc.vector.tensor_copy(rope[:, 4, :], pos_i[:, :]))
            link(nc.vector.tensor_scalar(rope[:, 4, :], rope[:, 4, :], consts[:, C_FREQ:C_FREQ + 1], None, ALU.mult))
            link(nc.vector.tensor_scalar(rope[:, 5, :], rope[:, 4, :], 1.0 / two_pi, ROUND, ALU.mult, ALU.add))
            link(nc.vector.tensor_scalar(rope[:, 5, :], rope[:, 5, :], ROUND, None, ALU.subtract))
            for part in (C1, C2, C3):
                link(nc.vector.scalar_tensor_tensor(rope[:, 4, :], rope[:, 5, :], -part, rope[:, 4, :], ALU.mult, ALU.add))
            link(nc.vector.tensor_scalar(rope[:, 3, :], rope[:, 4, :], PI_IN, -PI_IN, ALU.min, ALU.max))
            link(nc.vector.tensor_scalar(rope[:, 2, :], rope[:, 4, :], np.pi / 2, None, ALU.add))
            link(nc.vector.tensor_scalar(rope[:, 5, :], rope[:, 2, :], np.pi, -two_pi, ALU.is_gt, ALU.mult))
            link(nc.vector.tensor_tensor(rope[:, 2, :], rope[:, 2, :], rope[:, 5, :], ALU.add))
            nc.vector.tensor_scalar(rope[:, 2, :], rope[:, 2, :], PI_IN, -PI_IN, ALU.min, ALU.max)\
                .then_inc(sem("angle_ready"), 1)

            dve.wait_ge(sem("fox_in"), 16)
            ps, b = product(dve, "flogit")
            nc.vector.tensor_scalar(fox[:, 2, :], ps[0:NHB, 0:SEQ], fbias[:, 0:1], None, ALU.add).then_inc(bank_free(b), 1)
            evacuated(dve, "flogit")
            nc.vector.scalar_tensor_tensor(fox[:, 3, :], fox[:, 2, :], -1.0, fox[:, 2, :], ALU.mult, ALU.max)\
                .then_inc(sem("fox_abs"), 1)
            link(nc.vector.tensor_scalar(fox[:, 2, :], fox[:, 2, :], 0.0, None, ALU.min))
            link(nc.vector.memset(fox[:, 4, :], 1.0))

            def rotate(name, n):
                for jj in range(2):
                    ps, b = product(dve, ("rot", name, jj))
                    raw_ = RAW_ROT[name][:, 2 * jj:2 * jj + 2, :]
                    rt = rtmp.rearrange("p (u q) -> p u q", u=2)
                    if n == jj == 0:
                        dve.wait_ge(sem("trig_ready"), 1)
                    link(nc.vector.tensor_tensor(raw_, raw_, cosT.unsqueeze(1).to_broadcast([P, 2, SEQ]), ALU.mult))
                    nc.vector.tensor_tensor(rt, ps[:, :].rearrange("p (u q) -> p u q", u=2),
                                            sinT.unsqueeze(1).to_broadcast([P, 2, SEQ]), ALU.mult).then_inc(bank_free(b), 1)
                    evacuated(dve, ("rot", name, jj))
                    if name == "qa":
                        if jj == 0:
                            dve.wait_ge(sem("queries_cleared"), 1)
                        for u in range(2):
                            rows = slice(HD * u, HD * u + HD)
                            last = nc.vector.tensor_tensor(Q["a"][rows, 2 * jj:2 * jj + 2, u, :], raw_[rows], rt[rows], ALU.add)
                    else:
                        last = nc.vector.tensor_tensor(raw_, raw_, rt, ALU.add)
                    last.then_inc(sem("rope_ready"), 1)
                    dve.wait_ge(sem("rope_ready"), 2 * n + jj + 1)

            def copy_tokens(name, dst, c0):
                for t in range(T):
                    ps, b = product(dve, (name, t))
                    nc.vector.tensor_copy(dst[:, t, c0:c0 + 512], ps[:, :]).then_inc(bank_free(b), 1)

            low("ab", 1, 1)
            low("ab", 2, 0)
            low("ab", 2, 1)
            low("ab", 3, 0)
            copy_tokens("va", V, 0)
            rotate("qa", 0)
            rotate("ka", 1)
            low("ab", 3, 1)
            low("ab", 4, 0)
            dve.wait_ge(sem("fox_ln"), 1)
            dve.wait_ge(sem("onehot_placed"), 2)
            link(nc.vector.tensor_tensor(fox[:, 2, :], fox[:, 2, :], fox[:, 3, :], ALU.subtract))
            link(nc.vector.tensor_tensor_scan(fox[:, 0, :], fox[:, 4, :], fox[:, 2, :], 0.0, ALU.mult, ALU.add))
            link(nc.vector.tensor_copy(gate_rows[0:NHB, :], fox[:, 0, :]))
            link(nc.vector.tensor_tensor(gate_rows[32:32 + NHB, :], fox[:, 0, :], gate_rows[0:NHB, :].bitcast(F32), ALU.subtract))
            link(nc.vector.tensor_scalar(fox[:, 1, :], gate_rows[0:NHB, :].bitcast(F32), -1.0, None, ALU.mult))
            link(nc.vector.tensor_scalar(fox[:, 5, :], gate_rows[32:32 + NHB, :].bitcast(F32), -1.0, None, ALU.mult))
            for row, part in ((64, 1), (96, 5)):
                nc.vector.tensor_copy(gate_rows[row:row + NHB, :], fox[:, 4, :])
                last = nc.vector.tensor_tensor(gate_cols[row:row + NHB], gate_cols[0:NHB].bitcast(F32),
                                               fox[:, part, :].unsqueeze(1).to_broadcast([NHB, NHB, SEQ]), ALU.mult)
            last.then_inc(sem("fox_ready"), 1)
            low("ab", 4, 1)

            def beside_head(i):
                if i in (0, 3):
                    low("ab", 5, i // 3)
                if i in (6, 8, 10):
                    low("oab", *((0, 0), (0, 1), (1, 0))[(i - 6) // 2])
                if i == 9:
                    copy_tokens("vb", V, 512)

            for i in range(NH + 5):
                if i < NH:
                    h = i
                    if h >= SRING:
                        dve.wait_ge(bank_full(work.where[("p", h - SRING)][0]), work.where[("p", h - SRING)][1])
                    ps, b = product(dve, ("s", h))
                    m = score_mask["a" if h < NHA else "b"]
                    for t in range(T):
                        at = slice(P * t, P * t + P * (t + 1))
                        last = nc.vector.tensor_tensor_reduce(
                            out=S[h % SRING][:, at], in0=ps[:, at], in1=m[:, at], scale=1.0, scalar=-3.0e38,
                            op0=ALU.add, op1=ALU.max, accum_out=small[:, MX + 2 * h + t:MX + 2 * h + t + 1])
                    last.then_inc(bank_free(b), 1)
                    evacuated(dve, ("s", h))
                    nc.vector.tensor_scalar(small[:, MX + 2 * h:MX + 2 * h + 2], small[:, MX + 2 * h:MX + 2 * h + 2],
                                            -1.0, None, ALU.mult).then_inc(sem("max_ready"), 1)
                if 1 <= i <= NH:
                    h = i - 1
                    dve.wait_ge(sem("exp_ready"), 2 * h + 2)
                    link(nc.vector.reciprocal(small[:, RI + 2 * h:RI + 2 * h + 2], small[:, SM + 2 * h:SM + 2 * h + 2]))
                    for t in range(T):
                        s_ = S[h % SRING][:, P * t:P * t + P * (t + 1)]
                        last = nc.vector.tensor_scalar(s_, s_, small[:, RI + 2 * h + t:RI + 2 * h + t + 1], None, ALU.mult)
                    last.then_inc(sem("probs_ready"), 1)
                if i >= 5 + 2 * len(PARKED) and i % 2 == 1:
                    pair = (i - 5) // 2
                    b = work.where[("o", pair)][0]
                    for early in range(len(PARKED) if pair == len(PARKED) else 0):
                        dve.wait_ge(sem("out_high"), early + 1)
                        nc.vector.tensor_tensor(HTL[:, early, :], PARKED[early], HTH[:, early, :].bitcast(F32), ALU.subtract)
                    dve.wait_ge(sem("out_high"), pair + 1)
                    nc.vector.tensor_tensor(HTL[:, pair, :], psum[b][:, 0:SEQ], HTH[:, pair, :].bitcast(F32),
                                            ALU.subtract).then_inc(bank_free(b), 1)
                beside_head(i)

            low("oab", 1, 1)
            low("ff", 0, 0)
            narrow_low(wr, 2)
            dve.wait_ge(sem("level_in"), 16)
            nc.vector.tensor_copy(level_mask[:, :, :], level_words).then_inc(sem("level_masks"), 1)
            residual([(sem("acc_full"), n + 1) for n in range(4)])
            low("ff", 0, 1)
            norm(1)
            evacuate_T("ffn0", gain["ffn0"])
            for g in range(FG + 1):
                if g > 0:
                    b, _ = work.where[("ht", g - 1)]
                    dve.wait_ge(sem("hT_high"), g)
                    nc.vector.tensor_tensor(hT[:, (g - 1) % 2, 1, :], psum[b][:, :],
                                            hT[:, (g - 1) % 2, 0, :].bitcast(F32), ALU.subtract).then_inc(bank_free(b), 1)
                if g < FG - 1:
                    low("ff", g + 1, 0)
                elif g == FG - 1:
                    low("c", C_ORDER[0], 0)
                if g < FG:
                    for t in range(T):
                        b, _ = work.where[("gu", g, t)]
                        dve.wait_ge(sem("silu_ready"), 2 * g + t + 1)
                        ht_ = hbuf[:, g % 2, 256 * t:256 * t + 256]
                        nc.vector.tensor_tensor(ht_, ht_, psum[b][:, 256:512], ALU.mult).then_inc(bank_free(b), 1)
                    if g < FG - 1:
                        low("ff", g + 1, 1)
                    else:
                        low("c", C_ORDER[0], 1)
                    low("ff", g, 2)
            residual([(sem("ffn_sums"), n + 1) for n in range(3)] + [(sem("down_used"), FG)], by_tile=True)
            low("c", C_ORDER[1], 0)

            l0, l1 = vec_cols[:, 4 * KD:5 * KD], vec_cols[:, 5 * KD:6 * KD]
            lb, oml = small[:, LBC:LBC + 8], small[:, OML:OML + 8]
            link(nc.vector.tensor_tensor(small[:, 120:128], l0, l1, ALU.max))
            link(nc.vector.tensor_tensor(lb, l1, small[:, 120:128], ALU.subtract))
            nc.vector.tensor_tensor(oml, l0, small[:, 120:128], ALU.subtract).then_inc(sem("lb_max"), 1)
            norm(2)
            dve.wait_ge(sem("lb_exp"), 1)
            link(nc.vector.tensor_tensor(oml, oml, lb, ALU.add))
            link(nc.vector.reciprocal(oml, oml))
            link(nc.vector.tensor_tensor(lb, lb, oml, ALU.mult))
            link(nc.vector.tensor_scalar(oml, lb, -1.0, 1.0, ALU.mult, ALU.add))
            evacuate_T("mix1", gain["mix1"])
            low("c", C_ORDER[1], 1)
            low("c", C_ORDER[2], 0)
            low("c", C_ORDER[2], 1)
            low("c", C_ORDER[3], 0)
            for c in range(2):
                for jj in range(2):
                    evacuated(dve, (f"f{c}", jj))
            for h in range(NHC):
                last = nc.vector.tensor_scalar(BC[:, h, :], BC[:, h, :], oml[:, h:h + 1], lb[:, h:h + 1], ALU.mult, ALU.add)
            link(last)
            nc.vector.tensor_scalar(KC[:, :, :], BC[:, :, :], -1.0, 1.0, ALU.mult, ALU.add).then_inc(sem("kc_ready"), 1)
            dve.wait_ge(sem("kc_ready"), 1)
            nc.vector.tensor_scalar(BC[:, :, :], BC[:, :, :], 2.0 ** -63, None, ALU.max).then_inc(sem("f_ready"), 1)
            low("c", C_ORDER[3], 1)
            low("c", C_ORDER[4], 0)
            low("c", C_ORDER[4], 1)
            low("c", C_ORDER[5], 0)
            copy_tokens("v0", VC, 0)
            dve.wait_ge(sem("logf_ready"), 1)
            for h in range(NHC):
                last = nc.vector.tensor_tensor_scan(BC[:, h, :], consts[:, C_RST:C_RST + SEQ], BC[:, h, :], 0.0,
                                                    ALU.mult, ALU.add)
            link(last)

            def delta(half, n):
                bh = BC[:, 4 * half:4 * half + 4, :]
                if n == 1:
                    ends = [bh[:, :, CHUNK * c + CHUNK - 1:CHUNK * c + CHUNK] for c in range(4)]
                    wide = [P, 4, CHUNK]
                    d = [DL[:, :, CHUNK * c:CHUNK * c + CHUNK] for c in range(4)]
                    s4 = [bh[:, :, CHUNK * c:CHUNK * c + CHUNK] for c in range(4)]
                    nc.vector.tensor_tensor(d[1], s4[1], ends[1].to_broadcast(wide), ALU.subtract)
                    link(nc.vector.tensor_tensor(d[0], s4[0], ends[0].to_broadcast(wide), ALU.subtract))
                    nc.vector.tensor_tensor(d[0], d[0], ends[1].to_broadcast(wide), ALU.subtract)
                    nc.vector.tensor_copy(d[2], s4[2])
                    last = nc.vector.tensor_tensor(d[3], s4[3], ends[2].to_broadcast(wide), ALU.add)
                elif LEVELS[n - 2] == CHUNK:
                    v, dv = (u.rearrange("p h (m side z) -> p (h m) side z", side=2, z=CHUNK) for u in (bh, DL))
                    nc.vector.tensor_tensor(dv[:, :, 0, :], v[:, :, 0, :],
                                            v[:, :, 0, CHUNK - 1:CHUNK].to_broadcast([P, 8, CHUNK]), ALU.subtract)
                    last = nc.vector.tensor_copy(dv[:, :, 1, :], v[:, :, 1, :])
                else:
                    width = LEVELS[n - 2]
                    v, dv = (u.rearrange("p h (m z) -> p (h m) z", z=2 * width) for u in (bh, DL))
                    last = nc.vector.tensor_tensor(dv, v, v[:, :, width - 1:width].to_broadcast([P, 4 * SEQ // (2 * width), 2 * width]),
                                                   ALU.subtract)
                last.then_inc(sem("delta_ready"), 1)

            def scale_operands(half, n):
                width = P if n == 1 else LEVELS[n - 2]
                for r, src in enumerate((KC, QC)):
                    dst, sv = (v.rearrange("p h (m side z) -> p (h m) side z", side=2, z=width)[:, :, r, :]
                               for v in (LV[:, n % 2], src[:, 4 * half:4 * half + 4, :]))
                    last = nc.vector.tensor_tensor(dst, dst, sv, ALU.mult)
                last.then_inc(sem("level_ready"), 1)

            def beside_level(step):
                if step == 8:
                    copy_tokens("v1", VC, 512)

            def select(half, n):
                if n == 1:
                    ps, b = product(dve, ("lv", half, 1, 0))
                    nc.vector.tensor_copy(AX_, ps[:, :].rearrange("p (h q) -> p h q", h=4)).then_inc(bank_free(b), 1)
                    return
                for g in range(2):
                    ps, b = product(dve, ("lv", half, n, g))
                    dst = AT[:, 2 * g:2 * g + 2].rearrange("p h t q -> p (h t) q")
                    pv = ps[:, :].rearrange("p (h q) -> p h q", h=4)
                    if n == 0:
                        last = nc.vector.tensor_tensor(dst, pv, consts[:, C_ID:C_ID + P].unsqueeze(1)
                                                       .to_broadcast([P, 4, P]), ALU.mult)
                    else:
                        last = nc.vector.copy_predicated(dst, level_mask[:, n - 2, :].unsqueeze(1)
                                                         .to_broadcast([P, 4, P]), pv)
                    last.then_inc(bank_free(b), 1)
                evacuated(dve, ("lv", half, n, 1))

            def head_of(half, t, i):
                return XN[:, t, 512 * half + P * i:512 * half + P * i + P]


            def head_squares(half):
                for t in range(T):
                    evacuated(dve, ("hgrn_o", half, t))
                    for i in range(4):
                        o = head_of(half, t, i)
                        last = nc.vector.tensor_tensor_reduce(
                            out=XN[:, 0, 512 + P * i:640 + P * i] if half == 0 else DL[:, i, P * t:P * t + P], in0=o, in1=o, scale=1.0, scalar=0.0,
                            op0=ALU.mult, op1=ALU.add, accum_out=small[:, MX + 8 * half + 4 * t + i:MX + 8 * half + 4 * t + i + 1])
                    link(last)
                hm = small[:, MX + 8 * half:MX + 8 * half + 8]
                nc.vector.tensor_scalar(hm, hm, 1.0 / P, EPS, ALU.mult, ALU.add).then_inc(sem("head_ms"), 1)

            def head_scale(half):
                dve.wait_ge(sem("head_rms"), half + 1)
                hm = small[:, MX + 8 * half:MX + 8 * half + 8]
                link(nc.vector.reciprocal(hm, hm))
                dve.wait_ge(sem("gate_ready"), 2 * half + 2)
                for t in range(T):
                    for i in range(4):
                        last = nc.vector.scalar_tensor_tensor(
                            head_of(half, t, i), head_of(half, t, i),
                            small[:, MX + 8 * half + 4 * t + i:MX + 8 * half + 4 * t + i + 1],
                            SG[:, t, 512 * half + P * i:512 * half + P * i + P], ALU.mult, ALU.mult)
                last.then_inc(sem("hgrn_ready"), 1)

            dve.wait_ge(sem("level_masks"), 1)
            for half in range(2):
                for jj in range(2):
                    evacuated(dve, (f"q{half}", jj))
            delta(0, 1)
            for half in range(2):
                for n in range(1, NLV + 1):
                    dve.wait_ge(sem("decay_ready"), half * NLV + n)
                    if n < NLV:
                        delta(half, n + 1)
                    elif half == 0:
                        delta(1, 1)
                    scale_operands(half, n)
                    if half == 0 and n == NLV:
                        select(0, n - 1)
                        select(0, NLV)
                    elif n > 1 or half == 0:
                        select(half, n - 1)
                    else:
                        dve.wait_ge(*done_at[("at", 0)])
                        select(1, 0)
                    beside_level(half * (NLV + 1) + n)
                    if half == 1 and n == 3:
                        head_squares(0)
            select(1, NLV)
            head_scale(0)
            head_squares(1)
            head_scale(1)
            evacuate_T("hgrn_out", None)
            low("oc", 1, 1)
            residual([(sem("acc_full"), n + 5) for n in range(4)])

            def low_e(kind, g, slot, value):
                dve.wait_ge(sem("split_hi"), value)
                high_, low_ = e_split(kind, g)
                nc.vector.tensor_tensor(low_, raw[:, slot, :], high_.bitcast(F32), ALU.subtract).then_inc(sem("split_lo"), 1)

            def pass_start(p, which):
                for kind, g, n in which:
                    low_e(kind, g, (N0 + n) % RAW, p * NE * PER_ITEM + N0 + n + 1)

            norm(3)
            evacuate_T("ffn1", gain["ffn1"])
            dve.wait_ge(sem("gain_row_in"), 16)
            dve.wait_ge(sem("xn_ready"), 8)
            dve.wait_ge(*product_of(("ffn1", KD // 2 - 1)))
            nc.vector.tensor_tensor(XN[:, :, :], XN[:, :, :], gain_row[:, :].unsqueeze(1).to_broadcast([P, T, D]),
                                    ALU.mult).then_inc(sem("xg_ready"), 1)
            ps, b = product(dve, "router_T")
            nc.vector.tensor_copy(logits, ps[0:NE, 0:SEQ]).then_inc(bank_free(b), 1)

            ps, b = product(dve, "router")
            nc.vector.tensor_copy(route[:, :, 0:NE], ps[:, 0:2 * NE].rearrange("p (t e) -> p t e", t=T)).then_inc(bank_free(b), 1)
            evacuated(dve, "router")
            for t in range(T):
                link(nc.vector.max(route[:, t, 8:16], route[:, t, 0:NE]))
                link(nc.vector.max_index(route[:, t, 16:24].bitcast(U32), route[:, t, 8:16], route[:, t, 0:NE]))
            link(nc.vector.tensor_copy(route[:, :, 24:32], route[:, :, 16:24].bitcast(U32)))
            nc.vector.tensor_tensor(route[:, :, 32:33], route[:, :, 9:10], route[:, :, 8:9], ALU.subtract)\
                .then_inc(sem("top_gap"), 1)
            dve.wait_ge(sem("gap_exp"), 1)
            link(nc.vector.tensor_scalar(route[:, :, 33:34], route[:, :, 32:33], 1.0, None, ALU.add))
            link(nc.vector.reciprocal(route[:, :, 34:35], route[:, :, 33:34]))
            link(nc.vector.tensor_tensor(route[:, :, 35:36], route[:, :, 32:33], route[:, :, 34:35], ALU.mult))
            iota = consts[:, C_IOTA:C_IOTA + NE]
            for t in range(T):
                nc.vector.tensor_scalar(route[:, t, 40:48], iota, route[:, t, 24:25], None, ALU.is_equal)
                link(nc.vector.tensor_scalar(route[:, t, 48:56], iota, route[:, t, 25:26], None, ALU.is_equal))
            nc.vector.tensor_tensor(route[:, :, 56:64], route[:, :, 40:48], route[:, :, 48:56], ALU.add)\
                .then_inc(sem("chosen_ready"), 1)
            link(nc.vector.memset(rank_of[:, :, :], -1.0))
            link(nc.vector.memset(combine[:, :, :], 0.0))
            for t in range(T):
                link(nc.vector.tensor_scalar(route[:, t, 40:48], iota, route[:, t, 24:25], route[:, t, 34:35],
                                             ALU.is_equal, ALU.mult))
                link(nc.vector.tensor_scalar(route[:, t, 48:56], iota, route[:, t, 25:26], route[:, t, 35:36],
                                             ALU.is_equal, ALU.mult))
            for p in range(2):
                last = nc.vector.tensor_tensor(combine[:, :, NE * p:NE * p + NE], route[:, :, 40:48], route[:, :, 48:56], ALU.add)
            link(last)

            ps, b = product(dve, "rank")
            rank = rank_of[:, :, 0:NE]
            link(nc.vector.tensor_scalar(rank, ps[:, 0:2 * NE].rearrange("p (t e) -> p t e", t=T), 1.0, None, ALU.add))
            nc.vector.reduce_max(small[:, 120:121], ps[:, 2 * NE:3 * NE], AX_X).then_inc(bank_free(b), 1)
            evacuated(dve, "rank")
            link(nc.vector.tensor_tensor(rank, rank, route[:, :, 56:64], ALU.mult))
            link(nc.vector.tensor_scalar(rank, rank, -1.0, None, ALU.add))
            link(nc.vector.tensor_scalar(rank_of[:, :, NE:2 * NE], rank, -float(P), None, ALU.add))
            nc.vector.tensor_scalar(overflow[:, 0:1], small[:, 120:121], float(P), None, ALU.is_gt)\
                .then_inc(sem("overflow_ready"), 1)

            slots = consts[:, C_SLOT:C_SLOT + P]

            def select_tokens(nxt):
                nc.vector.tensor_scalar(sel[:, 0, :], slots, rank_of[:, 0, bass.ds(nxt, 1)], None, ALU.is_equal)
                nc.vector.tensor_scalar(sel[:, 1, :], slots, rank_of[:, 1, bass.ds(nxt, 1)], None, ALU.is_equal)\
                    .then_inc(sem("sel_ready"), 1)

            def place_x(par, nxt, wait, bank, freed):
                for h in range(2):
                    dve.wait_ge(sem("xe_high"), nxt * 2 + (h + 1))
                    ps = bank(("x", h))
                    nc.vector.tensor_tensor(XE[:, par, 1, 4 * h:4 * h + 4, :], ps[:, :].rearrange("p (k q) -> p k q", k=4),
                                            XE[:, par, 0, 4 * h:4 * h + 4, :].bitcast(F32), ALU.subtract).then_inc(freed(("x", h)), 1)
                wait(("gate",))
                nc.vector.tensor_copy(slot_gate[:, par:par + 1], bank(("gate",))[:, 0:1]).then_inc(freed(("gate",)), 1)

            select_tokens(0)
            place_x(0, 0, lambda key: product(dve, ("first",) + key),
                    lambda key: psum[work.where[("first",) + key][0]],
                    lambda key: bank_free(work.where[("first",) + key][0]))
            dve.wait_ge(sem("split_lo"), N0 + len(PASS_START))

            def item(i, par, last):
                def bank(key):
                    return ebank[item_at[key] % BANKS_E]

                def split_step(g, which):
                    for (kind, gg, n), (_, _, n0) in zip(item_splits(i, g, last), item_splits(0, g, last)):
                        if kind in which:
                            low_e(kind, gg, (N0 + n0) % RAW, n + (N0 + 1))

                for g in range(GE + 1):
                    if g > 0:
                        dve.wait_ge(sem("hT_high"), i * GE + (FG + g))
                        nc.vector.tensor_tensor(hT[:, (g - 1) % 2, 1, 0:256], bank(("ht", g - 1))[:, 0:256],
                                                hT[:, (g - 1) % 2, 0, 0:256].bitcast(F32), ALU.subtract)\
                            .then_inc(e_read(("ht", g - 1), i)[0], 1)
                        split_step(g - 1, (2,))
                    if g == GE // 2 + 1:
                        place_x(1 - par, i + 1, lambda key: dve.wait_ge(*e_full(key, i)), bank,
                                lambda key: e_read(key, i)[0])
                    if g < GE:
                        split_step(g, (0,))
                        dve.wait_ge(sem("silu_ready"), i * GE + (2 * FG + g + 1))
                        nc.vector.tensor_tensor(hexp[:, g % 2, :], hexp[:, g % 2, :], bank(("gu", g))[:, 256:512], ALU.mult)\
                            .then_inc(e_read(("gu", g), i)[0], 1)
                        if g == GE // 2 - 1:
                            select_tokens(i + 1)
                        split_step(g, (1,))
                for n in range(4):
                    c, t = divmod(n, 2)
                    dve.wait_ge(*e_full(("y", n), i))
                    xs = X[:, t, 512 * c:512 * c + 512]
                    nc.vector.tensor_tensor(xs, xs, bank(("y", n))[:, :], ALU.add).then_inc(e_read(("y", n), i)[0], 1)

            def items(p):
                if p:
                    pass_start(p, PASS_START)
                with dve.Fori(0, NE // 2 - 1) as m:
                    for u in range(2):
                        item(m * 2 + (NE * p + u), u, False)
                item(NE * p + NE - 2, 0, False)
                item(NE * p + NE - 1, 1, True)
                for n in range(4):
                    dve.wait_ge(*e_read(("y", n), NE * p + NE - 1))

            passes(dve, items)
            dve.sem_inc(sem("x_final"), 1)
            norm(4)
            dve.wait_ge(sem("xn_ready"), 10)
            dve.wait_ge(sem("final_in"), 16)
            for t in range(T):
                nc.vector.tensor_tensor(XN[:, t, :], XN[:, t, :], gain_row[:, :], ALU.mult).then_inc(sem("out_ready"), 1)


_INS = ["x", "positions", "norm_mix", "norm_ffn", "w_in_ab", "fgate_bias", "w_out_ab", "w_in_c",
        "lower_bounds", "gnorm_c", "w_out_c", "w_gate_ffn", "w_up_ffn", "w_down_ffn", "router",
        "w_gate_moe", "w_up_moe", "w_down_moe", "norm_final"]


def kernel(**inputs):
    import numpy as _np
    import concourse.bacc as _bacc
    from concourse import mybir as _mybir
    from concourse.bass_utils import run_bass_kernel_spmd as _run

    nc = _bacc.Bacc("TRN2", target_bir_lowering=False, num_devices=1)
    arrays, args = {}, []
    every = {n: _np.ascontiguousarray(inputs[n]) for n in _INS}
    every.update(shape_constants())
    for name, a in every.items():
        arrays[f"in_{name}"] = a
        args.append(nc.dram_tensor(f"in_{name}", a.shape, _mybir.dt.from_np(a.dtype), kind="ExternalInput").ap())
    args.append(nc.dram_tensor("out_0", (1, SEQ, D), F32, kind="ExternalOutput").ap())
    trunk(nc, *args)
    r = _run(nc, [arrays], core_ids=[0])
    return r.results[0]["out_0"]
```
